# Optimizing a Trainium2 kernel written in Bass

```python
import math
import jax
import jax.numpy as jnp
from jax import lax
import numpy as np

D_MODEL = 2048
BATCH = 1
SEQ = 256
DEPTH = 1
DEC_BATCH = 8
DEC_SEQ = 4
PAST_LEN = 1024
PAGE_SIZE = 128

HEAD_DIM = 128
A_GROUPS = ((128, 1), (512, 4), (2048, 16))
A_HPG = 2
A_HEADS = A_HPG * len(A_GROUPS)
A_QBLK = 128
B_HEADS = 4
B_BLOCK = 256
B_TOPK = 3
B_QBLK = 128
C_CHUNK = 128
C_GROUPS = 4
C_GROUP_DIM = 128
C_WIDTH = C_GROUPS * C_GROUP_DIM
D_WINDOWS = (2, 4, 8, 16)
D_GROUP_DIM = 128
D_WIDTH = len(D_WINDOWS) * D_GROUP_DIM
D_STATE = max(D_WINDOWS) - 1
D_FF = 5632
CONV_W = 3
REL_BUCKETS = 32
REL_MAX_EXACT = 16
REL_MAX_DIST = 2048
N_BIAS_HEADS = A_HEADS + B_HEADS
N_BRANCH = 4
EPS = 1e-6
NEG = -1e30

A_W = A_HEADS * HEAD_DIM
A_OUT = A_HPG * HEAD_DIM
B_W = B_HEADS * HEAD_DIM
OFF_AQ = 0
OFF_AK = OFF_AQ + A_W
OFF_AV = OFF_AK + A_W
OFF_BQ = OFF_AV + A_W
OFF_BK = OFF_BQ + B_W
OFF_BV = OFF_BK + B_W
OFF_C = OFF_BV + B_W
OFF_D = OFF_C + 2 * C_WIDTH
OFF_G = OFF_D + D_WIDTH
N_IN = OFF_G + N_BRANCH * D_MODEL

kernel_name = 'hybrid_gated_branch_decoder_step'

def rmsnorm(x, g):
    xf = x.astype(jnp.float32)
    y = xf * lax.rsqrt(jnp.mean(xf * xf, -1, keepdims=True) + EPS)
    return (y * g.astype(jnp.float32)).astype(x.dtype)

def layernorm(x, g):
    xf = x.astype(jnp.float32)
    xc = xf - jnp.mean(xf, -1, keepdims=True)
    y = xc * lax.rsqrt(jnp.mean(xc * xc, -1, keepdims=True) + EPS)
    return (y * g.astype(jnp.float32)).astype(x.dtype)

def rel_bucket(dist):
    n = jnp.maximum(dist, 0)
    nf = jnp.maximum(n, 1).astype(jnp.float32)
    large = REL_MAX_EXACT + (jnp.log(nf / REL_MAX_EXACT) / math.log(REL_MAX_DIST / REL_MAX_EXACT)
                             * (REL_BUCKETS - REL_MAX_EXACT)).astype(jnp.int32)
    return jnp.where(n < REL_MAX_EXACT, n, jnp.minimum(large, REL_BUCKETS - 1))

def dilated_group_prompt(q, k, v, win, dil, tab):
    N, S, H, hd = q.shape
    taps = win // dil
    L = S // dil
    qb = min(A_QBLK, L)
    nb = -(-L // qb)
    Lp = nb * qb
    qs = jnp.pad(q.reshape(N, L, dil, H, hd), ((0, 0), (0, Lp - L), (0, 0), (0, 0), (0, 0)))
    qs = qs.reshape(N, nb, qb, dil, H, hd)
    idx = jnp.arange(nb)[:, None] * qb + jnp.arange(qb + taps)[None, :]

    def banded(a):
        a = jnp.pad(a.reshape(N, L, dil, H, hd), ((0, 0), (taps, Lp - L), (0, 0), (0, 0), (0, 0)))
        return a[:, idx]

    ks, vs = banded(k), banded(v)
    off = jnp.arange(qb)[:, None] + taps - jnp.arange(qb + taps)[None, :]
    valid = ((off >= 0) & (off <= taps))[None] & (idx >= taps)[:, None, :]
    bias = tab[rel_bucket(off * dil)].astype(jnp.float32).transpose(2, 0, 1)
    logits = jnp.einsum('nbqrhd,nbkrhd->nbrhqk', qs, ks).astype(jnp.float32) + bias
    logits = jnp.where(valid[None, :, None, None], logits, NEG)
    lse = jax.nn.logsumexp(logits, axis=-1)
    p = jnp.exp(logits - lse[..., None]).astype(v.dtype)
    o = jnp.einsum('nbrhqk,nbkrhd->nbqrhd', p, vs).reshape(N, Lp, dil, H, hd)[:, :L].reshape(N, S, H, hd)
    lse = lse.transpose(0, 1, 4, 2, 3).reshape(N, Lp, dil, H)[:, :L].reshape(N, S, H)
    return o, lse

def dilated_group_sample(q, k, v, buf, win, dil, tab):
    N, T, H, hd = q.shape
    W = buf.shape[1]
    taps = win // dil
    kk = jnp.concatenate([buf[:, :, 0], k], 1)
    vv = jnp.concatenate([buf[:, :, 1], v], 1)
    j = jnp.arange(taps + 1)
    idx = W + jnp.arange(T)[:, None] - j[None, :] * dil
    valid = idx >= 0
    idx = jnp.maximum(idx, 0)
    bias = tab[rel_bucket(j * dil)].astype(jnp.float32).T
    logits = jnp.einsum('nthd,ntjhd->nthj', q, kk[:, idx]).astype(jnp.float32) + bias
    logits = jnp.where(valid[None, :, None, :], logits, NEG)
    lse = jax.nn.logsumexp(logits, axis=-1)
    p = jnp.exp(logits - lse[..., None]).astype(v.dtype)
    o = jnp.einsum('nthj,ntjhd->nthd', p, vv[:, idx])
    new_len = min(win, W + T)
    new_buf = jnp.concatenate([buf, jnp.stack([k, v], 2)], 1)[:, W + T - new_len:]
    return o, lse, new_buf

def combine_groups(outs, lses):
    w = jax.nn.softmax(jnp.stack(lses, 0), axis=0)
    return jnp.einsum('gnth,gnthd->nthd', w.astype(outs[0].dtype), jnp.stack(outs, 0))

def moba_select(q, means, own_blk):
    nb = means.shape[1]
    kk = min(B_TOPK, nb)
    s = jnp.einsum('nqhd,nbhd->nqhb', q, means).astype(jnp.float32)
    past = jnp.arange(nb)[None, :] < own_blk[:, None]
    s = jnp.where(past[None, :, None, :], s, NEG)
    idx = lax.top_k(s, kk)[1]
    valid = jnp.arange(kk)[None, :] < own_blk[:, None]
    return idx, valid

def sel_positions(idx, valid):
    N, Q, H, kk = idx.shape
    pos = (idx[..., None] * B_BLOCK + jnp.arange(B_BLOCK)).reshape(N, Q, H, kk * B_BLOCK)
    ok = jnp.broadcast_to(valid[None, :, None, :, None], (N, Q, H, kk, B_BLOCK)).reshape(N, Q, H, kk * B_BLOCK)
    return pos, ok

def moba_core(q, q_pos, k_sel, v_sel, sel_pos, sel_ok, k_own, v_own, own_pos, tab):
    H = q.shape[2]
    h_i = jnp.arange(H)[None, None, :, None]
    s_sel = jnp.einsum('nqhd,nqhkd->nqhk', q, k_sel).astype(jnp.float32)
    s_sel = s_sel + tab[rel_bucket(q_pos[None, :, None, None] - sel_pos), h_i].astype(jnp.float32)
    s_sel = jnp.where(sel_ok, s_sel, NEG)
    d_own = q_pos[:, None] - own_pos[None, :]
    s_own = jnp.einsum('nqhd,nkhd->nqhk', q, k_own).astype(jnp.float32)
    s_own = s_own + tab[rel_bucket(d_own)].astype(jnp.float32).transpose(0, 2, 1)
    s_own = jnp.where((d_own >= 0)[:, None, :], s_own, NEG)
    p = jax.nn.softmax(jnp.concatenate([s_sel, s_own], -1), axis=-1).astype(v_own.dtype)
    ks = k_sel.shape[3]
    return (jnp.einsum('nqhk,nqhkd->nqhd', p[..., :ks], v_sel)
            + jnp.einsum('nqhk,nkhd->nqhd', p[..., ks:], v_own))

def moba_prompt(q, k, v, tab):
    N, S, H, hd = q.shape
    nblk = -(-S // B_BLOCK)
    pad = ((0, 0), (0, nblk * B_BLOCK - S), (0, 0), (0, 0))
    kb = jnp.pad(k, pad).reshape(N, nblk, B_BLOCK, H, hd)
    vb = jnp.pad(v, pad).reshape(N, nblk, B_BLOCK, H, hd)
    means = kb.astype(jnp.float32).mean(2).astype(k.dtype)
    kbh = kb.transpose(0, 3, 1, 2, 4)
    vbh = vb.transpose(0, 3, 1, 2, 4)
    n_i = jnp.arange(N)[:, None, None, None]
    h_i = jnp.arange(H)[None, None, :, None]

    def q_block(qb):
        q0 = qb * B_QBLK
        qq = lax.dynamic_slice_in_dim(q, q0, B_QBLK, 1)
        q_pos = q0 + jnp.arange(B_QBLK)
        idx, valid = moba_select(qq, means, q_pos // B_BLOCK)
        sel_pos, sel_ok = sel_positions(idx, valid)
        k_sel = kbh[n_i, h_i, idx].reshape(N, B_QBLK, H, -1, hd)
        v_sel = vbh[n_i, h_i, idx].reshape(N, B_QBLK, H, -1, hd)
        ob = q0 // B_BLOCK
        k_own = lax.dynamic_index_in_dim(kb, ob, 1, keepdims=False)
        v_own = lax.dynamic_index_in_dim(vb, ob, 1, keepdims=False)
        own_pos = ob * B_BLOCK + jnp.arange(B_BLOCK)
        return moba_core(qq, q_pos, k_sel, v_sel, sel_pos, sel_ok, k_own, v_own, own_pos, tab)

    o = lax.map(q_block, jnp.arange(S // B_QBLK))
    return o.transpose(1, 0, 2, 3, 4).reshape(N, S, H, hd)

def moba_sample(q, k, v, k_pool, v_pool, page_table, tab):
    N, T, H, hd = q.shape
    own0 = (PAST_LEN // B_BLOCK) * B_BLOCK
    n_full = own0 // B_BLOCK
    q_pos = PAST_LEN + jnp.arange(T)
    k_past = k_pool[page_table].reshape(N, PAST_LEN, H, hd)
    tail = jnp.arange(own0, PAST_LEN)
    v_tail = v_pool[page_table[:, tail // PAGE_SIZE], tail % PAGE_SIZE]
    k_own = jnp.concatenate([k_past[:, own0:], k], 1)
    v_own = jnp.concatenate([v_tail, v], 1)
    own_pos = own0 + jnp.arange(PAST_LEN - own0 + T)
    if n_full > 0:
        means = k_past[:, :own0].reshape(N, n_full, B_BLOCK, H, hd).astype(jnp.float32).mean(2).astype(k.dtype)
        idx, valid = moba_select(q, means, q_pos // B_BLOCK)
        sel_pos, sel_ok = sel_positions(idx, valid)
        n_i = jnp.arange(N)[:, None, None, None]
        h_i = jnp.arange(H)[None, None, :, None]
        k_sel = k_past[n_i, sel_pos, h_i]
        v_sel = v_pool[page_table[n_i, sel_pos // PAGE_SIZE], sel_pos % PAGE_SIZE, h_i]
    else:
        k_sel = jnp.zeros((N, T, H, 0, hd), q.dtype)
        v_sel = jnp.zeros((N, T, H, 0, hd), q.dtype)
        sel_pos = jnp.zeros((N, T, H, 0), jnp.int32)
        sel_ok = jnp.zeros((N, T, H, 0), bool)
    return moba_core(q, q_pos, k_sel, v_sel, sel_pos, sel_ok, k_own, v_own, own_pos, tab)

def chunk_mix(u, v, w_s, b_s):
    N, T, _ = v.shape
    L = min(T, C_CHUNK)
    nc = T // L
    vg = v.reshape(N, nc, L, C_GROUPS, C_GROUP_DIM)
    w = jnp.where(jnp.tril(jnp.ones((L, L), bool)), w_s[:, :L, :L], 0.0)
    s = jnp.einsum('gts,ncsge->nctge', w, vg) + b_s[:, :L].T[None, None, :, :, None]
    return u * s.reshape(N, T, C_WIDTH)

def pool_mix(hist, xd, w_pool, scale):
    N, T, C = xd.shape
    Hn = hist.shape[1]
    xe = jnp.concatenate([hist, xd], 1)
    cs = jnp.pad(jnp.cumsum(xe.astype(jnp.float32), axis=1), ((0, 0), (1, 0), (0, 0)))
    win = jnp.repeat(jnp.asarray(D_WINDOWS, jnp.int32), D_GROUP_DIM)
    hi = Hn + 1 + jnp.arange(T)
    lo = jnp.maximum(hi[:, None] - win[None, :], 0)
    upper = cs[:, hi]
    lower = jnp.take_along_axis(cs, jnp.broadcast_to(lo[None], (N, T, C)), axis=1)
    cnt = jnp.minimum(hi[:, None], win[None, :]).astype(jnp.float32)
    pooled = ((upper - lower) / cnt - xd.astype(jnp.float32)).astype(xd.dtype)
    y = jnp.einsum('ntgc,gce->ntge', pooled.reshape(N, T, len(D_WINDOWS), D_GROUP_DIM), w_pool)
    return y.reshape(N, T, D_WIDTH) * scale, xe[:, -D_STATE:]

def conv_ffn(xn, hist, w_up, conv_w, conv_b, w_down):
    T = xn.shape[1]
    h = jnp.einsum('ntd,df->ntf', xn, w_up)
    he = jnp.concatenate([hist, h], 1)
    hc = conv_b + sum(conv_w[i] * he[:, i:i + T] for i in range(CONV_W))
    gate, val = jnp.split(hc, 2, axis=-1)
    y = jnp.einsum('ntf,fd->ntd', jax.nn.gelu(gate) * val, w_down)
    return y, he[:, -(CONV_W - 1):]

def layer(x, w, tab, st):
    N, T, _ = x.shape
    xn = rmsnorm(x, w['norm_mix_pre'])
    z = jnp.einsum('ntd,de->nte', xn, w['w_in'])

    def heads(a, b, n):
        return z[..., a:b].reshape(N, T, n, HEAD_DIM)

    aq = heads(OFF_AQ, OFF_AK, A_HEADS) * HEAD_DIM ** -0.5
    ak = heads(OFF_AK, OFF_AV, A_HEADS)
    av = heads(OFF_AV, OFF_BQ, A_HEADS)
    bq = heads(OFF_BQ, OFF_BK, B_HEADS) * HEAD_DIM ** -0.5
    bk = heads(OFF_BK, OFF_BV, B_HEADS)
    bv = heads(OFF_BV, OFF_C, B_HEADS)
    u, vc = jnp.split(jax.nn.gelu(z[..., OFF_C:OFF_D]), 2, axis=-1)
    vc = layernorm(vc, w['c_ln_g'])
    xd = z[..., OFF_D:OFF_G]
    gates = jax.nn.sigmoid(z[..., OFF_G:].reshape(N, T, N_BRANCH, D_MODEL))
    new = {}
    outs, lses = [], []
    for g, (win, dil) in enumerate(A_GROUPS):
        hs = slice(g * A_HPG, (g + 1) * A_HPG)
        qg, kg, vg, tg = aq[:, :, hs], ak[:, :, hs], av[:, :, hs], tab[:, hs]
        if st is None:
            o, l = dilated_group_prompt(qg, kg, vg, win, dil, tg)
            keep = min(win, T)
            new['win' + str(g)] = jnp.stack([kg[:, T - keep:], vg[:, T - keep:]], 2)
        else:
            o, l, new['win' + str(g)] = dilated_group_sample(qg, kg, vg, st['win'][g], win, dil, tg)
        outs.append(o)
        lses.append(l)
    o_a = combine_groups(outs, lses).reshape(N, T, A_OUT)
    tb = tab[:, A_HEADS:]
    if st is None:
        o_b = moba_prompt(bq, bk, bv, tb)
    else:
        o_b = moba_sample(bq, bk, bv, st['k_pool'], st['v_pool'], st['page_table'], tb)
        new['c_v'] = vc
    new['k'] = bk
    new['v'] = bv
    o_b = o_b.reshape(N, T, B_W)
    o_c = chunk_mix(u, vc, w['c_ws'], w['c_bs'])
    hist = xd[:, :0] if st is None else st['pool']
    o_d, new['pool'] = pool_mix(hist, xd, w['d_w'], w['d_scale'])
    merged = (gates[:, :, 0] * jnp.einsum('nte,ed->ntd', o_a, w['p_a'])
              + gates[:, :, 1] * jnp.einsum('nte,ed->ntd', o_b, w['p_b'])
              + gates[:, :, 2] * jnp.einsum('nte,ed->ntd', o_c, w['p_c'])
              + gates[:, :, 3] * jnp.einsum('nte,ed->ntd', o_d, w['p_d']))
    x = x + rmsnorm(jnp.einsum('ntd,de->nte', merged, w['w_o']), w['norm_mix_post'])
    hn = rmsnorm(x, w['norm_ffn_pre'])
    conv_hist = jnp.zeros((N, CONV_W - 1, 2 * D_FF), x.dtype) if st is None else st['conv']
    f, new['conv'] = conv_ffn(hn, conv_hist, w['w_up'], w['conv_w'], w['conv_b'], w['w_down'])
    x = x + rmsnorm(f, w['norm_ffn_post'])
    return x, new

def setup_inputs(seed: int = 0) -> dict:
    key = jax.random.key(seed)
    ks = iter(jax.random.split(key, 40))

    def nrm(shape, scale):
        return jax.random.normal(next(ks), shape, jnp.float32) * scale

    n_pages = PAST_LEN // PAGE_SIZE
    used = DEC_BATCH * n_pages
    n_phys = used + max(1, used // 4)
    page_table = jax.random.permutation(next(ks), n_phys)[:used].reshape(DEC_BATCH, n_pages).astype(jnp.int32)
    win_shape = lambda g: (DEPTH, DEC_BATCH, min(A_GROUPS[g][0], PAST_LEN), 2, A_HPG, HEAD_DIM)
    return {
        'x_prompt': nrm((BATCH, SEQ, D_MODEL), 1.0),
        'x_sample': nrm((DEC_BATCH, DEC_SEQ, D_MODEL), 1.0),
        'cache_win0': nrm(win_shape(0), 1.0),
        'cache_win1': nrm(win_shape(1), 1.0),
        'cache_win2': nrm(win_shape(2), 1.0),
        'cache_k': nrm((DEPTH, n_phys, PAGE_SIZE, B_HEADS, HEAD_DIM), 1.0),
        'cache_v': nrm((DEPTH, n_phys, PAGE_SIZE, B_HEADS, HEAD_DIM), 1.0),
        'page_table': page_table,
        'state_pool': nrm((DEPTH, DEC_BATCH, D_STATE, D_WIDTH), 1.0),
        'state_conv': nrm((DEPTH, DEC_BATCH, CONV_W - 1, 2 * D_FF), 1.0),
        'rel_bias_table': nrm((REL_BUCKETS, N_BIAS_HEADS), 0.5),
        'norm_mix_pre': 1.0 + nrm((DEPTH, D_MODEL), 0.1),
        'w_in': nrm((DEPTH, D_MODEL, N_IN), D_MODEL ** -0.5),
        'c_ln_g': 1.0 + nrm((DEPTH, C_WIDTH), 0.1),
        'c_ws': nrm((DEPTH, C_GROUPS, C_CHUNK, C_CHUNK), C_CHUNK ** -0.5),
        'c_bs': 1.0 + nrm((DEPTH, C_GROUPS, C_CHUNK), 0.1),
        'd_w': nrm((DEPTH, len(D_WINDOWS), D_GROUP_DIM, D_GROUP_DIM), D_GROUP_DIM ** -0.5),
        'd_scale': 1.0 + nrm((DEPTH, D_WIDTH), 0.1),
        'p_a': nrm((DEPTH, A_OUT, D_MODEL), A_OUT ** -0.5),
        'p_b': nrm((DEPTH, B_W, D_MODEL), B_W ** -0.5),
        'p_c': nrm((DEPTH, C_WIDTH, D_MODEL), C_WIDTH ** -0.5),
        'p_d': nrm((DEPTH, D_WIDTH, D_MODEL), D_WIDTH ** -0.5),
        'w_o': nrm((DEPTH, D_MODEL, D_MODEL), D_MODEL ** -0.5),
        'norm_mix_post': 1.0 + nrm((DEPTH, D_MODEL), 0.1),
        'norm_ffn_pre': 1.0 + nrm((DEPTH, D_MODEL), 0.1),
        'w_up': nrm((DEPTH, D_MODEL, 2 * D_FF), D_MODEL ** -0.5),
        'conv_w': nrm((DEPTH, CONV_W, 2 * D_FF), CONV_W ** -0.5),
        'conv_b': nrm((DEPTH, 2 * D_FF), 0.01),
        'w_down': nrm((DEPTH, D_FF, D_MODEL), D_FF ** -0.5),
        'norm_ffn_post': 1.0 + nrm((DEPTH, D_MODEL), 0.1),
    }

def reference(x_prompt, x_sample, cache_win0, cache_win1, cache_win2, cache_k, cache_v, page_table,
              state_pool, state_conv, rel_bias_table, norm_mix_pre, w_in, c_ln_g, c_ws, c_bs, d_w, d_scale,
              p_a, p_b, p_c, p_d, w_o, norm_mix_post, norm_ffn_pre, w_up, conv_w, conv_b, w_down,
              norm_ffn_post):
    yp, ys = x_prompt, x_sample
    pn, sn = [], []
    for l in range(DEPTH):
        w = dict(norm_mix_pre=norm_mix_pre[l], w_in=w_in[l], c_ln_g=c_ln_g[l], c_ws=c_ws[l], c_bs=c_bs[l],
                 d_w=d_w[l], d_scale=d_scale[l], p_a=p_a[l], p_b=p_b[l], p_c=p_c[l], p_d=p_d[l], w_o=w_o[l],
                 norm_mix_post=norm_mix_post[l], norm_ffn_pre=norm_ffn_pre[l], w_up=w_up[l],
                 conv_w=conv_w[l], conv_b=conv_b[l], w_down=w_down[l], norm_ffn_post=norm_ffn_post[l])
        yp, new_p = layer(yp, w, rel_bias_table, None)
        st = dict(win=(cache_win0[l], cache_win1[l], cache_win2[l]), k_pool=cache_k[l], v_pool=cache_v[l],
                  page_table=page_table, pool=state_pool[l], conv=state_conv[l])
        ys, new_s = layer(ys, w, rel_bias_table, st)
        pn.append(new_p)
        sn.append(new_s)

    def stk(lst, name):
        return jnp.stack([s[name] for s in lst], 0)

    return (yp, ys,
            stk(pn, 'win0'), stk(pn, 'win1'), stk(pn, 'win2'), stk(pn, 'k'), stk(pn, 'v'),
            stk(pn, 'pool'), stk(pn, 'conv'),
            stk(sn, 'win0'), stk(sn, 'win1'), stk(sn, 'win2'), stk(sn, 'k'), stk(sn, 'v'),
            stk(sn, 'c_v'), stk(sn, 'pool'), stk(sn, 'conv'))


_drawn_inputs = setup_inputs


def setup_inputs(seed=0):
    import zlib

    import numpy as np

    out = dict(_drawn_inputs(seed))
    spreads = {}
    factors = {'conv_b': 6.857}
    for name, (base, spread) in spreads.items():
        noise = np.random.default_rng([zlib.crc32(name.encode()), seed]).standard_normal(out[name].shape)
        drawn = base * np.exp(spread * noise) if base else spread * noise
        out[name] = jnp.asarray(drawn.astype(out[name].dtype))
    for name, factor in factors.items():
        out[name] = (out[name] * factor).astype(out[name].dtype)
    return out
```

```python
from contextlib import ExitStack

import numpy as np
import concourse.bass as bass
from concourse import mybir

F32 = mybir.dt.float32
F32R = mybir.dt.float32r
I32 = mybir.dt.int32
ALU = mybir.AluOpType
ACT = mybir.ActivationFunctionType
AX = mybir.AxisListType

P = 128
D_MODEL, KC = 2048, 16
NP_TOK, NB, NT = 256, 8, 4
NS = NB * NT
TOK = NP_TOK + NS
DILATION = (1, 4, 16)
TAPS = 128
A_HEADS, B_HEADS, HPG = 6, 4, 2
N_HEADS = A_HEADS + B_HEADS
PAST, PAGE, NPG = 1024, 128, 8
WIN_LEN = (128, 512, 1024)
BLOCK_KEYS, N_BLOCKS = 256, 4
D_WIN = (2, 4, 8, 16)
HIST = 15
D_FF = 5632
FC = D_FF // P
SCALE = 128.0 ** -0.5
EPS = 1e-6
NEG = -1e30
Q_A, K_A, V_A, Q_B, K_B, V_B, U_C, V_C, X_D, N_MIX = 0, 6, 12, 18, 22, 26, 30, 34, 38, 42
OFF_G = N_MIX * P
O_CHUNK = (0, 2, 6, 10)
P_CHUNKS = (2, 4, 4, 4)
N_O = 14
SEG = 4
UNIT_COLS = 512
N_RAW, N_SPLIT = 4, 2
U_MIX = 44
U_GATE = U_MIX + 4 * 20
U_FFN = U_GATE + 16
XE = HIST + NP_TOK + NB * (HIST + NT)
XS = HIST + NP_TOK
HW = 2 + NP_TOK + NB * (2 + NT)
HS = 2 + NP_TOK
TAIL = 2 + NB * 2


class Count:

    def __init__(self, sem, known, key):
        self.sem, self.known, self.key = sem, known, key
        self.n, self.round = 0, None

    def step(self, name, by=1):
        self.n += by
        self.known[self.key, name] = (self.n, self.round)
        return by

    def begin(self, loop):
        self.start, self.round = self.n, loop

    def end(self, rounds):
        self.known[self.key, "per", self.round] = self.n - self.start
        self.n = self.start + rounds * (self.n - self.start)
        self.round = None

    def at(self, name, i=None, back=0):
        n, loop = self.known.get((self.key, name), (1, None))
        if loop is None:
            return n
        per = self.known.get((self.key, "per", loop), 0)
        n -= back * per
        assert n >= 0, (self.key, name)
        return n if i is None else i * per + n


def constants():
    def bucket(dist):
        n = np.maximum(dist, 0)
        big = 16 + (np.log(np.maximum(n, 1) / 16) / np.log(128.0) * 16).astype(np.int64)
        return np.where(n < 16, n, np.minimum(big, 31))

    def onehot(dist, ok):
        dist, ok = np.broadcast_arrays(np.asarray(dist), np.asarray(ok))
        rows = np.where(ok, bucket(dist), 32)
        return (rows[None] == np.arange(33).reshape((33,) + (1,) * rows.ndim)).astype(np.float32)

    d = 255 - np.arange(384)
    prompt = np.stack([onehot(d, (d >= 0) & (d <= 128)), onehot(d, (d >= 0) & (d % 4 == 0)),
                       onehot(d, (d >= 0) & (d % 16 == 0)), onehot(d, d >= 0)], 1)
    past = onehot(PAST + 3 - np.arange(PAST + 3), True)
    i = np.arange(131)
    win0 = onehot(131 - i, i >= 3)
    win1 = onehot(4 * (128 - np.arange(128)), True)
    win2 = onehot(16 * (64 - np.arange(64)), True)
    t = np.arange(NT)[:, None, None, None]
    n = np.arange(NB)[:, None, None]
    m = np.arange(NB)[:, None]
    j = np.arange(NT)
    own_causal = onehot(t - j + 0 * n + 0 * m, (n == m) & (j <= t)).reshape(33, NT, NB * NS)
    own_self = onehot(t - j + 0 * n + 0 * m, (n == m) & (j == t)).reshape(33, NT, NB * NS)
    sample = np.concatenate([past, win0, win1, win2, own_causal.reshape(33, -1), own_self.reshape(33, -1)], 1)
    count = np.minimum(np.arange(16) + 1, np.array(D_WIN)[:, None])
    ramp = (np.array(D_WIN)[:, None] / count).astype(np.float32).reshape(1, 64)
    spread = (np.arange(NS) % NT == np.arange(NT)[:, None]).astype(np.float32)
    same = (np.arange(NS)[:, None] // NT == np.arange(NB)).astype(np.float32)
    return {"c_prompt": prompt.reshape(33, 4 * 384), "c_sample": sample, "c_ramp": ramp,
            "c_spread": spread, "c_same": same, "c_rank": np.tile(np.arange(1, 5, dtype=np.float32), (16, 1))}


S_PAST, S_W0 = 0, PAST + 3
S_W1, S_W2 = S_W0 + 131, S_W0 + 259
S_CAUSAL = S_W2 + 64
S_SELF = S_CAUSAL + NT * NB * NS
S_ALL = S_SELF + NT * NB * NS


def build(nc, known, d, o, ctx):
    def sem(name):
        return ctx.enter_context(nc.semaphore(name))

    base = (nc.sbuf_base + 63) // 32 * 32
    CH = TOK * 4
    R_XN = base
    R_Z = R_XN + 2 * KC * CH
    R_RAW = R_Z + 49152
    R_SPLIT = R_RAW + N_RAW * 8192
    R_M = R_SPLIT + 2 * N_SPLIT * 8192
    R_VTOK = R_M + N_O * CH
    R_U = R_VTOK + 2 * 1280 * 4 + 256
    R_SMALL = R_M + 2 * KC * CH
    assert R_U + 10240 <= R_SMALL

    def sb(name, shape, dt, at):
        return nc.alloc_sbuf_tensor_at(name, shape, dt, offset=at)

    small = [R_SMALL]

    def keep(name, shape, dt=F32):
        n = 4
        for s in shape[1:]:
            n *= s
        at = small[0]
        small[0] += (n + 31) // 32 * 32
        return sb(name, shape, dt, at)

    xn_hi = sb("xn_hi", [P, KC, TOK], F32R, R_XN)
    xn_lo = sb("xn_lo", [P, KC, TOK], F32R, R_XN + KC * CH)
    Z = sb("Z", [P, N_MIX, TOK], F32, R_Z)
    w_raw = [sb(f"w_raw{s}", [P, SEG, UNIT_COLS], F32, R_RAW + 8192 * s) for s in range(N_RAW)]
    w_hi = [sb(f"w_hi{s}", [P, SEG, UNIT_COLS], F32R, R_SPLIT + 8192 * s) for s in range(N_SPLIT)]
    w_lo = [sb(f"w_lo{s}", [P, SEG, UNIT_COLS], F32R, R_SPLIT + 8192 * (N_SPLIT + s)) for s in range(N_SPLIT)]
    x_nat = sb("x_nat", [P, 3, D_MODEL], F32, R_Z)
    xw = sb("xw", [P, KC, TOK], F32, R_Z + 3 * D_MODEL * 4)
    sq_a = sb("sq_a", [P, 4, SEG, TOK], F32, R_Z + 3 * D_MODEL * 4)
    oh_prompt = sb("oh_prompt", [33, 4, 384], F32, R_Z + 3 * D_MODEL * 4 + KC * CH)
    x_T = sb("x_T", [P, KC, TOK], F32, R_M)
    prow = sb("prow", [88, 4, P], F32, R_M + KC * CH)
    nrow = sb("nrow", [72, P], F32, R_M + KC * CH + 2048)
    tabx = sb("tabx", [33, N_HEADS, P], F32, R_M + KC * CH + 2560)
    urow = sb("urow", [P, 4, 384], F32, R_U)
    U = sb("U", [P, N_HEADS, 256], F32, R_U)
    xe_a = sb("xe_a", [P, 4, XE], F32, R_RAW)
    xe_b = sb("xe_b", [P, 4, XE], F32, R_RAW + 6784)
    pooled = sb("pooled", [P, 4, TOK], F32, R_RAW + 13568)
    vn = sb("vn", [P, 4, TOK], F32, R_RAW + 18176)
    vc_tok = sb("vc_tok", [P, 3, 512], F32, R_RAW + 22784)
    sq_c = sb("sq_c", [P, 4, TOK], F32, R_RAW + 13568)
    dw = sb("dw", [P, 4, P], F32, R_RAW + 28928)
    Lp = sb("Lp", [P, 2, 768], F32, R_SPLIT)
    PTp = sb("PTp", [P, 2, 768], F32, R_SPLIT + 6144)
    k_tok = sb("k_tok", [P, 3, 1280], F32, R_SPLIT + 12288)
    ws_nat = sb("ws_nat", [P, 4, P], F32, R_SPLIT + 27648)
    ws_T = sb("ws_T", [P, 4, P], F32, R_SPLIT + 29696)
    v_tok = sb("v_tok", [P, 2, 1280], F32, R_VTOK)
    O = sb("O", [P, N_O, TOK], F32, R_M)
    oh_sample = sb("oh_sample", [33, S_ALL], F32, R_VTOK)
    QA = 176
    qpad_a = sb("qpad_a", [P, NB, QA], F32, R_VTOK + 13600)
    kv = [sb(f"kv{s}", [P, 4, 512], F32, R_Z + 8192 * s) for s in range(6)]
    bias_b = sb("bias_b", [16, PAST + NB * NS], F32, R_SPLIT)
    bias_a = sb("bias_a", [8, 320 + NB * 96], F32, R_SPLIT + 5120)
    kt_b = sb("kt_b", [P, 2, 512], F32, R_SPLIT + 9472)
    kt_a = sb("kt_a", [P, 4, 512], F32, R_SPLIT + 13568)
    L_b = sb("L_b", [16, PAST + NS], F32, R_SPLIT + 21760)
    L_a = sb("L_a", [8, 416], F32, R_SPLIT + 25984)
    pt_b = sb("pt_b", [P, 9, 16], F32, R_SPLIT + 27648)
    pt_a = sb("pt_a", [P, 8 + 32 + 32 + 24], F32, R_SPLIT + 28224)
    ob = sb("ob", [16, 512], F32, R_SPLIT + 28608)
    oa = sb("oa", [8, 256], F32, R_SPLIT + 30656)
    O_hi = sb("O_hi", [P, N_O, TOK], F32R, R_Z)
    O_lo = sb("O_lo", [P, N_O, TOK], F32R, R_Z + N_O * CH)
    sig = sb("sig", [P, 4, TOK], F32, R_Z + 2 * N_O * CH)
    acc = sb("acc", [P, 4, TOK], F32, R_Z + 2 * N_O * CH + 4 * CH)
    tmp = sb("tmp", [P, 4, TOK], F32, R_Z + 2 * N_O * CH + 8 * CH)
    M_hi = sb("M_hi", [P, KC, TOK], F32R, R_M)
    M_lo = sb("M_lo", [P, KC, TOK], F32R, R_M + KC * CH)
    m_T = sb("m_T", [P, KC, TOK], F32, R_Z)
    x1 = sb("x1", [P, KC, TOK], F32, R_Z + KC * CH)
    hist_c = sb("hist_c", [P, 2 * FC, 16], F32, R_Z + 2 * KC * CH)
    crow = sb("crow", [P, 11, P], F32, R_Z + 2 * KC * CH + 2 * FC * 64)
    sq_b = sb("sq_b", [P, 4, SEG, TOK], F32, R_XN)
    xw_b = sb("xw_b", [P, KC, TOK], F32, R_M)
    H = [sb(f"H{s}", [P, 4, HW], F32, R_M + 4896 * s) for s in range(2)]
    hc = [sb(f"hc{s}", [P, 4, HW], F32, R_M + 9792 + 4896 * s) for s in range(2)]
    act_hi = sb("act_hi", [P, 4, TOK], F32R, R_M + 19584)
    act_lo = sb("act_lo", [P, 4, TOK], F32R, R_M + 24192)
    tails = sb("tails", [P, 2 * FC, TAIL], F32, R_M + 28800)
    tail_rows = sb("tail_rows", [7 * TAIL, 13, P], F32, R_RAW)
    y_nat = sb("y_nat", [P, 3, D_MODEL], F32, R_XN)
    sq_f = sb("sq_f", [P, 4, SEG, TOK], F32, R_M)

    ident = keep("ident", [P, P])
    ones = keep("ones", [P, P])
    conv = keep("conv", [P, 4, 2 * FC])
    gains = keep("gains", [P, 72])
    stat = keep("stat", [P, 3, TOK])
    hist_rows = sb("hist_rows", [120, 512], F32, small[0])
    qpad_b = keep("qpad_b", [P, NB, 64])
    v_own = keep("v_own", [NS, 1280])
    z_own = keep("z_own", [P, 30, NS])
    tab = keep("tab", [33, N_HEADS])
    tab_t = keep("tab_t", [33, NT, N_HEADS, NT])
    tab_all = keep("tab_all", [33, N_HEADS, NT])
    pages = keep("pages", [1, NB * NPG], I32)
    ramp = keep("ramp", [P, 64])
    spread = keep("spread", [NT, NS])
    same = keep("same", [NS, NB])
    rank = keep("rank", [16, 4])
    bs = keep("bs", [1, 4, P])
    bs_own = keep("bs_own", [1, 4, NB, NT])
    wd = keep("wd", [NS, 4, NB, NT])
    col = keep("col", [P, 16])
    win0 = keep("win0", [P, 512])
    qs_b = keep("qs_b", [P, 64])
    qs_a = keep("qs_a", [P, QA])
    xd_rows = sb("xd_rows", [NS, 2, 512], F32, small[0])
    small[0] += 4096
    if small[0] > nc.sbuf_usable_end:
        raise ValueError(f"SBUF: {small[0]} over {nc.sbuf_usable_end}")
    NORM = {"mix_pre": 0, "mix_post": 16, "ffn_pre": 32, "ffn_post": 48, "c_ln": 64, "d_scale": 68}

    ps = nc.alloc_psum_tensor("ps", [P, 8, 512], F32)
    u_dram = nc.dram_tensor("u_dram", [N_HEADS, P, 384], F32)
    x_dram = nc.dram_tensor("x_dram", [P, KC, TOK], F32)

    def view(t, n_part, off, dims):
        a = t[:]
        return bass.AP(a.tensor, a.offset + off, [[a.ap[0][0], n_part]] + dims)

    pe = Count(sem("pe_done"), known, "pe")
    act = Count(sem("act_done"), known, "act")
    dve = Count(sem("dve_done"), known, "dve")
    pool = Count(sem("pool_done"), known, "pool")
    landed = {k: sem(f"landed_{k}") for k in
              ["prow", "nrow", "tab", "oh_prompt", "x", "u", "x_saved", "hist", "ws", "dw", "small", "pages",
               "oh_sample", "x_back", "crow", "win0"]}
    u_stored = [sem(f"u_stored{s}") for s in range(4)]
    w_landed = [sem(f"w_landed{s}") for s in range(N_RAW)]
    kv_landed = [sem(f"kv_landed{s}") for s in range(6)]
    stored = sem("stored")
    copied = sem("copied")
    n_stored = [0]
    hi_ready, lo_ready, unit_done = sem("hi_ready"), sem("lo_ready"), sem("unit_done")
    z_copied = sem("z_copied")
    sig_ready, p_used = sem("sig_ready"), sem("p_used")
    merge_step, merged_f, merged_hi, merged_lo = sem("merge_step"), sem("merged_f"), sem("merged_hi"), sem("merged_lo")
    m_copied = sem("m_copied")
    y_added = sem("y_added")
    h_copied, hist_put, tails_put = sem("h_copied"), sem("hist_put"), sem("tails_put")
    conv_step = sem("conv_step")
    gelu_done, act_f, act_hi_ready, act_ready = sem("gelu_done"), sem("act_f"), sem("act_hi_ready"), sem("act_ready")

    block = ctx.enter_context(nc.Block())

    def store(e, dst, src):
        n_stored[0] += 16
        e.dma_start(dst, src).then_inc(stored, 16)

    units = []
    for slot in range(HPG):
        for m in range(2):
            units.append(([(Q_A + 2 * g + slot, K_A + 2 * g + slot, 2 * g + slot, 2 * g + slot) for g in range(3)],
                          slot, m))
    for h in range(B_HEADS):
        for m in range(2):
            units.append(([(Q_B + h, K_B + h, A_HEADS + h, A_HEADS + h)], 2 + h, m))
    NU = len(units)

    def unit_no(u0, per, i, j):
        if isinstance(i, int):
            return u0 + per * i + j, (u0 + per * i + j) // N_RAW, j % N_RAW, j % N_SPLIT
        return i * per + (u0 + j), i * (per // N_RAW) + (u0 + j) // N_RAW, j % N_RAW, j % N_SPLIT

    def ffn_unit(i, j):
        if isinstance(i, int) and i == 0:
            return unit_no(U_FFN, 12, 0, j)
        return unit_no(U_FFN - 4, 12, i, j)

    @block.sync
    def _(sp):
        sp.dma_start(x_nat[:, 0:2, :], d["x_prompt"][0].rearrange("(m p) c -> p m c", p=P)).then_inc(landed["x"], 16)
        sp.dma_start(x_nat[0:NS, 2, :], d["x_sample"].rearrange("n t c -> (n t) c")).then_inc(landed["x"], 16)

        def load(no, src):
            u, _, slot, _ = no
            if not isinstance(u, int) or u >= N_RAW:
                need = u - (N_RAW - 1)
                if not isinstance(need, int):
                    need = sp.snap(sp.to_reg(need))
                    sp.wait_ge(landed["x"], 32)
                sp.wait_ge(lo_ready, need)
            sp.dma_start(w_raw[slot][:, 0:src.shape[1], 0:src.shape[2]], src).then_inc(w_landed[slot], 16)

        def rows(w, r0, k, c0, n=UNIT_COLS):
            return w[bass.ds(r0, k * P), bass.ds(c0, n)].rearrange("(k p) c -> p k c", p=P)

        w_in, w_up, w_down = d["w_in"][0], d["w_up"][0], d["w_down"][0]

        def mix_group(i, h, g):
            for j in range(4):
                load(unit_no(4, 8, i, 4 * h + j), rows(w_in, j * 512, SEG, g * UNIT_COLS))
        for j in range(4):
            load(unit_no(0, 8, 0, j), rows(w_in, j * 512, SEG, 0))
        for h in range(N_HEADS):
            sp.wait_ge(act.sem, act.at(("urow", h)))
            sp.dma_start(u_dram.ap()[h], urow[:, h % 4, :]).then_inc(u_stored[h % 4], 16)
        for s in range(4):
            sp.wait_ge(u_stored[s], 16 * len(range(s, N_HEADS, 4)))
        sp.dma_start(U[:, :, :], bass.AP(u_dram.ap().tensor, P - 1, [[383, P], [P * 384, N_HEADS], [1, 256]]))\
            .then_inc(landed["u"], 16)
        with sp.Fori(0, 4) as i:
            for h in range(2):
                mix_group(i, h, i * 2 + (1 + h))
        for j in range(4):
            load(unit_no(36, 8, 0, j), rows(w_in, j * 512, SEG, 9 * UNIT_COLS))
        for j in range(4):
            load(unit_no(40, 8, 0, j), rows(w_in, j * 512, SEG, 10 * UNIT_COLS, 256))

        def store(dst, src):
            n_stored[0] += 16
            sp.dma_start(dst, src).then_inc(stored, 16)

        for m in range(2):
            sp.wait_ge(act.sem, act.at(("k_tok", m)))
            sp.wait_ge(dve.sem, dve.at(("v_tok", m)))
            for g in range(3):
                if g == 0 and m == 0:
                    continue
                t0 = 0 if g == 0 else m * P
                dst = o[2 + g][0, 0, t0:t0 + P]
                store(dst[:, 0].rearrange("p h e -> p (h e)"), k_tok[:, m, 256 * g:256 * g + 256])
                store(dst[:, 1].rearrange("p h e -> p (h e)"), v_tok[:, m, 256 * g:256 * g + 256])
            store(o[5][0, 0, m * P:m * P + P].rearrange("p h e -> p (h e)"), k_tok[:, m, 768:1280])
            store(o[6][0, 0, m * P:m * P + P].rearrange("p h e -> p (h e)"), v_tok[:, m, 768:1280])
        sp.wait_ge(act.sem, act.at(("k_tok", 2)))
        sp.wait_ge(dve.sem, dve.at(("v_tok", 2)))
        for g in range(3):
            L = WIN_LEN[g] + (NT if g == 2 else 0)
            dst = o[9 + g][0]
            for kv_i, src in ((0, k_tok[0:NS, 2, 256 * g:256 * g + 256]), (1, v_own[:, 256 * g:256 * g + 256])):
                for n in range(NB):
                    store(dst[n, L - NT:L, kv_i].rearrange("t h e -> t (h e)"), src[NT * n:NT * n + NT, :])
        store(o[12][0].rearrange("n t h e -> (n t) (h e)"), k_tok[0:NS, 2, 768:1280])
        store(o[13][0].rearrange("n t h e -> (n t) (h e)"), v_own[:, 768:1280])
        sp.wait_ge(dve.sem, dve.at(("vc", 2)))
        store(o[14][0].rearrange("n t c -> (n t) c"), vc_tok[0:NS, 2, :])
        sp.wait_ge(act.sem, act.at("xd_own"))
        store(o[7][0, 0], xd_rows[0:HIST, 0, :])
        for n in range(NB):
            store(o[15][0, n, HIST - NT:HIST], xd_rows[NT * n:NT * n + NT, 1, :])
        store(o[15][0, :, 0:HIST - NT], d["state_pool"][0, :, NT:HIST])

        sp.wait_ge(pe.sem, pe.at(("PV", NU - 1)))
        sp.wait_ge(dve.sem, dve.at(("P", NU - 1)))
        sp.wait_ge(pool.sem, pool.at("z_own"))
        sp.wait_ge(stored, n_stored[0])
        sp.dma_start(oh_sample[:, :], d["c_sample"]).then_inc(landed["oh_sample"], 16)
        sp.wait_ge(landed["pages"], 16)
        with sp.Fori(0, NB) as i:
            def page_loads(cache, half, slot):
                for q in range(4):
                    page = sp.value_load(pages[0:1, bass.ds(i * NPG + (4 * half + q), 1)], min_val=0,
                                         max_val=cache.shape[0] - 1)
                    sp.dma_start(kv[slot][:, q:q + 1, :], cache[bass.ds(page, 1)].rearrange("a p h e -> p a (h e)"))\
                        .then_inc(kv_landed[slot], 16)
            for half in range(2):
                need = sp.snap(sp.to_reg(pe.at(("kT", 4 * half + 3), i, back=1)))
                sp.wait_ge(landed["pages"], 16)
                sp.wait_ge(pe.sem, need)
                page_loads(d["cache_k"][0], half, half)
            need = sp.snap(sp.to_reg(pe.at("pv_b", i, back=1)))
            sp.wait_ge(landed["pages"], 16)
            sp.wait_ge(pe.sem, need)
            for half in range(2):
                page_loads(d["cache_v"][0], half, 4 + half)
            sp.wait_ge(pe.sem, pe.at("pv_a", i, back=1))
            sp.dma_start(kv[2][:, :, :], d["cache_win1"][0, bass.ds(i, 1)]
                         .rearrange("a (p r) k h e -> p (a r) (k h e)", r=4)).then_inc(kv_landed[2], 16)
            sp.dma_start(kv[3][0:64, :, :], d["cache_win2"][0, bass.ds(i, 1)]
                         .rearrange("a (p r) k h e -> p (a r) (k h e)", r=16)[:, 0:4, :]).then_inc(kv_landed[3], 16)
            sp.dma_start(win0[:, :], d["cache_win0"][0, bass.ds(i, 1)].rearrange("a p k h e -> p (a k h e)"))\
                .then_inc(landed["win0"], 16)

        with sp.Fori(0, 4) as i:
            for b in range(4):
                for j in range(4):
                    load(unit_no(U_MIX, 20, i, 5 * b + j),
                         rows(w_in, j * 512, SEG, i * UNIT_COLS + (OFF_G + b * D_MODEL)))
                load(unit_no(U_MIX, 20, i, 5 * b + 4), rows(d["p_" + "abcd"[b]][0], 0, P_CHUNKS[b], i * UNIT_COLS))

        with sp.Fori(0, 2) as i:
            for g in range(2):
                for j in range(4):
                    load(unit_no(U_GATE, 8, i, 4 * g + j), rows(d["w_o"][0], j * 512, SEG, i * 1024 + g * UNIT_COLS))

        def up(i):
            for v in range(2):
                for j in range(4):
                    load(ffn_unit(i, 4 * v + j), rows(w_up, j * 512, SEG, i * UNIT_COLS + v * D_FF))

        def down(i):
            for j in range(4):
                load(ffn_unit(i, 8 + j if not (isinstance(i, int) and i == 11) else j),
                     rows(w_down, i * 512 - 512, SEG, j * UNIT_COLS))
        up(0)
        up(1)
        down(1)
        with sp.Fori(2, 11) as i:
            up(i)
            down(i)
        down(11)

        sp.wait_ge(act.sem, act.at("tail_rows"))
        for c in range(7):
            nk = 13 if c < 2 * FC - 84 else 12
            r = c * TAIL
            for t, rows_out in ((0, o[8][0, 0]), (2, o[16][0].rearrange("n t c -> (n t) c"))):
                k = rows_out.shape[0]
                dst = bass.AP(rows_out.tensor, rows_out.offset + c * P, [[2 * D_FF, k], [7 * P, nk], [1, P]])
                store(dst, tail_rows[r + t:r + t + k, 0:nk, :])
        for m in range(3):
            sp.wait_ge(act.sem, act.at(("y", m)))
            sp.wait_ge(dve.sem, dve.at(("y", m)))
            if m < 2:
                store(o[0][0, m * P:m * P + P], y_nat[:, m, :])
            else:
                store(o[1].rearrange("n t c -> (n t) c"), y_nat[0:NS, 2, :])
        sp.wait_ge(stored, n_stored[0])
        sp.wait_ge(copied, 16 * 16)

    @block.gpsimd
    def _(e):
        e.memset(ident[:, :], 0.0).then_inc(pool.sem, pool.step("ident0"))
        e.memset(ones[:, :], 1.0).then_inc(pool.sem, pool.step("ones"))
        e.wait_ge(pool.sem, pool.at("ident0"))
        e.affine_select(out=ident[:, :], in_=ident[:, :], compare_op=ALU.not_equal, fill=1.0, base=0,
                        pattern=[[-1, P]], channel_multiplier=1).then_inc(pool.sem, pool.step("ident"))
        e.wait_ge(pool.sem, pool.at("ident"))
        e.memset(tab[32:33, :], NEG).then_inc(pool.sem, pool.step("tab_neg"))
        e.wait_ge(pool.sem, pool.at("tab_neg"))
        e.memset(tab_t[:, :, :, :], 0.0).then_inc(pool.sem, pool.step("tab_t0"))
        e.wait_ge(lo_ready, U_MIX)
        e.wait_ge(z_copied, 11)
        e.memset(xe_a[:, :, 0:HIST], 0.0).then_inc(pool.sem, pool.step("xe0"))
        e.tensor_copy(xe_a[:, :, HIST:XS], Z[:, X_D:N_MIX, 0:NP_TOK]).then_inc(pool.sem, pool.step("xe1"))
        for c in range(4):
            e.tensor_copy(view(xe_a, P, c * XE + XS + HIST, [[HIST + NT, NB], [1, NT]]),
                          view(Z, P, (X_D + c) * TOK + NP_TOK, [[NT, NB], [1, NT]]))\
                .then_inc(pool.sem, pool.step(("xe2", c)))
        e.wait_ge(pool.sem, pool.at(("xe2", 3)))
        e.wait_ge(dve.sem, dve.at("xe_hist"))
        e.tensor_tensor(xe_b[:, :, 1:XE], xe_a[:, :, 1:XE], xe_a[:, :, 0:XE - 1], ALU.add)\
            .then_inc(pool.sem, pool.step("s2"))
        e.wait_ge(pool.sem, pool.at("s2"))
        e.tensor_tensor(xe_a[:, 1:4, 3:XE], xe_b[:, 1:4, 3:XE], xe_b[:, 1:4, 1:XE - 2], ALU.add)\
            .then_inc(pool.sem, pool.step("s4"))
        e.wait_ge(pool.sem, pool.at("s4"))
        e.tensor_tensor(xe_b[:, 2:4, 7:XE], xe_a[:, 2:4, 7:XE], xe_a[:, 2:4, 3:XE - 4], ALU.add)\
            .then_inc(pool.sem, pool.step("s8"))
        e.wait_ge(pool.sem, pool.at("s8"))
        e.tensor_tensor(xe_a[:, 3, 15:XE], xe_b[:, 3, 15:XE], xe_b[:, 3, 7:XE - 8], ALU.add)\
            .then_inc(pool.sem, pool.step("s16"))
        e.wait_ge(act.sem, act.at("ws_T"))
        e.affine_select(out=ws_T[:, :, :], in_=ws_T[:, :, :], compare_op=ALU.is_ge, fill=0.0, base=0,
                        pattern=[[0, 4], [1, P]], channel_multiplier=-1).then_inc(pool.sem, pool.step("ws_T"))
        e.tensor_copy(z_own[:, :, :], Z[:, 0:30, NP_TOK:TOK]).then_inc(pool.sem, pool.step("z_own"))
        e.wait_ge(landed["oh_sample"], 16)
        e.memset(qpad_b[:, :, :], 0.0).then_inc(pool.sem, pool.step("qb0"))
        e.memset(qpad_a[:, :, :], 0.0).then_inc(pool.sem, pool.step("qa0"))
        e.memset(pt_a[:, :], 0.0).then_inc(pool.sem, pool.step("pt_a0"))
        e.wait_ge(pool.sem, pool.at("qa0"))
        for h in range(B_HEADS):
            e.tensor_copy(view(qpad_b, P, 20 * h, [[64, NB], [1, NT]]),
                          z_own[:, Q_B + h, :].rearrange("p (n t) -> p n t", t=NT))\
                .then_inc(pool.sem, pool.step(("qb", h)))
        for g in range(3):
            for h in range(HPG):
                src = z_own[:, Q_A + 2 * g + h, :].rearrange("p (n t) -> p n t", t=NT)
                e.tensor_copy(view(qpad_a, P, 16 * g + 12 * h, [[QA, NB], [1, NT]]), src)\
                    .then_inc(pool.sem, pool.step(("qa", g, h)))
                if g:
                    e.tensor_copy(view(qpad_a, P, 48 + 64 * (g - 1) + 36 * h, [[QA, NB], [9, NT]]), src)\
                        .then_inc(pool.sem, pool.step(("qa9", g, h)))
        e.wait_ge(pool.sem, pool.at(("qa9", 2, 1)))
        pool.begin("sample")
        with e.Fori(0, NB) as i:
            e.wait_ge(pe.sem, pe.at("own_b", i, back=1))
            e.tensor_copy(qs_b[:, :], view(qpad_b, P, i * 64, [[1, 64]])).then_inc(pool.sem, pool.step("qs_b"))
            e.wait_ge(pe.sem, pe.at("s_a", i, back=1))
            e.tensor_copy(qs_a[:, :], view(qpad_a, P, i * QA, [[1, QA]])).then_inc(pool.sem, pool.step("qs_a"))
        pool.end(NB)

        e.wait_ge(dve.sem, dve.at("hist_c"))
        e.wait_ge(dve.sem, dve.at(("ffn_pre", "lo", 3)))
        for s in range(2):
            e.memset(H[s][:, :, 0:2], 0.0).then_inc(pool.sem, pool.step(("H0", s)))
        with e.Fori(0, 11) as i:
            e.wait_ge(conv_step, i * 24)
            for s in range(2):
                for k in range(2):
                    e.tensor_copy(view(H[s], P, HS + k, [[HW, 4], [NT + 2, NB]]),
                                  view(hist_c, P, i * 64 + (FC * s * 16 + k), [[16, 4], [2, NB]]))\
                        .then_inc(hist_put, 1)
            for s in range(2):
                e.wait_ge(h_copied, i * 4 + (2 * s + 2))
                e.tensor_copy(view(tails, P, i * (4 * TAIL) + FC * s * TAIL, [[TAIL, 4], [1, 2]]),
                              H[s][:, :, NP_TOK:HS]).then_inc(tails_put, 1)
                for k in range(2):
                    e.tensor_copy(view(tails, P, i * (4 * TAIL) + (FC * s * TAIL + 2 + k), [[TAIL, 4], [2, NB]]),
                                  view(H[s], P, HS + NT + k, [[HW, 4], [NT + 2, NB]])).then_inc(tails_put, 1)

    @block.scalar
    def _(e):
        for name, dst, src in (
                ("nrow", nrow[0:16, :], d["norm_mix_pre"][0].rearrange("(c p) -> c p", p=P)),
                ("nrow", nrow[16:32, :], d["norm_mix_post"][0].rearrange("(c p) -> c p", p=P)),
                ("nrow", nrow[32:48, :], d["norm_ffn_pre"][0].rearrange("(c p) -> c p", p=P)),
                ("nrow", nrow[48:64, :], d["norm_ffn_post"][0].rearrange("(c p) -> c p", p=P)),
                ("nrow", nrow[64:68, :], d["c_ln_g"][0].rearrange("(c p) -> c p", p=P)),
                ("nrow", nrow[68:72, :], d["d_scale"][0].rearrange("(c p) -> c p", p=P)),
                ("tab", tab[0:32, :], d["rel_bias_table"]),
                ("prow", prow[:, 0:3, :], d["conv_w"][0].rearrange("w (c p) -> c w p", p=P)),
                ("prow", prow[:, 3, :], d["conv_b"][0].rearrange("(c p) -> c p", p=P)),
                ("oh_prompt", oh_prompt[:, :, :], d["c_prompt"].rearrange("b (g i) -> b g i", g=4)),
                ("pages", pages[:, :], d["page_table"].rearrange("n q -> (n q)").rearrange("(a m) -> a m", a=1)),
                ("small", bs[:, :, :], d["c_bs"]),
                ("small", ramp[:, :], d["c_ramp"].to_broadcast([P, 64])),
                ("small", spread[:, :], d["c_spread"]),
                ("small", same[:, :], d["c_same"]),
                ("small", rank[:, :], d["c_rank"])):
            e.dma_start(dst, src).then_inc(landed[name], 16)

        def hi(no, k=SEG, n=UNIT_COLS):
            u, r, slot, s = no
            e.wait_ge(w_landed[slot], r * 16 + 16)
            if not isinstance(u, int) or u >= N_SPLIT:
                e.wait_ge(unit_done, u - 1)
            e.activation(w_hi[s][:, 0:k, 0:n], w_raw[slot][:, 0:k, 0:n], ACT.Copy).then_inc(hi_ready, 1)

        def squares(tag, src, sq, q, ready):
            for s, v in ready:
                e.wait_ge(s, v)
            e.activation(sq[:, q], src[:, 4 * q:4 * q + 4, :], ACT.Square).then_inc(act.sem, act.step((tag, "sq", q)))

        def root(tag):
            e.wait_ge(dve.sem, dve.at((tag, "var")))
            e.activation(stat[:, 1, :], stat[:, 0, :], ACT.Sqrt).then_inc(act.sem, act.step((tag, "sd")))

        def norm_hi(tag, src, q):
            e.wait_ge(dve.sem, dve.at((tag, "w", 4 * q + 3)))
            e.activation(xn_hi[:, 4 * q:4 * q + 4, :], src[:, 4 * q:4 * q + 4, :], ACT.Copy)\
                .then_inc(act.sem, act.step((tag, "hi", q)))

        for c in range(1, KC, 2):
            e.wait_ge(pe.sem, pe.at(("xT", c)))
            e.activation(x_T[:, c, :], ps[:, 5, 0:TOK], ACT.Copy).then_inc(act.sem, act.step(("x_T", c)))
        e.wait_ge(dve.sem, dve.at(("x_T", KC - 2)))
        e.wait_ge(act.sem, act.at(("x_T", KC - 1)))
        e.dma_start(x_dram.ap(), x_T[:, :, :]).then_inc(landed["x_saved"], 16)
        for q in range(4):
            squares("mix_pre", x_T, sq_a, q, [])
        hi(unit_no(0, 8, 0, 0))
        root("mix_pre")
        hi(unit_no(0, 8, 0, 1))

        def bias_rows(h0, h1):
            for h in range(h0, h1):
                e.wait_ge(pe.sem, pe.at(("urow", h)))
                if h >= 4:
                    e.wait_ge(u_stored[h % 4], 16 * (h // 4))
                e.activation(urow[:, h % 4, :], ps[:, 4 + h % 3, 0:384], ACT.Copy)\
                    .then_inc(act.sem, act.step(("urow", h)))
        bias_rows(0, 2)
        norm_hi("mix_pre", xw, 0)
        bias_rows(2, 3)
        for q in range(1, 4):
            norm_hi("mix_pre", xw, q)
        bias_rows(3, 6)

        def z_out(g, side, n, done):
            e.wait_ge(unit_done, done)
            e.activation(Z[:, bass.ds(g * 4, n), :], ps[:, 4 * side:4 * side + n, 0:TOK], ACT.Copy).then_inc(z_copied, 1)
        hi(unit_no(0, 8, 0, 2))
        bias_rows(6, 9)
        hi(unit_no(0, 8, 0, 3))
        bias_rows(9, N_HEADS)
        with e.Fori(0, 4) as i:
            for h in range(2):
                for j in range(4):
                    hi(unit_no(4, 8, i, 4 * h + j))
                    if j == 1:
                        z_out(i * 2 + h, h, 4, i * 8 + (4 + 4 * h))
        for g in range(2):
            for j in range(4):
                hi(unit_no(36 + 4 * g, 8, 0, j), n=256 if g else UNIT_COLS)
                if j == 1:
                    z_out(8 + g, g, 4, 36 + 4 * g)
        z_out(10, 0, 2, U_MIX)
        e.wait_ge(unit_done, U_MIX)
        e.dma_start(ws_nat[:, :, :], d["c_ws"][0].rearrange("g t s -> t g s")).then_inc(landed["ws"], 16)
        e.wait_ge(lo_ready, U_MIX)
        e.dma_start(dw[:, :, :], d["d_w"][0].rearrange("g c e -> c g e")).then_inc(landed["dw"], 16)
        e.wait_ge(landed["u"], 16)
        e.dma_start(hist_rows[:, :], d["state_pool"][0].rearrange("n j c -> (n j) c")).then_inc(landed["hist"], 16)
        e.wait_ge(z_copied, 11)
        e.activation(Z[:, U_C:X_D, :], Z[:, U_C:X_D, :], ACT.Gelu_apprx_tanh).then_inc(act.sem, act.step("gelu"))
        for m in range(3):
            n = P if m < 2 else NS
            e.wait_ge(pe.sem, pe.at(("tok", 2 * m)))
            e.activation(k_tok[0:n, m, :], view(ps, n, 0, [[1, 1280]]), ACT.Copy)\
                .then_inc(act.sem, act.step(("k_tok", m)))
        e.wait_ge(dve.sem, dve.at("xc"))
        e.activation(sq_c[:, :, :], vn[:, :, :], ACT.Square).then_inc(act.sem, act.step("xc_sq"))
        e.wait_ge(dve.sem, dve.at("c_var"))
        e.activation(stat[:, 1, :], stat[:, 0, :], ACT.Sqrt).then_inc(act.sem, act.step("c_sd"))
        e.wait_ge(pe.sem, pe.at("ws_T"))
        e.activation(ws_T[:, :, :], view(ps, P, 6 * 512, [[P, 4], [1, P]]), ACT.Copy)\
            .then_inc(act.sem, act.step("ws_T"))
        e.wait_ge(pe.sem, pe.at("xdT"))
        e.activation(xd_rows[0:HIST, 0, :], ps[0:HIST, 7, :], ACT.Copy).then_inc(act.sem, act.step("xd_prompt"))
        e.activation(xd_rows[:, 1, :], ps[0:NS, 3, :], ACT.Copy).then_inc(act.sem, act.step("xd_own"))
        e.wait_ge(landed["x_saved"], 16)
        for c in range(4):
            e.wait_ge(pe.sem, pe.at(("dy", c)))
            e.activation(O[:, 10 + c, :], ps[:, (1, 2, 6, 7)[c], 0:TOK], ACT.Identity,
                         scale=gains[:, NORM["d_scale"] + c:NORM["d_scale"] + c + 1])\
                .then_inc(act.sem, act.step(("od", c)))

        def prompt_out(k):
            groups, oc, m = units[k]
            e.wait_ge(pe.sem, pe.at(("PV", k)))
            e.activation(O[:, oc, m * P:m * P + P], ps[:, 3 * (k % 2), 384:512], ACT.Copy)\
                .then_inc(act.sem, act.step(("O", k)))
        for k, (groups, oc, m) in enumerate(units):
            n = len(groups) * (m + 1) * P
            e.wait_ge(dve.sem, dve.at(("nm", k)))
            e.activation(Lp[:, k % 2, 0:n], Lp[:, k % 2, 0:n], ACT.Exp, bias=col[:, k % 2:k % 2 + 1],
                         accum_out=col[:, 2 + k % 2:3 + k % 2]).then_inc(act.sem, act.step(("E", k)))
            if k:
                prompt_out(k - 1)
            e.wait_ge(pe.sem, pe.at(("PT", k)))
            e.activation(PTp[:, k % 2, 0:n], view(ps, P, 6 * 512, [[1, n]]), ACT.Copy)\
                .then_inc(act.sem, act.step(("pt", k)))
        prompt_out(NU - 1)

        act.begin("sample")
        with e.Fori(0, NB) as i:
            for q in range(0, 8, 2):
                e.wait_ge(pe.sem, pe.at(("kT", q), i))
                e.activation(kt_b[:, 0, :], ps[:, q % 4, :], ACT.Copy).then_inc(act.sem, act.step(("kt_b", q)))
            for b in (0, 2):
                e.wait_ge(pe.sem, pe.at(("kTa", b), i))
                e.activation(kt_a[:, b, :], ps[:, b, :], ACT.Copy).then_inc(act.sem, act.step(("kt_a", b)))
            e.wait_ge(dve.sem, dve.at("nm_b", i))
            e.activation(L_b[:, :], L_b[:, :], ACT.Exp, bias=col[0:16, 0:1], accum_out=col[0:16, 1:2])\
                .then_inc(act.sem, act.step("E_b"))
            e.wait_ge(pe.sem, pe.at("ptb", i))
            e.activation(pt_b[:, 0:8, :], view(ps, P, 7 * 512, [[16, 8], [1, 16]]), ACT.Copy)\
                .then_inc(act.sem, act.step("pt_b0"))
            e.activation(pt_b[0:NS, 8, :], ps[0:NS, 7, 128:144], ACT.Copy).then_inc(act.sem, act.step("pt_b"))
            e.wait_ge(dve.sem, dve.at("nm_a", i))
            e.activation(L_a[:, :], L_a[:, :], ACT.Exp, bias=col[0:8, 3:4], accum_out=col[0:8, 4:5])\
                .then_inc(act.sem, act.step("E_a"))
            e.wait_ge(pe.sem, pe.at("pv_b", i))
            e.wait_ge(dve.sem, dve.at("rs_b", i))
            e.activation(ob[:, :], ps[0:16, 4, :], ACT.Identity, scale=col[0:16, 2:3]).then_inc(act.sem, act.step("ob"))
            e.wait_ge(pe.sem, pe.at("pv_a", i))
            e.wait_ge(dve.sem, dve.at("rs_a", i))
            e.activation(oa[:, :], ps[0:8, 6, 0:256], ACT.Identity, scale=col[0:8, 5:6]).then_inc(act.sem, act.step("oa"))
        act.end(NB)

        e.wait_ge(pe.sem, pe.at("ota", NB - 1))
        e.wait_ge(dve.sem, dve.at("o_a", NB - 1))
        for j in range(2):
            hi(unit_no(U_MIX, 20, 0, j))
        for h in range(2):
            e.activation(O_hi[:, 7 * h:7 * h + 7, :], O[:, 7 * h:7 * h + 7, :], ACT.Copy)\
                .then_inc(act.sem, act.step(("O_hi", h)))
        with e.Fori(0, 4) as i:
            for b in range(4):
                for j in range(2, 4):
                    hi(unit_no(U_MIX, 20, i, 5 * b + j))
                hi(unit_no(U_MIX, 20, i, 5 * b + 4), k=P_CHUNKS[b])
                hi(unit_no(U_MIX, 20, i, 5 * b + 5))
                e.wait_ge(unit_done, i * 20 + (U_MIX + 5 * b + 4))
                e.wait_ge(p_used, i * 4 + b)
                e.activation(sig[:, :, :], ps[:, 0:4, 0:TOK], ACT.Sigmoid).then_inc(sig_ready, 1)
                g, n0, nb = ((1, 0, 2), (2, 0, 1), (2, 1, 1), (0, 0, 2))[b]
                first = NT if g < 2 else 0
                e.dma_start(o[9 + g][0, bass.ds(i * 2 + n0, nb), 0:WIN_LEN[g] - first],
                            d[f"cache_win{g}"][0, bass.ds(i * 2 + n0, nb), first:WIN_LEN[g]]).then_inc(copied, 16)
                hi(unit_no(U_MIX, 20, i, 5 * b + 6))
            e.wait_ge(merged_f, i + 1)
            e.activation(M_hi[:, bass.ds(i * 4, 4), :], acc[:, :, :], ACT.Copy).then_inc(merged_hi, 1)

        e.wait_ge(merged_lo, 4)
        e.dma_start(x1[:, :, :], x_dram.ap()).then_inc(landed["x_back"], 16)
        for c in range(8):
            rows_in = d["state_conv"][0].rearrange("n t c -> (n t) c")
            e.dma_start(crow[16 * c:16 * c + 16, :, :],
                        bass.AP(rows_in.tensor, rows_in.offset + c * P, [[2 * D_FF, 16], [8 * P, 11], [1, P]]))\
                .then_inc(landed["crow"], 16)
        for n in range(2, 18):
            hi(unit_no(U_GATE, 8, 0, n))
            if n % 4 == 1:
                g = n // 4 - 1
                e.wait_ge(unit_done, U_GATE + 4 * g + 4)
                e.activation(m_T[:, 4 * g:4 * g + 4, :], ps[:, 4 * (g % 2):4 * (g % 2) + 4, 0:TOK], ACT.Copy)\
                    .then_inc(m_copied, 1)
                squares("mix_post", m_T, sq_b, g, [(m_copied, g + 1)])
        root("mix_post")
        for q in range(4):
            squares("ffn_pre", x1, sq_b, q, [(dve.sem, dve.at(("x1", q)))])
        root("ffn_pre")
        for q in range(4):
            norm_hi("ffn_pre", xw_b, q)

        def h_out(i, s, done):
            e.wait_ge(unit_done, done)
            e.wait_ge(conv_step, i * 24)
            e.wait_ge(tails_put, i * 6)
            e.wait_ge(pool.sem, pool.at(("H0", 1)))
            src = ps[:, 4 * s:4 * s + 4, :]
            e.activation(H[s][:, :, 2:HS], src[:, :, 0:NP_TOK], ACT.Copy).then_inc(h_copied, 1)
            e.activation(view(H[s], P, HS + 2, [[HW, 4], [NT + 2, NB], [1, NT]]),
                         view(ps, P, 2048 * s + NP_TOK, [[512, 4], [NT, NB], [1, NT]]), ACT.Copy).then_inc(h_copied, 1)

        def act_high(i):
            e.wait_ge(act_f, i)
            e.activation(act_hi[:, :, 0:NP_TOK], hc[0][:, :, 0:NP_TOK], ACT.Copy).then_inc(act_hi_ready, 1)
            e.activation(view(act_hi, P, NP_TOK, [[TOK, 4], [NT, NB], [1, NT]]),
                         view(hc[0], P, HS, [[HW, 4], [NT + 2, NB], [1, NT]]), ACT.Copy).then_inc(act_hi_ready, 1)

        def ffn_round(i):
            down = not isinstance(i, int) or i > 0
            u0 = ffn_unit(i, 0)[0]
            if not isinstance(i, int):
                hi(ffn_unit(i, 0))
                hi(ffn_unit(i, 1))
            if down:
                act_high(i)
            for j in range(2, 6):
                hi(ffn_unit(i, j))
            h_out(i, 0, u0 + 4)
            hi(ffn_unit(i, 6))
            hi(ffn_unit(i, 7))
            for j in (8, 9):
                hi(ffn_unit(i, j) if down else ffn_unit(1, j - 8))
            h_out(i, 1, u0 + 8)
            e.wait_ge(conv_step, i * 24 + 12)
            e.activation(hc[0][:, :, 0:HW - 2], hc[0][:, :, 0:HW - 2], ACT.Gelu_apprx_tanh).then_inc(gelu_done, 1)
            if down:
                hi(ffn_unit(i, 10))
                hi(ffn_unit(i, 11))
        ffn_round(0)
        ffn_round(1)
        with e.Fori(2, 11) as i:
            ffn_round(i)
        hi(ffn_unit(11, 0))
        e.wait_ge(unit_done, ffn_unit(11, 0)[0])
        act_high(11)
        hi(ffn_unit(11, 1))
        hi(ffn_unit(11, 2))
        hi(ffn_unit(11, 3))
        e.wait_ge(lo_ready, 272)
        e.wait_ge(pe.sem, pe.at("tailT"))
        e.activation(tail_rows[:, 0:12, :], view(ps, 7 * TAIL, 0, [[P, 12], [1, P]]), ACT.Copy)\
            .then_inc(act.sem, act.step("tail_rows0"))
        e.activation(tail_rows[0:4 * TAIL, 12, :], ps[0:4 * TAIL, 3, 0:P], ACT.Copy)\
            .then_inc(act.sem, act.step("tail_rows"))
        for q in range(4):
            squares("ffn_post", m_T, sq_f, q, [(y_added, 4 + 4 * 10 + q + 1)])
        root("ffn_post")
        for m in range(3):
            n = P if m < 2 else NS
            e.wait_ge(pe.sem, pe.at(("yT", m)))
            b = 4 * ((m + 1) % 2)
            e.activation(y_nat[0:n, m, 0:1024], view(ps, n, b * 512, [[1, 1024]]), ACT.Copy)\
                .then_inc(act.sem, act.step(("y", m)))

    @block.vector
    def _(e):
        def lo(no, k=SEG, n=UNIT_COLS):
            u, _, slot, s = no
            e.wait_ge(hi_ready, u + 1)
            e.tensor_tensor(w_lo[s][:, 0:k, 0:n], w_raw[slot][:, 0:k, 0:n], w_hi[s][:, 0:k, 0:n].bitcast(F32),
                            ALU.subtract).then_inc(lo_ready, 1)

        def variance(tag, bank, n, name):
            e.wait_ge(pe.sem, pe.at(name))
            e.tensor_scalar(stat[:, 0, :], ps[:, bank, 0:TOK], 1.0 / n, EPS, ALU.mult, ALU.add)\
                .then_inc(dve.sem, dve.step((tag, "var")))

        def rstd(tag):
            e.wait_ge(act.sem, act.at((tag, "sd")))
            e.reciprocal(stat[:, 2, :], stat[:, 1, :]).then_inc(dve.sem, dve.step((tag, "rstd")))
            e.wait_ge(dve.sem, dve.at((tag, "rstd")))

        def scaled(tag, dst, src, q):
            g = NORM[tag]
            for c in range(4 * q, 4 * q + 4):
                e.scalar_tensor_tensor(out=dst[:, c, :], in0=src[:, c, :], scalar=gains[:, g + c:g + c + 1],
                                       in1=stat[:, 2, :], op0=ALU.mult, op1=ALU.mult)\
                    .then_inc(dve.sem, dve.step((tag, "w", c)))

        def norm_lo(tag, src, q):
            e.wait_ge(act.sem, act.at((tag, "hi", q)))
            e.tensor_tensor(xn_lo[:, 4 * q:4 * q + 4, :], src[:, 4 * q:4 * q + 4, :],
                            xn_hi[:, 4 * q:4 * q + 4, :].bitcast(F32), ALU.subtract)\
                .then_inc(dve.sem, dve.step((tag, "lo", q)))

        def norm(tag, dst, src, before):
            for q in (0, 1):
                scaled(tag, dst, src, q)
                before(q)
                norm_lo(tag, dst, q)
            for q in (2, 3):
                scaled(tag, dst, src, q)
            for q in (2, 3):
                norm_lo(tag, dst, q)

        for c in range(0, KC, 2):
            e.wait_ge(pe.sem, pe.at(("xT", c)))
            e.tensor_copy(x_T[:, c, :], ps[:, 4, 0:TOK]).then_inc(dve.sem, dve.step(("x_T", c)))
        e.wait_ge(landed["tab"], 16)
        e.wait_ge(pool.sem, pool.at("tab_t0"))
        e.tensor_copy(tabx[:, :, :], view(tab, 33, 0, [[1, N_HEADS], [0, P]])).then_inc(dve.sem, dve.step("tabx"))
        e.tensor_copy(view(tab_t, 33, 0, [[4, N_HEADS], [41, NT]]), view(tab, 33, 0, [[1, N_HEADS], [0, NT]]))\
            .then_inc(dve.sem, dve.step("tab_t"))
        e.tensor_copy(tab_all[:, :, :], view(tab, 33, 0, [[1, N_HEADS], [0, NT]]))\
            .then_inc(dve.sem, dve.step("tab_all"))
        e.wait_ge(pe.sem, pe.at("nrowT"))
        e.tensor_copy(gains[:, :], ps[:, 6, 0:72]).then_inc(dve.sem, dve.step("gains"))
        variance("mix_pre", 7, D_MODEL, ("mix_pre", "ss", 3))
        e.wait_ge(pe.sem, pe.at("prowT"))
        e.tensor_copy(conv[:, :, :], view(ps, P, 5 * 512, [[88, 4], [1, 88]])).then_inc(dve.sem, dve.step("conv"))
        rstd("mix_pre")
        e.wait_ge(act.sem, act.at(("x_T", KC - 1)))
        norm("mix_pre", xw, x_T, lambda q: lo(unit_no(0, 8, 0, q)))

        for j in range(2, 4):
            lo(unit_no(0, 8, 0, j))
        with e.Fori(0, 4) as i:
            for j in range(8):
                lo(unit_no(4, 8, i, j))
        for j in range(4):
            lo(unit_no(36, 8, 0, j))
        for j in range(4):
            lo(unit_no(40, 8, 0, j), n=256)

        e.wait_ge(pe.sem, pe.at("vsum"))
        e.wait_ge(lo_ready, U_MIX)
        e.scalar_tensor_tensor(out=vn[:, :, :], in0=view(ps, P, 6 * 512, [[0, 4], [1, TOK]]), scalar=-1.0 / 512,
                               in1=Z[:, V_C:X_D, :], op0=ALU.mult, op1=ALU.add).then_inc(dve.sem, dve.step("xc"))
        e.wait_ge(landed["x_saved"], 16)
        for m in range(3):
            e.wait_ge(pe.sem, pe.at(("tok", 2 * m + 1)))
            n = P if m < 2 else NS
            dst = v_tok[:, m, :] if m < 2 else v_own[:, :]
            e.tensor_copy(dst, view(ps, n, 3 * 512, [[1, 1280]])).then_inc(dve.sem, dve.step(("v_tok", m)))
        e.wait_ge(pe.sem, pe.at("vvar"))
        e.tensor_scalar(stat[:, 0, :], ps[:, 7, 0:TOK], 1.0 / 512, EPS, ALU.mult, ALU.add)\
            .then_inc(dve.sem, dve.step("c_var"))
        e.wait_ge(pe.sem, pe.at("histT"))
        for c in range(4):
            e.tensor_copy(view(xe_a, P, c * XE + XS, [[HIST + NT, NB], [1, HIST]]),
                          view(ps, P, 6 * 512 + 120 * c, [[HIST, NB], [1, HIST]]))\
                .then_inc(dve.sem, dve.step("xe_hist" if c == 3 else ("xe_hist", c)))
        e.wait_ge(act.sem, act.at("c_sd"))
        e.reciprocal(stat[:, 2, :], stat[:, 1, :]).then_inc(dve.sem, dve.step("c_rstd"))
        e.wait_ge(dve.sem, dve.at("c_rstd"))
        for c in range(4):
            g = NORM["c_ln"] + c
            e.scalar_tensor_tensor(out=vn[:, c, :], in0=vn[:, c, :], scalar=gains[:, g:g + 1], in1=stat[:, 2, :],
                                   op0=ALU.mult, op1=ALU.mult).then_inc(dve.sem, dve.step(("vn", c)))
        for m in range(3):
            n = P if m < 2 else NS
            e.wait_ge(pe.sem, pe.at(("vnT", m)))
            e.tensor_copy(vc_tok[0:n, m, :], ps[0:n, m, :]).then_inc(dve.sem, dve.step(("vc", m)))
        e.wait_ge(pe.sem, pe.at("wrep"))
        for g in range(4):
            e.tensor_tensor(wd[:, g, :, :], view(ps, NS, 7 * 512 + 4 * g, [[0, NB], [1, NT]]),
                            view(same, NS, 0, [[1, NB], [0, NT]]), ALU.mult)\
                .then_inc(dve.sem, dve.step(("wd", g)))
        for g in range(4):
            e.tensor_copy(bs_own[:, g, :, :], view(bs, 1, P * g, [[0, NB], [1, NT]]))\
                .then_inc(dve.sem, dve.step(("bs_own", g)))
        for m in range(3):
            e.wait_ge(pe.sem, pe.at(("mix", m)))
            t0, n = m * P, P if m < 2 else NS
            e.tensor_tensor(O[:, 6:10, t0:t0 + n], view(ps, P, (3 + m) * 512, [[n, 4], [1, n]]),
                            Z[:, U_C:V_C, t0:t0 + n], ALU.mult).then_inc(dve.sem, dve.step(("oc", m)))
        e.wait_ge(pool.sem, pool.at("s16"))
        sums = [xe_b, xe_a, xe_b, xe_a]
        for c in range(4):
            e.tensor_tensor(sums[c][:, c, HIST:HIST + 15], sums[c][:, c, HIST:HIST + 15],
                            ramp[:, 16 * c:16 * c + 15], ALU.mult).then_inc(dve.sem, dve.step(("ramp", c)))
        e.wait_ge(dve.sem, dve.at(("ramp", 3)))
        for c in range(4):
            e.scalar_tensor_tensor(out=pooled[:, c, 0:NP_TOK], in0=sums[c][:, c, HIST:XS], scalar=1.0 / D_WIN[c],
                                   in1=Z[:, X_D + c, 0:NP_TOK], op0=ALU.mult, op1=ALU.subtract)\
                .then_inc(dve.sem, dve.step(("pooled0", c)))
            e.scalar_tensor_tensor(out=view(pooled, P, c * TOK + NP_TOK, [[NT, NB], [1, NT]]),
                                   in0=view(sums[c], P, c * XE + XS + HIST, [[HIST + NT, NB], [1, NT]]),
                                   scalar=1.0 / D_WIN[c],
                                   in1=view(Z, P, (X_D + c) * TOK + NP_TOK, [[NT, NB], [1, NT]]),
                                   op0=ALU.mult, op1=ALU.subtract).then_inc(dve.sem, dve.step(("pooled", c)))

        def logits(k):
            groups, oc, m = units[k]
            ng, nk, h0 = len(groups), (m + 1) * P, groups[0][3]
            n = ng * nk
            e.wait_ge(pe.sem, pe.at(("S", k)))
            if k >= 2:
                e.wait_ge(pe.sem, pe.at(("PT", k - 2)))
            e.scalar_tensor_tensor(out=view(Lp, P, 768 * (k % 2), [[nk, ng], [1, nk]]),
                                   in0=view(ps, P, 1536 * (k % 2), [[512, ng], [1, nk]]), scalar=SCALE,
                                   in1=view(U, P, h0 * 256 + 256 - nk, [[512, ng], [1, nk]]),
                                   op0=ALU.mult, op1=ALU.add).then_inc(dve.sem, dve.step(("L", k)))
            e.wait_ge(dve.sem, dve.at(("L", k)))
            e.tensor_reduce(col[:, k % 2:k % 2 + 1], Lp[:, k % 2, 0:n], AX.X, ALU.max, negate=True)\
                .then_inc(dve.sem, dve.step(("nm", k)))

        def normalise(k):
            groups, oc, m = units[k]
            n = len(groups) * (m + 1) * P
            e.wait_ge(act.sem, act.at(("E", k)))
            e.reciprocal(col[:, 4 + k % 2:5 + k % 2], col[:, 2 + k % 2:3 + k % 2])\
                .then_inc(dve.sem, dve.step(("rs", k)))
            e.wait_ge(dve.sem, dve.at(("rs", k)))
            e.tensor_scalar(Lp[:, k % 2, 0:n], Lp[:, k % 2, 0:n], col[:, 4 + k % 2:5 + k % 2], None, ALU.mult)\
                .then_inc(dve.sem, dve.step(("P", k)))
        e.wait_ge(landed["u"], 16)
        logits(0)
        for k in range(NU):
            if k + 1 < NU:
                logits(k + 1)
            normalise(k)

        for k in range(2):
            e.wait_ge(pe.sem, pe.at(("bias_b", k)))
            e.tensor_copy(bias_b[:, 512 * k:512 * k + 512], ps[0:16, k, :]).then_inc(dve.sem, dve.step(("bias_b", k)))
        e.wait_ge(pe.sem, pe.at("bias_a"))
        e.tensor_copy(bias_a[:, 0:320], ps[0:8, 2, 0:320]).then_inc(dve.sem, dve.step("bias_past"))
        for g in range(3):
            e.tensor_copy(view(bias_a, 8, 320 + 32 * g, [[96, NB], [1, NS]]),
                          view(ps, 8, (3 * 512, 4 * 512, 4 * 512 + 256)[g], [[NS, NB], [1, NS]]))\
                .then_inc(dve.sem, dve.step(("bias_own", g)))
        e.tensor_copy(bias_b[:, PAST:PAST + NB * NS], ps[0:16, 5, 0:NB * NS]).then_inc(dve.sem, dve.step("bias"))
        e.wait_ge(dve.sem, dve.at("bias"))
        e.wait_ge(pool.sem, pool.at("pt_a0"))

        dve.begin("sample")
        with e.Fori(0, NB) as i:
            def then(ins, name):
                ins.then_inc(dve.sem, dve.step(name))
                e.wait_ge(dve.sem, dve.at(name, i))
            for q in range(1, 8, 2):
                e.wait_ge(pe.sem, pe.at(("kT", q), i))
                e.tensor_copy(kt_b[:, 1, :], ps[:, q % 4, :]).then_inc(dve.sem, dve.step(("kt_b", q)))
            e.wait_ge(pe.sem, pe.at(("S_b", 7), i))
            e.wait_ge(pe.sem, pe.at("ptb", i, back=1))
            e.tensor_reduce(col[0:16, 6:10], view(ps, 16, 4 * 512, [[BLOCK_KEYS, N_BLOCKS], [1, BLOCK_KEYS]]),
                            AX.X, ALU.add).then_inc(dve.sem, dve.step("blocks"))
            e.scalar_tensor_tensor(out=L_b[:, 0:PAST], in0=view(ps, 16, 4 * 512, [[1, PAST]]), scalar=SCALE,
                                   in1=bias_b[:, 0:PAST], op0=ALU.mult, op1=ALU.add)\
                .then_inc(dve.sem, dve.step("L_b0"))
            e.wait_ge(pe.sem, pe.at("own_b", i))
            e.scalar_tensor_tensor(out=L_b[:, PAST:PAST + NS], in0=ps[0:16, 7, 0:NS], scalar=SCALE,
                                   in1=view(bias_b, 16, i * NS + PAST, [[1, NS]]), op0=ALU.mult, op1=ALU.add)\
                .then_inc(dve.sem, dve.step("L_b"))
            for b in (1, 3):
                n = 512 if b == 1 else 256
                e.wait_ge(pe.sem, pe.at(("kTa", b), i))
                e.tensor_copy(kt_a[:, b, 0:n], ps[:, b, 0:n]).then_inc(dve.sem, dve.step(("kt_a", b)))
            e.wait_ge(dve.sem, dve.at("L_b", i))
            then(e.tensor_reduce(col[0:16, 10:11], col[0:16, 6:10], AX.X, ALU.min), "least")
            then(e.scalar_tensor_tensor(out=col[0:16, 12:16], in0=col[0:16, 6:10], scalar=col[0:16, 10:11],
                                        in1=rank[:, :], op0=ALU.is_equal, op1=ALU.mult), "ranks")
            then(e.tensor_reduce(col[0:16, 11:12], col[0:16, 12:16], AX.X, ALU.max), "last")
            then(e.tensor_scalar(col[0:16, 12:16], col[0:16, 12:16], col[0:16, 11:12], NEG,
                                 ALU.is_equal, ALU.mult), "drop")
            then(e.tensor_tensor(L_b[:, 0:PAST], L_b[:, 0:PAST],
                                 view(col, 16, 12, [[1, N_BLOCKS], [0, BLOCK_KEYS]]), ALU.add), "masked")
            e.tensor_reduce(col[0:16, 0:1], L_b[:, :], AX.X, ALU.max, negate=True).then_inc(dve.sem, dve.step("nm_b"))
            e.wait_ge(pe.sem, pe.at("s_a", i))
            e.scalar_tensor_tensor(out=L_a[:, 0:320], in0=ps[0:8, 6, 0:320], scalar=SCALE, in1=bias_a[:, 0:320],
                                   op0=ALU.mult, op1=ALU.add).then_inc(dve.sem, dve.step("L_a0"))
            then(e.scalar_tensor_tensor(out=L_a[:, 320:416], in0=ps[0:8, 6, 320:416], scalar=SCALE,
                                        in1=view(bias_a, 8, i * 96 + 320, [[1, 96]]),
                                        op0=ALU.mult, op1=ALU.add), "L_a")
            e.tensor_reduce(col[0:8, 3:4], L_a[:, :], AX.X, ALU.max, negate=True).then_inc(dve.sem, dve.step("nm_a"))
            e.wait_ge(act.sem, act.at("E_b", i))
            e.reciprocal(col[0:16, 2:3], col[0:16, 1:2]).then_inc(dve.sem, dve.step("rs_b"))
            e.wait_ge(act.sem, act.at("E_a", i))
            e.reciprocal(col[0:8, 5:6], col[0:8, 4:5]).then_inc(dve.sem, dve.step("rs_a"))
            e.wait_ge(pe.sem, pe.at("pta", i))
            e.tensor_copy(pt_a[:, 0:8], ps[:, 5, 0:8]).then_inc(dve.sem, dve.step("pt_a0"))
            e.tensor_copy(view(pt_a, P, 8, [[4, HPG], [9, NT]]), view(ps, P, 5 * 512 + 8, [[4, HPG], [1, NT]]))\
                .then_inc(dve.sem, dve.step("pt_a1"))
            e.tensor_copy(view(pt_a, 64, 40, [[4, HPG], [9, NT]]), view(ps, 64, 5 * 512 + 16, [[4, HPG], [1, NT]]))\
                .then_inc(dve.sem, dve.step("pt_a2"))
            e.tensor_copy(pt_a[0:NS, 72:96], ps[0:NS, 5, 24:48]).then_inc(dve.sem, dve.step("pt_a"))
            e.wait_ge(pe.sem, pe.at("otb", i))
            e.tensor_copy(view(O, P, i * NT + (2 * TOK + NP_TOK), [[TOK, B_HEADS], [1, NT]]),
                          view(ps, P, 7 * 512, [[20, B_HEADS], [1, NT]])).then_inc(dve.sem, dve.step("o_b"))
            e.wait_ge(pe.sem, pe.at("ota", i))
            e.tensor_copy(view(O, P, i * NT + NP_TOK, [[TOK, HPG], [1, NT]]),
                          view(ps, P, 5 * 512, [[12, HPG], [1, NT]])).then_inc(dve.sem, dve.step("o_a"))
        dve.end(NB)

        for j in range(2):
            lo(unit_no(U_MIX, 20, 0, j))
        for h in range(2):
            e.wait_ge(act.sem, act.at(("O_hi", h)))
            e.tensor_tensor(O_lo[:, 7 * h:7 * h + 7, :], O[:, 7 * h:7 * h + 7, :],
                            O_hi[:, 7 * h:7 * h + 7, :].bitcast(F32), ALU.subtract)\
                .then_inc(dve.sem, dve.step(("O_lo", h)))
        with e.Fori(0, 4) as i:
            def merge(b):
                e.wait_ge(unit_done, i * 20 + (U_MIX + 5 * b + 5))
                e.wait_ge(sig_ready, i * 4 + (b + 1))
                if b == 0:
                    e.wait_ge(merged_lo, i)
                dst = tmp if b else acc
                e.tensor_tensor(dst[:, :, :], ps[:, 4:8, 0:TOK], sig[:, :, :], ALU.mult).then_inc(p_used, 1)
                if b:
                    e.wait_ge(p_used, i * 4 + (b + 1))
                    if b >= 2:
                        e.wait_ge(merge_step, i * 2 + (b - 1))
                    e.tensor_tensor(acc[:, :, :], acc[:, :, :], tmp[:, :, :], ALU.add)\
                        .then_inc(merge_step if b < 3 else merged_f, 1)
            for b in range(4):
                for j in range(2, 4):
                    lo(unit_no(U_MIX, 20, i, 5 * b + j))
                lo(unit_no(U_MIX, 20, i, 5 * b + 4), k=P_CHUNKS[b])
                lo(unit_no(U_MIX, 20, i, 5 * b + 5))
                merge(b)
                lo(unit_no(U_MIX, 20, i, 5 * b + 6))
            e.wait_ge(merged_hi, i + 1)
            e.tensor_tensor(M_lo[:, bass.ds(i * 4, 4), :], acc[:, :, :], M_hi[:, bass.ds(i * 4, 4), :].bitcast(F32),
                            ALU.subtract).then_inc(merged_lo, 1)

        with e.Fori(0, 2) as i:
            for j in range(2, 10):
                lo(unit_no(U_GATE, 8, i, j))
        variance("mix_post", 3, D_MODEL, ("mix_post", "ss", 3))
        e.wait_ge(pe.sem, pe.at("histc"))
        e.tensor_copy(view(hist_c, P, 0, [[1, 1408]]), view(ps, P, 0, [[1, 1408]])).then_inc(dve.sem, dve.step("hist_c"))
        rstd("mix_post")
        e.wait_ge(m_copied, 4)
        for q in range(4):
            scaled("mix_post", m_T, m_T, q)
        e.wait_ge(landed["x_back"], 16)
        for q in range(4):
            e.wait_ge(dve.sem, dve.at(("mix_post", "w", 4 * q + 3)))
            e.tensor_tensor(x1[:, 4 * q:4 * q + 4, :], x1[:, 4 * q:4 * q + 4, :], m_T[:, 4 * q:4 * q + 4, :], ALU.add)\
                .then_inc(dve.sem, dve.step(("x1", q)))
        e.wait_ge(dve.sem, dve.at(("x1", 3)))
        for q in range(4):
            e.memset(m_T[:, 4 * q:4 * q + 4, :], 0.0).then_inc(y_added, 1)
        variance("ffn_pre", 3, D_MODEL, ("ffn_pre", "ss", 3))
        rstd("ffn_pre")
        norm("ffn_pre", xw_b, x1, lambda q: None)

        def conv_pair(i, s, k):
            if k == 0:
                e.wait_ge(h_copied, i * 4 + (2 * s + 2))
                e.wait_ge(hist_put, i * 4 + (2 * s + 2))
            base = 12 * s + 6 * (k // 2)
            for tap in range(3):
                for c in (k, k + 1):
                    w = [view(conv, P, i * 4 + (FC * s + c + 88 * r), [[1, 1]]) for r in range(4)]
                    src = H[s][:, c, tap:tap + HW - 2]
                    dst = hc[s][:, c, 0:HW - 2]
                    if tap == 0:
                        e.tensor_scalar(dst, src, w[0], w[3], ALU.mult, ALU.add).then_inc(conv_step, 1)
                    else:
                        e.wait_ge(conv_step, i * 24 + (base + 2 * (tap - 1) + (c - k) + 1))
                        e.scalar_tensor_tensor(out=dst, in0=src, scalar=w[tap], in1=dst, op0=ALU.mult, op1=ALU.add)\
                            .then_inc(conv_step, 1)

        def product(i):
            e.wait_ge(gelu_done, i)
            e.wait_ge(conv_step, i * 24)
            e.tensor_tensor(hc[0][:, :, 0:HW - 2], hc[0][:, :, 0:HW - 2], hc[1][:, :, 0:HW - 2], ALU.mult)\
                .then_inc(act_f, 1)

        def act_low(i):
            e.wait_ge(act_hi_ready, i * 2)
            e.tensor_tensor(act_lo[:, :, 0:NP_TOK], hc[0][:, :, 0:NP_TOK], act_hi[:, :, 0:NP_TOK].bitcast(F32),
                            ALU.subtract).then_inc(act_ready, 1)
            lo_own = view(act_lo, P, NP_TOK, [[TOK, 4], [NT, NB], [1, NT]])
            hi_own = act_hi[:, :, NP_TOK:TOK].rearrange("p c (n t) -> p c n t", t=NT).bitcast(F32)
            e.tensor_tensor(lo_own, view(hc[0], P, HS, [[HW, 4], [NT + 2, NB], [1, NT]]), hi_own,
                            ALU.subtract).then_inc(act_ready, 1)

        def y_add(i, j, no):
            e.wait_ge(unit_done, no[0] + 1)
            e.wait_ge(y_added, i * 4 + (j - 0))
            e.tensor_tensor(m_T[:, 4 * j:4 * j + 4, :], ps[:, 4 * (j % 2):4 * (j % 2) + 4, 0:TOK],
                            m_T[:, 4 * j:4 * j + 4, :], ALU.add).then_inc(y_added, 1)

        def ffn_round(i):
            fixed = isinstance(i, int)
            down, before = not fixed or i > 0, not fixed or i > 1
            if before:
                y_add(i - 1, 2, ffn_unit(i - 1, 10))
                lo(ffn_unit(i, 0))
                y_add(i - 1, 3, ffn_unit(i - 1, 11))
                lo(ffn_unit(i, 1))
            if down:
                product(i)
            lo(ffn_unit(i, 2))
            if down:
                act_low(i)
            for j in range(3, 7):
                lo(ffn_unit(i, j))
            conv_pair(i, 0, 0)
            lo(ffn_unit(i, 7))
            conv_pair(i, 0, 2)
            if not down:
                lo(ffn_unit(1, 0))
                lo(ffn_unit(1, 1))
            if down:
                lo(ffn_unit(i, 8))
                lo(ffn_unit(i, 9))
                y_add(i, 0, ffn_unit(i, 8))
                lo(ffn_unit(i, 10))
            conv_pair(i, 1, 0)
            if down:
                y_add(i, 1, ffn_unit(i, 9))
                lo(ffn_unit(i, 11))
            conv_pair(i, 1, 2)
        ffn_round(0)
        ffn_round(1)
        with e.Fori(2, 11) as i:
            ffn_round(i)
        lo(ffn_unit(11, 0))
        product(11)
        y_add(10, 2, ffn_unit(10, 10))
        act_low(11)
        y_add(10, 3, ffn_unit(10, 11))
        lo(ffn_unit(11, 1))
        y_add(11, 0, ffn_unit(11, 0))
        lo(ffn_unit(11, 2))
        y_add(11, 1, ffn_unit(11, 1))
        lo(ffn_unit(11, 3))
        y_add(11, 2, ffn_unit(11, 2))
        y_add(11, 3, ffn_unit(11, 3))

        variance("ffn_post", 7, D_MODEL, ("ffn_post", "ss", 3))
        rstd("ffn_post")
        for q in range(4):
            scaled("ffn_post", m_T, m_T, q)
        for q in range(4):
            e.wait_ge(dve.sem, dve.at(("ffn_post", "w", 4 * q + 3)))
            e.tensor_tensor(m_T[:, 4 * q:4 * q + 4, :], m_T[:, 4 * q:4 * q + 4, :], x1[:, 4 * q:4 * q + 4, :], ALU.add)\
                .then_inc(dve.sem, dve.step(("yf", q)))
        for m in range(3):
            n = P if m < 2 else NS
            e.wait_ge(pe.sem, pe.at(("yT", m)))
            b = 4 * ((m + 1) % 2) + 2
            e.tensor_copy(y_nat[0:n, m, 1024:2048], view(ps, n, b * 512, [[1, 1024]]))\
                .then_inc(dve.sem, dve.step(("y", m)))

    @block.tensor
    def _(e):
        def turn(dst, src, n):
            return e.transpose(dst, src, ident[0:n, 0:n])

        def sums(tag, sq, q, bank):
            e.wait_ge(act.sem, act.at((tag, "sq", q)))
            for k in range(4):
                mm = e.matmul(ps[:, bank, 0:TOK], ones[:, :], sq[:, q, k, :], start=q == 0 and k == 0,
                              stop=q == 3 and k == 3)
            mm.then_inc(pe.sem, pe.step((tag, "ss", q)))

        def unit(no, x_hi, x_lo, k0, side, first, last, k=SEG, n=4):
            u, _, _, s = no
            e.wait_ge(lo_ready, u + 1)
            for r in range(k):
                for c in range(n):
                    dst = ps[:, 4 * side + c, 0:TOK]
                    cols = slice(c * P, c * P + P)
                    e.matmul(dst, w_hi[s][:, r, cols], x_hi[:, k0 + r, :], start=first and r == 0, stop=False)
                    e.matmul(dst, w_hi[s][:, r, cols], x_lo[:, k0 + r, :], start=False, stop=False)
                    mm = e.matmul(dst, w_lo[s][:, r, cols], x_hi[:, k0 + r, :], start=False,
                                  stop=last and r == k - 1)
            mm.then_inc(unit_done, 1)

        e.wait_ge(pool.sem, pool.at("ident"))
        e.wait_ge(landed["x"], 32)
        for c in range(KC):
            if c >= 2:
                k = act if c % 2 else dve
                e.wait_ge(k.sem, k.at(("x_T", c - 2)))
            for m in range(3):
                n = P if m < 2 else NS
                mm = turn(ps[:, 4 + c % 2, m * P:m * P + n], x_nat[0:n, m, c * P:c * P + P], n)
            mm.then_inc(pe.sem, pe.step(("xT", c)))
        def bias_rows(h0, h1):
            for h in range(h0, h1):
                if h >= 3:
                    e.wait_ge(act.sem, act.at(("urow", h - 3)))
                e.matmul(ps[:, 4 + h % 3, 0:384], tabx[:, h, :], oh_prompt[:, h // 2 if h < A_HEADS else 3, :],
                         start=True, stop=True).then_inc(pe.sem, pe.step(("urow", h)))
        e.wait_ge(landed["nrow"], 16 * 6)
        turn(ps[:, 6, 0:72], nrow[:, :], 72).then_inc(pe.sem, pe.step("nrowT"))
        for q in range(4):
            sums("mix_pre", sq_a, q, 7)
        e.wait_ge(landed["prow"], 32)
        e.wait_ge(act.sem, act.at(("x_T", KC - 1)))
        for r in range(4):
            mm = turn(ps[:, 5, 88 * r:88 * r + 88], prow[:, r, :], 88)
        mm.then_inc(pe.sem, pe.step("prowT"))
        e.wait_ge(landed["oh_prompt"], 16)
        e.wait_ge(dve.sem, dve.at("tabx"))
        e.wait_ge(dve.sem, dve.at("conv"))
        bias_rows(0, 3)

        def group(nos, side, n=4):
            for j, no in enumerate(nos):
                unit(no, xn_hi, xn_lo, 4 * j, side, j == 0, j == 3, n=n)
        for j in range(4):
            e.wait_ge(dve.sem, dve.at(("mix_pre", "lo", j)))
            unit(unit_no(0, 8, 0, j), xn_hi, xn_lo, 4 * j, 0, j == 0, j == 3)
            bias_rows(3 * j + 3, min(3 * j + 6, N_HEADS))
        e.wait_ge(act.sem, act.at(("urow", N_HEADS - 1)))
        with e.Fori(0, 4) as i:
            for h in range(2):
                e.wait_ge(z_copied, i * 2 + h)
                group([unit_no(4, 8, i, 4 * h + j) for j in range(4)], 1 - h)
        e.wait_ge(z_copied, 8)
        group([unit_no(36, 8, 0, j) for j in range(4)], 1)
        e.wait_ge(z_copied, 9)
        group([unit_no(40, 8, 0, j) for j in range(4)], 0, n=2)

        e.wait_ge(z_copied, 11)
        e.wait_ge(act.sem, act.at("gelu"))
        for k in range(4):
            mm = e.matmul(ps[:, 6, 0:TOK], ones[:, :], Z[:, V_C + k, :], start=k == 0, stop=k == 3)
        mm.then_inc(pe.sem, pe.step("vsum"))
        for r in range(6):
            m, v = r // 2, r % 2
            n = P if m < 2 else NS
            if r >= 2:
                k, name = (dve, "v_tok") if v else (act, "k_tok")
                e.wait_ge(k.sem, k.at((name, m - 1)))
            chunks = [(V_A if v else K_A) + c for c in range(6)] + [(V_B if v else K_B) + c for c in range(4)]
            for c, chunk in enumerate(chunks):
                mm = turn(view(ps, n, 1536 * v + P * c, [[1, P]]), Z[:, chunk, m * P:m * P + n], P)
            mm.then_inc(pe.sem, pe.step(("tok", r)))
        e.wait_ge(act.sem, act.at("xc_sq"))
        for k in range(4):
            mm = e.matmul(ps[:, 7, 0:TOK], ones[:, :], sq_c[:, k, :], start=k == 0, stop=k == 3)
        mm.then_inc(pe.sem, pe.step("vvar"))
        e.wait_ge(landed["ws"], 16)
        for g in range(4):
            mm = turn(ps[:, 6, g * P:g * P + P], ws_nat[:, g, :], P)
        mm.then_inc(pe.sem, pe.step("ws_T"))
        e.wait_ge(dve.sem, dve.at("c_var"))
        e.wait_ge(dve.sem, dve.at(("v_tok", 2)))
        for c in range(4):
            turn(ps[0:HIST, 7, c * P:c * P + P], Z[:, X_D + c, NP_TOK - HIST:NP_TOK], P)
            mm = turn(ps[0:NS, 3, c * P:c * P + P], Z[:, X_D + c, NP_TOK:TOK], P)
        mm.then_inc(pe.sem, pe.step("xdT"))
        e.wait_ge(landed["hist"], 16)
        e.wait_ge(act.sem, act.at("ws_T"))
        for c in range(4):
            mm = turn(ps[:, 6, 120 * c:120 * c + 120], hist_rows[:, c * P:c * P + P], 120)
        mm.then_inc(pe.sem, pe.step("histT"))
        e.wait_ge(act.sem, act.at(("k_tok", 2)))
        e.wait_ge(dve.sem, dve.at(("vn", 3)))
        for m in range(3):
            n = P if m < 2 else NS
            for c in range(4):
                mm = turn(ps[0:n, m, c * P:c * P + P], vn[:, c, m * P:m * P + n], P)
            mm.then_inc(pe.sem, pe.step(("vnT", m)))
        e.wait_ge(landed["small"], 16 * 5)
        e.wait_ge(pool.sem, pool.at("ws_T"))
        e.wait_ge(act.sem, act.at("xd_own"))
        e.matmul(ps[0:NS, 7, 0:16], spread[:, :], ws_T[0:NT, :, 0:NT], start=True, stop=True)\
            .then_inc(pe.sem, pe.step("wrep"))
        for m in range(3):
            n = P if m < 2 else NS
            e.wait_ge(dve.sem, dve.at(("vc", m)))
            if m == 2:
                e.wait_ge(dve.sem, dve.at(("bs_own", 3)))
            bias = view(bs, 1, 0, [[1, 512]]) if m < 2 else view(bs_own, 1, 0, [[1, 128]])
            e.matmul(ps[:, 3 + m, 0:4 * n], ones[0:1, :], bias, start=True, stop=False, skip_group_check=True)
            for g in range(4):
                w = ws_T[:, g, :] if m < 2 else view(wd, NS, g * NS, [[1, NS]])
                mm = e.matmul(ps[:, 3 + m, g * n:g * n + n], vc_tok[0:n, m, g * P:g * P + P], w,
                              start=False, stop=g == 3, skip_group_check=True)
            mm.then_inc(pe.sem, pe.step(("mix", m)))
        e.wait_ge(landed["dw"], 16)
        for c in range(4):
            e.wait_ge(dve.sem, dve.at(("pooled", c)))
            e.matmul(ps[:, (1, 2, 6, 7)[c], 0:TOK], dw[:, c, :], pooled[:, c, :], start=True, stop=True)\
                .then_inc(pe.sem, pe.step(("dy", c)))

        def logits(k):
            groups, oc, m = units[k]
            if k >= 2:
                e.wait_ge(act.sem, act.at(("O", k - 2)))
            for g, (qc, kc, _, _) in enumerate(groups):
                mm = e.matmul(ps[:, 3 * (k % 2) + g, 0:(m + 1) * P], Z[:, qc, m * P:m * P + P],
                              Z[:, kc, 0:(m + 1) * P], start=True, stop=True)
            mm.then_inc(pe.sem, pe.step(("S", k)))
        e.wait_ge(act.sem, act.at(("od", 3)))
        e.wait_ge(dve.sem, dve.at(("oc", 2)))
        logits(0)
        for k, (groups, oc, m) in enumerate(units):
            if k + 1 < NU:
                logits(k + 1)
            blocks = [(g, b) for g in range(len(groups)) for b in range(m + 1)]
            e.wait_ge(dve.sem, dve.at(("P", k)))
            if k:
                e.wait_ge(act.sem, act.at(("pt", k - 1)))
            for n, _ in enumerate(blocks):
                mm = turn(view(ps, P, 6 * 512 + n * P, [[1, P]]), Lp[:, k % 2, n * P:n * P + P], P)
            mm.then_inc(pe.sem, pe.step(("PT", k)))
            e.wait_ge(act.sem, act.at(("pt", k)))
            for n, (g, b) in enumerate(blocks):
                v = groups[g][2]
                mm = e.matmul(ps[:, 3 * (k % 2), 384:512], v_tok[:, b, v * P:v * P + P],
                              PTp[:, k % 2, n * P:n * P + P], start=n == 0, stop=n == len(blocks) - 1)
            mm.then_inc(pe.sem, pe.step(("PV", k)))

        e.wait_ge(landed["oh_sample"], 16)
        e.wait_ge(act.sem, act.at(("O", NU - 1)))

        def head_rows(h0, nh, t=None):
            return view(tab_t, 33, t * 40 + h0 * 4, [[1, 4 * nh]]) if t is not None \
                else view(tab_all, 33, h0 * 4, [[1, 4 * nh]])

        def biased(dst, h0, nh, off, n, step):
            for t in range(NT):
                mm = e.matmul(dst, head_rows(h0, nh, t), oh_sample[:, off + step * t:off + step * t + n],
                              start=t == 0, stop=t == NT - 1)
            return mm
        for k in range(2):
            biased(ps[0:16, k, :], A_HEADS, 4, S_PAST + 3 + 512 * k, 512, -1).then_inc(pe.sem, pe.step(("bias_b", k)))
        biased(ps[0:8, 2, 0:128], 0, 2, S_W0 + 3, 128, -1)
        e.matmul(ps[0:8, 2, 128:256], head_rows(2, 2), oh_sample[:, S_W1:S_W1 + 128], start=True, stop=True)
        e.matmul(ps[0:8, 2, 256:320], head_rows(4, 2), oh_sample[:, S_W2:S_W2 + 64], start=True, stop=True)
        biased(ps[0:8, 3, 0:256], 0, 2, S_CAUSAL, 256, 256)
        biased(ps[0:8, 4, 0:256], 2, 2, S_SELF, 256, 256)
        biased(ps[0:8, 4, 256:512], 4, 2, S_SELF, 256, 256)
        biased(ps[0:16, 5, 0:256], A_HEADS, 4, S_CAUSAL, 256, 256).then_inc(pe.sem, pe.step("bias_a"))
        e.wait_ge(dve.sem, dve.at("bias"))

        pe.begin("sample")
        with e.Fori(0, NB) as i:
            def scores_b(q):
                half, h = q // 4, q % 4
                k = dve if q % 2 else act
                e.wait_ge(k.sem, k.at(("kt_b", q), i))
                if q == 0:
                    e.wait_ge(act.sem, act.at("ob", i, back=1))
                if q == 4:
                    e.wait_ge(dve.sem, dve.at("o_a", i, back=1))
                e.matmul(ps[0:16, 4 + half, :], qs_b[:, 16 * h:16 * h + 16], kt_b[:, q % 2, :],
                         start=h == 0, stop=h == 3).then_inc(pe.sem, pe.step(("S_b", q)))
            e.wait_ge(pool.sem, pool.at("qs_b", i))
            for q in range(8):
                half, h = q // 4, q % 4
                if h == 0:
                    e.wait_ge(kv_landed[half], i * 64 + 64)
                k = dve if q % 2 else act
                if q < 4:
                    e.wait_ge(k.sem, k.at(("kt_a", q), i, back=1))
                else:
                    e.wait_ge(k.sem, k.at(("kt_b", q - 4), i))
                for pg in range(4):
                    mm = turn(ps[:, q % 4, pg * P:pg * P + P], kv[half][:, pg, h * P:h * P + P], P)
                mm.then_inc(pe.sem, pe.step(("kT", q)))
                if q:
                    scores_b(q - 1)
            scores_b(7)
            e.wait_ge(dve.sem, dve.at("o_b", i, back=1))
            for h in range(4):
                mm = e.matmul(ps[0:16, 7, 0:NS], qs_b[:, 16 * h:16 * h + 16], z_own[:, K_B + h, :],
                              start=h == 0, stop=h == 3)
            mm.then_inc(pe.sem, pe.step("own_b"))
            e.wait_ge(kv_landed[2], i * 16 + 16)
            for h in range(2):
                k = dve if h else act
                e.wait_ge(k.sem, k.at(("kt_b", 4 + h), i))
                for r in range(4):
                    mm = turn(ps[:, h, r * P:r * P + P], kv[2][:, r, h * P:h * P + P], P)
                mm.then_inc(pe.sem, pe.step(("kTa", h)))
            e.wait_ge(pool.sem, pool.at("ident"))
            e.wait_ge(kv_landed[3], i * 16 + 16)
            e.wait_ge(act.sem, act.at(("kt_b", 6), i))
            for h in range(2):
                for r in range(4):
                    at = (4 * h + r) * 64
                    mm = turn(ps[:, 2, at:at + 64], kv[3][0:64, r, h * P:h * P + P], 64)
            mm.then_inc(pe.sem, pe.step(("kTa", 2)))
            e.wait_ge(landed["win0"], i * 16 + 16)
            e.wait_ge(dve.sem, dve.at(("kt_b", 7), i))
            for h in range(2):
                mm = turn(ps[:, 3, h * P:h * P + P], win0[:, h * P:h * P + P], P)
            mm.then_inc(pe.sem, pe.step(("kTa", 3)))
            e.wait_ge(pool.sem, pool.at("qs_a", i))
            e.wait_ge(act.sem, act.at("oa", i, back=1))
            for g in range(3):
                for h in range(2):
                    e.matmul(ps[0:8, 6, 320 + 32 * g:352 + 32 * g], qs_a[:, 16 * g + 8 * h:16 * g + 8 * h + 8],
                             z_own[:, K_A + 2 * g + h, :], start=h == 0, stop=h == 1)
            for b in (0, 2):
                e.wait_ge(act.sem, act.at(("kt_a", b), i))
            e.wait_ge(dve.sem, dve.at(("kt_a", 1), i))
            for h in range(2):
                for r in range(4):
                    at = 48 + 8 * (4 * h + r)
                    e.matmul(ps[0:8, 6, 128:256], qs_a[:, at:at + 8], kt_a[:, h, r * P:r * P + P],
                             start=h + r == 0, stop=h + r == 4)
            for h in range(2):
                for r in range(4):
                    at, c = 112 + 8 * (4 * h + r), (4 * h + r) * 64
                    e.matmul(ps[0:8, 6, 256:320], qs_a[:, at:at + 8], kt_a[:, 2, c:c + 64],
                             start=h + r == 0, stop=h + r == 4)
            e.wait_ge(dve.sem, dve.at(("kt_a", 3), i))
            for h in range(2):
                mm = e.matmul(ps[0:8, 6, 0:128], qs_a[:, 8 * h:8 * h + 8], kt_a[:, 3, h * P:h * P + P],
                              start=h == 0, stop=h == 1)
            mm.then_inc(pe.sem, pe.step("s_a"))
            need = e.snap(e.to_reg(act.at("E_b", i)))
            e.wait_ge(pool.sem, pool.at("ident"))
            e.wait_ge(act.sem, need)
            for pg in range(8):
                turn(ps[:, 7, 16 * pg:16 * pg + 16], L_b[:, pg * P:pg * P + P], 16)
            turn(ps[0:NS, 7, 128:144], L_b[:, PAST:PAST + NS], 16).then_inc(pe.sem, pe.step("ptb"))
            e.wait_ge(act.sem, act.at("pt_b", i))
            for pg in range(8):
                if pg % 4 == 0:
                    e.wait_ge(kv_landed[4 + pg // 4], i * 64 + 64)
                e.matmul(ps[0:16, 4, :], pt_b[:, pg, :], kv[4 + pg // 4][:, pg % 4, :], start=pg == 0, stop=False)
            e.matmul(ps[0:16, 4, :], pt_b[0:NS, 8, :], v_own[:, 768:1280], start=False, stop=True)\
                .then_inc(pe.sem, pe.step("pv_b"))
            need = e.snap(e.to_reg(act.at("E_a", i)))
            e.wait_ge(pool.sem, pool.at("ident"))
            e.wait_ge(act.sem, need)
            turn(ps[:, 5, 0:8], L_a[:, 0:128], 8)
            turn(ps[:, 5, 8:16], L_a[:, 128:256], 8)
            turn(ps[0:64, 5, 16:24], L_a[:, 256:320], 8)
            for g in range(3):
                mm = turn(ps[0:NS, 5, 24 + 8 * g:32 + 8 * g], L_a[:, 320 + 32 * g:352 + 32 * g], 8)
            mm.then_inc(pe.sem, pe.step("pta"))
            e.wait_ge(dve.sem, dve.at("pt_a", i))
            e.matmul(ps[0:8, 6, 0:256], pt_a[:, 0:8], win0[:, 256:512], start=True, stop=False)
            for r in range(4):
                e.matmul(ps[0:8, 6, 0:256], pt_a[:, 8 + 8 * r:16 + 8 * r], kv[2][:, r, 256:512],
                         start=False, stop=False)
            for r in range(4):
                e.matmul(ps[0:8, 6, 0:256], pt_a[0:64, 40 + 8 * r:48 + 8 * r], kv[3][0:64, r, 256:512],
                         start=False, stop=False)
            for g in range(3):
                mm = e.matmul(ps[0:8, 6, 0:256], pt_a[0:NS, 72 + 8 * g:80 + 8 * g], v_own[:, 256 * g:256 * g + 256],
                              start=False, stop=g == 2)
            mm.then_inc(pe.sem, pe.step("pv_a"))
            need = e.snap(e.to_reg(act.at("ob", i)))
            e.wait_ge(pool.sem, pool.at("ident"))
            e.wait_ge(act.sem, need)
            for h in range(4):
                mm = turn(ps[:, 7, 16 * h:16 * h + 16], ob[:, h * P:h * P + P], 16)
            mm.then_inc(pe.sem, pe.step("otb"))
            need = e.snap(e.to_reg(act.at("oa", i)))
            e.wait_ge(pool.sem, pool.at("ident"))
            e.wait_ge(act.sem, need)
            for h in range(2):
                mm = turn(ps[:, 5, 8 * h:8 * h + 8], oa[:, h * P:h * P + P], 8)
            mm.then_inc(pe.sem, pe.step("ota"))
        pe.end(NB)

        with e.Fori(0, 4) as i:
            for b in range(4):
                e.wait_ge(sig_ready, i * 4 + b)
                for j in range(4):
                    unit(unit_no(U_MIX, 20, i, 5 * b + j), xn_hi, xn_lo, 4 * j, 0, j == 0, j == 3)
                e.wait_ge(dve.sem, dve.at(("O_lo", 1)))
                e.wait_ge(p_used, i * 4 + b)
                unit(unit_no(U_MIX, 20, i, 5 * b + 4), O_hi, O_lo, O_CHUNK[b], 1, True, True, k=P_CHUNKS[b])

        with e.Fori(0, 2) as i:
            for g in range(2):
                e.wait_ge(m_copied, i * (1 + g))
                e.wait_ge(*((p_used, 16) if g else (sig_ready, 16)))
                for j in range(4):
                    if g == 0 and j % 3 == 0:
                        e.wait_ge(merged_lo, 4 if j else 3)
                    unit(unit_no(U_GATE, 8, i, 4 * g + j), M_hi, M_lo, 4 * j, g, j == 0, j == 3)
        e.wait_ge(m_copied, 3)
        for q in range(4):
            sums("mix_post", sq_b, q, 3)
        e.wait_ge(landed["crow"], 16 * 8)
        for k in range(11):
            mm = turn(view(ps, P, k * P, [[1, P]]), crow[:, k, :], P)
        mm.then_inc(pe.sem, pe.step("histc"))
        e.wait_ge(dve.sem, dve.at(("mix_post", "var")))
        for q in range(4):
            sums("ffn_pre", sq_b, q, 3)

        def ffn_round(i):
            fixed = isinstance(i, int)
            for s in range(2):
                if not fixed or i > 0:
                    e.wait_ge(h_copied, i * 4 - 2 + 2 * s)
                    e.wait_ge(y_added, i * 4 - 1 + s)
                for j in range(4):
                    if fixed and i == 0 and s == 0:
                        e.wait_ge(dve.sem, dve.at(("ffn_pre", "lo", j)))
                    unit(ffn_unit(i, 4 * s + j), xn_hi, xn_lo, 4 * j, s, j == 0, j == 3)
            if not fixed or i > 0:
                down(i, 8)

        def down(i, j0):
            e.wait_ge(act_ready, i * 2)
            for j in range(4):
                if j < 2:
                    e.wait_ge(h_copied, i * 4 + (2 * j + 2) if j0 else 44)
                else:
                    e.wait_ge(y_added, i * 4 + (j - 1))
                unit(ffn_unit(i, j0 + j), act_hi, act_lo, 0, j % 2, True, True)
        ffn_round(0)
        ffn_round(1)
        with e.Fori(2, 11) as i:
            ffn_round(i)
        down(11, 0)

        e.wait_ge(tails_put, 66)
        e.wait_ge(y_added, 4 + 4 * 10 + 4)
        for k in range(13):
            n = 7 * TAIL if k < 12 else 4 * TAIL
            mm = turn(view(ps, n, k * P, [[1, P]]), view(tails, P, k * 7 * TAIL, [[1, n]]), P)
        mm.then_inc(pe.sem, pe.step("tailT"))
        for q in range(4):
            sums("ffn_post", sq_f, q, 7)
        e.wait_ge(dve.sem, dve.at(("ffn_post", "var")))
        e.wait_ge(dve.sem, dve.at(("yf", 3)))
        for m in range(3):
            n = P if m < 2 else NS
            b = 4 * ((m + 1) % 2)
            if m == 1:
                e.wait_ge(act.sem, act.at("tail_rows"))
            if m == 2:
                e.wait_ge(act.sem, act.at(("y", 0)))
                e.wait_ge(dve.sem, dve.at(("y", 0)))
            for c in range(KC):
                mm = turn(view(ps, n, b * 512 + c * P, [[1, P]]), m_T[:, c, m * P:m * P + n], P)
            mm.then_inc(pe.sem, pe.step(("yT", m)))


_INS = ["x_prompt", "x_sample", "cache_win0", "cache_win1", "cache_win2", "cache_k", "cache_v", "page_table",
        "state_pool", "state_conv", "rel_bias_table", "norm_mix_pre", "w_in", "c_ln_g", "c_ws", "c_bs", "d_w",
        "d_scale", "p_a", "p_b", "p_c", "p_d", "w_o", "norm_mix_post", "norm_ffn_pre", "w_up", "conv_w", "conv_b",
        "w_down", "norm_ffn_post"]
_OUTS = [(1, 256, 2048), (8, 4, 2048), (1, 1, 128, 2, 2, 128), (1, 1, 256, 2, 2, 128), (1, 1, 256, 2, 2, 128),
         (1, 1, 256, 4, 128), (1, 1, 256, 4, 128), (1, 1, 15, 512), (1, 1, 2, 11264),
         (1, 8, 128, 2, 2, 128), (1, 8, 512, 2, 2, 128), (1, 8, 1028, 2, 2, 128),
         (1, 8, 4, 4, 128), (1, 8, 4, 4, 128), (1, 8, 4, 512), (1, 8, 15, 512), (1, 8, 2, 11264)]


def kernel(**inputs):
    import concourse.bacc as bacc
    from concourse.bass_utils import run_bass_kernel_spmd

    arrays = {n: np.ascontiguousarray(inputs[n]) for n in _INS}
    arrays.update(constants())
    known = {}
    for _ in range(2):
        nc = bacc.Bacc("TRN2", target_bir_lowering=False, num_devices=1, dynamic_dma_scratch_size=2048)
        d = {n: nc.dram_tensor(f"in_{n}", a.shape, mybir.dt.from_np(a.dtype), kind="ExternalInput").ap()
             for n, a in arrays.items()}
        o = [nc.dram_tensor(f"out_{i}", s, F32, kind="ExternalOutput").ap() for i, s in enumerate(_OUTS)]
        with ExitStack() as ctx:
            build(nc, known, d, o, ctx)
    r = run_bass_kernel_spmd(nc, [{f"in_{n}": a for n, a in arrays.items()}], core_ids=[0])
    return tuple(r.results[0][f"out_{i}"] for i in range(len(_OUTS)))
```

```python
from contextlib import ExitStack

import numpy as np
import concourse.bass as bass
from concourse import mybir

F32 = mybir.dt.float32
F32R = mybir.dt.float32r
I32 = mybir.dt.int32
ALU = mybir.AluOpType
ACT = mybir.ActivationFunctionType
AX = mybir.AxisListType

P = 128
D_MODEL, KC = 2048, 16
NP_TOK, NB, NT = 256, 8, 4
NS = NB * NT
TOK = NP_TOK + NS
A_HEADS, B_HEADS, HPG = 6, 4, 2
N_HEADS = A_HEADS + B_HEADS
PAST, NPG = 1024, 8
WIN_LEN = (128, 512, 1024)
BLOCK_KEYS, N_BLOCKS = 256, 4
D_WIN = (2, 4, 8, 16)
HIST = 15
D_FF = 5632
FC = D_FF // P
SCALE = 128.0 ** -0.5
EPS = 1e-6
NEG = -1e30
Q_A, K_A, V_A, Q_B, K_B, V_B, U_C, V_C, X_D, N_MIX = 0, 6, 12, 18, 22, 26, 30, 34, 38, 42
OFF_G = N_MIX * P
O_CHUNK = (0, 2, 6, 10)
P_CHUNKS = (2, 4, 4, 4)
N_O = 14
SEG = 4
UNIT_COLS = 512
N_RAW, N_SPLIT = 4, 2
U_MIX = 44
U_GATE = U_MIX + 4 * 20
U_FFN = U_GATE + 16
XE = HIST + NP_TOK + NB * (HIST + NT)
XS = HIST + NP_TOK
HW = 2 + NP_TOK + NB * (2 + NT)
HS = 2 + NP_TOK
TAIL = 2 + NB * 2


class Count:

    def __init__(self, sem, known, key):
        self.sem, self.known, self.key = sem, known, key
        self.n, self.round = 0, None

    def step(self, name, by=1):
        self.n += by
        self.known[self.key, name] = (self.n, self.round)
        return by

    def begin(self, loop):
        self.start, self.round = self.n, loop

    def end(self, rounds):
        self.known[self.key, "per", self.round] = self.n - self.start
        self.n = self.start + rounds * (self.n - self.start)
        self.round = None

    def at(self, name, i=None, back=0):
        n, loop = self.known.get((self.key, name), (1, None))
        if loop is None:
            return n
        per = self.known.get((self.key, "per", loop), 0)
        n -= back * per
        assert n >= 0, (self.key, name)
        return n if i is None else i * per + n


def constants():
    def bucket(dist):
        n = np.maximum(dist, 0)
        big = 16 + (np.log(np.maximum(n, 1) / 16) / np.log(128.0) * 16).astype(np.int64)
        return np.where(n < 16, n, np.minimum(big, 31))

    def onehot(dist, ok):
        dist, ok = np.broadcast_arrays(np.asarray(dist), np.asarray(ok))
        rows = np.where(ok, bucket(dist), 32)
        return (rows[None] == np.arange(33).reshape((33,) + (1,) * rows.ndim)).astype(np.float32)

    d = 255 - np.arange(384)
    prompt = np.stack([onehot(d, (d >= 0) & (d <= 128)), onehot(d, (d >= 0) & (d % 4 == 0)),
                       onehot(d, (d >= 0) & (d % 16 == 0)), onehot(d, d >= 0)], 1)
    past = onehot(PAST + 3 - np.arange(PAST + 3), True)
    i = np.arange(131)
    win0 = onehot(131 - i, i >= 3)
    win1 = onehot(4 * (128 - np.arange(128)), True)
    win2 = onehot(16 * (64 - np.arange(64)), True)
    t = np.arange(NT)[:, None, None, None]
    n = np.arange(NB)[:, None, None]
    m = np.arange(NB)[:, None]
    j = np.arange(NT)
    own_causal = onehot(t - j + 0 * n + 0 * m, (n == m) & (j <= t)).reshape(33, NT, NB * NS)
    own_self = onehot(t - j + 0 * n + 0 * m, (n == m) & (j == t)).reshape(33, NT, NB * NS)
    sample = np.concatenate([past, win0, win1, win2, own_causal.reshape(33, -1), own_self.reshape(33, -1)], 1)
    count = np.minimum(np.arange(16) + 1, np.array(D_WIN)[:, None])
    ramp = (np.array(D_WIN)[:, None] / count).astype(np.float32).reshape(1, 64)
    spread = (np.arange(NS) % NT == np.arange(NT)[:, None]).astype(np.float32)
    same = (np.arange(NS)[:, None] // NT == np.arange(NB)).astype(np.float32)
    return {"c_prompt": prompt.reshape(33, 4 * 384), "c_sample": sample, "c_ramp": ramp,
            "c_spread": spread, "c_same": same, "c_rank": np.tile(np.arange(1, 5, dtype=np.float32), (16, 1))}


S_PAST, S_W0 = 0, PAST + 3
S_W1, S_W2 = S_W0 + 131, S_W0 + 259
S_CAUSAL = S_W2 + 64
S_SELF = S_CAUSAL + NT * NB * NS
S_ALL = S_SELF + NT * NB * NS


def build(nc, known, d, o, ctx):
    def sem(name):
        return ctx.enter_context(nc.semaphore(name))

    base = (nc.sbuf_base + 63) // 32 * 32
    CH = TOK * 4
    R_XN = base
    R_Z = R_XN + 2 * KC * CH
    R_RAW = R_Z + 49152
    R_SPLIT = R_RAW + N_RAW * 8192
    R_M = R_SPLIT + 2 * N_SPLIT * 8192
    R_VTOK = R_M + N_O * CH
    R_U = R_VTOK + 2 * 1280 * 4 + 256
    R_SMALL = R_M + 2 * KC * CH
    assert R_U + 10240 <= R_SMALL

    def sb(name, shape, dt, at):
        return nc.alloc_sbuf_tensor_at(name, shape, dt, offset=at)

    small = [R_SMALL]

    def keep(name, shape, dt=F32):
        n = 4
        for s in shape[1:]:
            n *= s
        at = small[0]
        small[0] += (n + 31) // 32 * 32
        return sb(name, shape, dt, at)

    xn_hi = sb("xn_hi", [P, KC, TOK], F32R, R_XN)
    xn_lo = sb("xn_lo", [P, KC, TOK], F32R, R_XN + KC * CH)
    Z = sb("Z", [P, N_MIX, TOK], F32, R_Z)
    w_raw = [sb(f"w_raw{s}", [P, SEG, UNIT_COLS], F32, R_RAW + 8192 * s) for s in range(N_RAW)]
    w_hi = [sb(f"w_hi{s}", [P, SEG, UNIT_COLS], F32R, R_SPLIT + 8192 * s) for s in range(N_SPLIT)]
    w_lo = [sb(f"w_lo{s}", [P, SEG, UNIT_COLS], F32R, R_SPLIT + 8192 * (N_SPLIT + s)) for s in range(N_SPLIT)]
    x_nat = sb("x_nat", [P, 3, D_MODEL], F32, R_Z)
    xw = sb("xw", [P, KC, TOK], F32, R_Z + 3 * D_MODEL * 4)
    sq_a = sb("sq_a", [P, 4, SEG, TOK], F32, R_Z + 3 * D_MODEL * 4)
    oh_prompt = sb("oh_prompt", [33, 4, 384], F32, R_Z + 3 * D_MODEL * 4 + KC * CH)
    x_T = sb("x_T", [P, KC, TOK], F32, R_M)
    prow = sb("prow", [88, 4, P], F32, R_M + KC * CH)
    nrow = sb("nrow", [72, P], F32, R_M + KC * CH + 2048)
    tabx = sb("tabx", [33, N_HEADS, P], F32, R_M + KC * CH + 2560)
    urow = sb("urow", [P, 4, 384], F32, R_U)
    U = sb("U", [P, N_HEADS, 256], F32, R_U)
    xe_a = sb("xe_a", [P, 4, XE], F32, R_RAW)
    xe_b = sb("xe_b", [P, 4, XE], F32, R_RAW + 6784)
    pooled = sb("pooled", [P, 4, TOK], F32, R_RAW + 13568)
    vn = sb("vn", [P, 4, TOK], F32, R_RAW + 18176)
    vc_tok = sb("vc_tok", [P, 3, 512], F32, R_RAW + 22784)
    sq_c = sb("sq_c", [P, 4, TOK], F32, R_RAW + 13568)
    dw = sb("dw", [P, 4, P], F32, R_RAW + 28928)
    Lp = sb("Lp", [P, 2, 768], F32, R_SPLIT)
    PTp = sb("PTp", [P, 2, 768], F32, R_SPLIT + 6144)
    k_tok = sb("k_tok", [P, 3, 1280], F32, R_SPLIT + 12288)
    ws_nat = sb("ws_nat", [P, 4, P], F32, R_SPLIT + 27648)
    ws_T = sb("ws_T", [P, 4, P], F32, R_SPLIT + 29696)
    v_tok = sb("v_tok", [P, 2, 1280], F32, R_VTOK)
    O = sb("O", [P, N_O, TOK], F32, R_M)
    oh_sample = sb("oh_sample", [65, S_ALL], F32, R_RAW)
    oh_r = sb("oh_r", [65, S_ALL], F32R, R_RAW + (S_ALL * 4 + 31) // 32 * 32)
    QA = 176
    qpad_a = sb("qpad_a", [P, NB, QA], F32, R_RAW)
    kv = [sb(f"kv{s}", [P, 4, 512], F32, R_Z + 8192 * s) for s in range(6)]
    bias_b = sb("bias_b", [16, PAST + NB * NS], F32, R_SPLIT)
    bias_a = sb("bias_a", [8, 320 + NB * 96], F32, R_SPLIT + 5120)
    kt_b = sb("kt_b", [P, 2, 512], F32, R_SPLIT + 9472)
    kt_a = sb("kt_a", [P, 4, 512], F32, R_SPLIT + 13568)
    L_b = sb("L_b", [16, PAST + NS], F32, R_SPLIT + 21760)
    L_a = sb("L_a", [8, 416], F32, R_SPLIT + 25984)
    v_hi = [sb(f"v_hi{s}", [P, 4, 512], F32R, R_VTOK + 8192 * s) for s in range(2)]
    v_lo = [sb(f"v_lo{s}", [P, 4, 512], F32R, R_Z + 8192 * (4 + s)) for s in range(2)]
    own_hi = sb("own_hi", [NS, 512], F32R, R_VTOK + 16384)
    own_lo = sb("own_lo", [NS, 512], F32R, R_VTOK + 18432)
    pt_a = sb("pt_a", [P, 8 + 32 + 32 + 24], F32, R_SPLIT + 28224)
    ob = sb("ob", [32, 512], F32, R_SPLIT + 28608)
    oa = sb("oa", [8, 256], F32, R_SPLIT + 30656)
    O_hi = sb("O_hi", [P, N_O, TOK], F32R, R_Z)
    O_lo = sb("O_lo", [P, N_O, TOK], F32R, R_Z + N_O * CH)
    sig = sb("sig", [P, 4, TOK], F32, R_Z + 2 * N_O * CH)
    acc = sb("acc", [P, 4, TOK], F32, R_Z + 2 * N_O * CH + 4 * CH)
    tmp = sb("tmp", [P, 4, TOK], F32, R_Z + 2 * N_O * CH + 8 * CH)
    M_hi = sb("M_hi", [P, KC, TOK], F32R, R_M)
    M_lo = sb("M_lo", [P, KC, TOK], F32R, R_M + KC * CH)
    m_T = sb("m_T", [P, KC, TOK], F32, R_Z)
    x1 = sb("x1", [P, KC, TOK], F32, R_Z + KC * CH)
    hist_c = sb("hist_c", [P, 2 * FC, 16], F32, R_Z + 2 * KC * CH)
    crow = sb("crow", [P, 11, P], F32, R_Z + 2 * KC * CH + 2 * FC * 64)
    sq_b = sb("sq_b", [P, 4, SEG, TOK], F32, R_XN)
    xw_b = sb("xw_b", [P, KC, TOK], F32, R_M)
    H = [sb(f"H{s}", [P, 4, HW], F32, R_M + 4896 * s) for s in range(2)]
    hc = [sb(f"hc{s}", [P, 4, HW], F32, R_M + 9792 + 4896 * s) for s in range(2)]
    act_hi = sb("act_hi", [P, 4, TOK], F32R, R_M + 19584)
    act_lo = sb("act_lo", [P, 4, TOK], F32R, R_M + 24192)
    tails = sb("tails", [P, 2 * FC, TAIL], F32, R_M + 28800)
    tail_rows = sb("tail_rows", [7 * TAIL, 13, P], F32, R_RAW)
    y_nat = sb("y_nat", [P, 3, D_MODEL], F32, R_XN)
    sq_f = sb("sq_f", [P, 4, SEG, TOK], F32, R_M)

    ident = keep("ident", [P, P])
    ones = keep("ones", [P, P])
    conv = keep("conv", [P, 4, 2 * FC])
    gains = keep("gains", [P, 72])
    stat = keep("stat", [P, 3, TOK])
    hist_rows = sb("hist_rows", [120, 512], F32, small[0])
    qpad_b = keep("qpad_b", [P, NB, 64])
    v_own = keep("v_own", [NS, 1280])
    pt_b = keep("pt_b", [P, 9, 32], F32R)
    z_own = keep("z_own", [P, 30, NS])
    tab = keep("tab", [33, N_HEADS])
    tab2 = keep("tab2", [65, N_HEADS])
    tab_t = keep("tab_t", [65, NT, N_HEADS, NT])
    tab_all = keep("tab_all", [65, N_HEADS, NT])
    tabr_t = keep("tabr_t", [65, NT, N_HEADS, NT], F32R)
    tabr_all = keep("tabr_all", [65, N_HEADS, NT], F32R)
    pages = keep("pages", [1, NB * NPG], I32)
    ramp = keep("ramp", [P, 64])
    spread = keep("spread", [NT, NS])
    same = keep("same", [NS, NB])
    ot_lo = keep("ot_lo", [P, B_HEADS, NT])
    rank = keep("rank", [16, 4])
    bs = keep("bs", [1, 4, P])
    bs_own = keep("bs_own", [1, 4, NB, NT])
    wd = keep("wd", [NS, 4, NB, NT])
    col = keep("col", [P, 16])
    win0 = keep("win0", [P, 512])
    qs_b = keep("qs_b", [P, 64])
    qs_a = keep("qs_a", [P, QA])
    xd_rows = sb("xd_rows", [NS, 2, 512], F32, small[0])
    small[0] += 4096
    if small[0] > nc.sbuf_usable_end:
        raise ValueError(f"SBUF: {small[0]} over {nc.sbuf_usable_end}")
    NORM = {"mix_pre": 0, "mix_post": 16, "ffn_pre": 32, "ffn_post": 48, "c_ln": 64, "d_scale": 68}

    ps = nc.alloc_psum_tensor("ps", [P, 8, 512], F32)
    u_dram = nc.dram_tensor("u_dram", [N_HEADS, P, 384], F32)
    x_dram = nc.dram_tensor("x_dram", [P, KC, TOK], F32)

    def view(t, n_part, off, dims):
        a = t[:]
        return bass.AP(a.tensor, a.offset + off, [[a.ap[0][0], n_part]] + dims)

    pe = Count(sem("pe_done"), known, "pe")
    act = Count(sem("act_done"), known, "act")
    dve = Count(sem("dve_done"), known, "dve")
    pool = Count(sem("pool_done"), known, "pool")
    landed = {k: sem(f"landed_{k}") for k in
              ["prow", "nrow", "tab", "tab2", "oh_prompt", "x", "u", "x_saved", "hist", "ws", "dw", "small", "pages",
               "oh_sample", "x_back", "crow"]}
    x_landed = [sem(f"x_landed{q}") for q in range(4)]
    u_stored = [sem(f"u_stored{s}") for s in range(4)]
    w_landed = [sem(f"w_landed{s}") for s in range(N_RAW)]
    kv_landed = [sem(f"kv_landed{s}") for s in range(6)]
    win_landed = [[sem(f"win{w}_{x}_landed") for w in (1, 2, 0)] for x in ("keys", "values")]
    stored = sem("stored")
    copied = sem("copied")
    n_stored = [0, 0]
    hi_ready, lo_ready, unit_done = sem("hi_ready"), sem("lo_ready"), sem("unit_done")
    keys_turned, scored = sem("keys_turned"), sem("scored")
    keys_even, keys_odd = sem("keys_even"), sem("keys_odd")
    q_put = sem("q_put")
    z_copied = sem("z_copied")
    sig_ready, p_used = sem("sig_ready"), sem("p_used")
    merge_step, merged_f, merged_hi, merged_lo = sem("merge_step"), sem("merged_f"), sem("merged_hi"), sem("merged_lo")
    m_copied = sem("m_copied")
    y_added = sem("y_added")
    h_copied, hist_put, tails_put = sem("h_copied"), sem("hist_put"), sem("tails_put")
    conv_step = sem("conv_step")
    gelu_done, act_f, act_hi_ready, act_ready = sem("gelu_done"), sem("act_f"), sem("act_hi_ready"), sem("act_ready")

    block = ctx.enter_context(nc.Block())

    def store(e, dst, src):
        n_stored[0] += 16
        e.dma_start(dst, src).then_inc(stored, 16)

    units = []
    for slot in range(HPG):
        for m in range(2):
            units.append(([(Q_A + 2 * g + slot, K_A + 2 * g + slot, 2 * g + slot, 2 * g + slot) for g in range(3)],
                          slot, m))
    for h in range(B_HEADS):
        for m in range(2):
            units.append(([(Q_B + h, K_B + h, A_HEADS + h, A_HEADS + h)], 2 + h, m))
    NU = len(units)
    NA = NU - 2 * B_HEADS

    def room(k):
        if k < NA:
            return 3 * (k % 2), 768 * (k % 2), k % 3, 6 * 512
        return (k - NA) % 6, 256 * (k % 3), k % 3, (6 + k % 2) * 512

    def ahead(k):
        return min(k + (2 if k >= NA - 1 else 1), NU - 1)

    def unit_no(u0, per, i, j):
        if isinstance(i, int):
            return u0 + per * i + j, (u0 + per * i + j) // N_RAW, j % N_RAW, j % N_SPLIT
        return i * per + (u0 + j), i * (per // N_RAW) + (u0 + j) // N_RAW, j % N_RAW, j % N_SPLIT

    def ffn_unit(i, j):
        if isinstance(i, int) and i == 0:
            return unit_no(U_FFN, 12, 0, j)
        return unit_no(U_FFN - 4, 12, i, j)

    def sample_steps(i, last):
        def name(x):
            return ("last", x) if last else x

        def at(count, x, back=0):
            if not last:
                return count.at(x, i, back=back)
            return count.at(x, NB - 2) if back else count.at(("last", x))
        return name, at

    @block.sync
    def _(sp):
        sp.dma_start(x_nat[0:NS, 2, :], d["x_sample"].rearrange("n t c -> (n t) c")).then_inc(landed["x"], 16)
        for q in range(4):
            cols = slice(512 * q, 512 * q + 512)
            sp.dma_start(x_nat[:, 0:2, cols], d["x_prompt"][0, :, cols].rearrange("(m p) c -> p m c", p=P))\
                .then_inc(x_landed[q], 16)
        for name, dst, src in (
                ("nrow", nrow[0:16, :], d["norm_mix_pre"][0].rearrange("(c p) -> c p", p=P)),
                ("nrow", nrow[16:32, :], d["norm_mix_post"][0].rearrange("(c p) -> c p", p=P)),
                ("nrow", nrow[32:48, :], d["norm_ffn_pre"][0].rearrange("(c p) -> c p", p=P)),
                ("nrow", nrow[48:64, :], d["norm_ffn_post"][0].rearrange("(c p) -> c p", p=P)),
                ("nrow", nrow[64:68, :], d["c_ln_g"][0].rearrange("(c p) -> c p", p=P)),
                ("nrow", nrow[68:72, :], d["d_scale"][0].rearrange("(c p) -> c p", p=P)),
                ("tab", tab[0:32, :], d["rel_bias_table"])):
            sp.dma_start(dst, src).then_inc(landed[name], 16)

        def load(no, src):
            u, _, slot, _ = no
            if not isinstance(u, int) or u >= N_RAW:
                need = u - (N_RAW - 1)
                if not isinstance(need, int):
                    need = sp.snap(sp.to_reg(need))
                    sp.wait_ge(landed["x"], 16)
                sp.wait_ge(lo_ready, need)
            sp.dma_start(w_raw[slot][:, 0:src.shape[1], 0:src.shape[2]], src).then_inc(w_landed[slot], 16)

        def rows(w, r0, k, c0, n=UNIT_COLS):
            return w[bass.ds(r0, k * P), bass.ds(c0, n)].rearrange("(k p) c -> p k c", p=P)

        w_in, w_up, w_down = d["w_in"][0], d["w_up"][0], d["w_down"][0]

        def mix_group(i, h, g):
            for j in range(4):
                load(unit_no(4, 8, i, 4 * h + j), rows(w_in, j * 512, SEG, g * UNIT_COLS))
        for j in range(4):
            load(unit_no(0, 8, 0, j), rows(w_in, j * 512, SEG, 0))
        for name, dst, src in (
                ("tab2", tab2[0:32, :], d["rel_bias_table"]),
                ("tab2", tab2[32:64, :], d["rel_bias_table"]),
                ("prow", prow[:, 0:3, :], d["conv_w"][0].rearrange("w (c p) -> c w p", p=P)),
                ("prow", prow[:, 3, :], d["conv_b"][0].rearrange("(c p) -> c p", p=P)),
                ("oh_prompt", oh_prompt[:, :, :], d["c_prompt"].rearrange("b (g i) -> b g i", g=4)),
                ("pages", pages[:, :], d["page_table"].rearrange("n q -> (n q)").rearrange("(a m) -> a m", a=1)),
                ("small", bs[:, :, :], d["c_bs"]),
                ("small", ramp[:, :], d["c_ramp"].to_broadcast([P, 64])),
                ("small", spread[:, :], d["c_spread"]),
                ("small", same[:, :], d["c_same"]),
                ("small", rank[:, :], d["c_rank"])):
            sp.dma_start(dst, src).then_inc(landed[name], 16)
        with sp.Fori(0, 4) as i:
            for h in range(2):
                mix_group(i, h, i * 2 + (1 + h))
        for s in range(4):
            sp.wait_ge(u_stored[s], 16 * len(range(s, N_HEADS, 4)))
        sp.dma_start(U[:, :, :], bass.AP(u_dram.ap().tensor, P - 1, [[383, P], [P * 384, N_HEADS], [1, 256]]))\
            .then_inc(landed["u"], 16)
        for j in range(4):
            load(unit_no(36, 8, 0, j), rows(w_in, j * 512, SEG, 9 * UNIT_COLS))
        for j in range(4):
            load(unit_no(40, 8, 0, j), rows(w_in, j * 512, SEG, 10 * UNIT_COLS, 256))

        def store(dst, src):
            n_stored[0] += 16
            sp.dma_start(dst, src).then_inc(stored, 16)

        for m in range(2):
            sp.wait_ge(act.sem, act.at(("k_tok", m)))
            sp.wait_ge(dve.sem, dve.at(("v_tok", m)))
            for g in range(3):
                if g == 0 and m == 0:
                    continue
                t0 = 0 if g == 0 else m * P
                dst = o[2 + g][0, 0, t0:t0 + P]
                store(dst[:, 0].rearrange("p h e -> p (h e)"), k_tok[:, m, 256 * g:256 * g + 256])
                store(dst[:, 1].rearrange("p h e -> p (h e)"), v_tok[:, m, 256 * g:256 * g + 256])
            store(o[5][0, 0, m * P:m * P + P].rearrange("p h e -> p (h e)"), k_tok[:, m, 768:1280])
            store(o[6][0, 0, m * P:m * P + P].rearrange("p h e -> p (h e)"), v_tok[:, m, 768:1280])
        sp.wait_ge(act.sem, act.at(("k_tok", 2)))
        sp.wait_ge(dve.sem, dve.at(("v_tok", 2)))
        for g in range(3):
            L = WIN_LEN[g] + (NT if g == 2 else 0)
            dst = o[9 + g][0]
            for kv_i, src in ((0, k_tok[0:NS, 2, 256 * g:256 * g + 256]), (1, v_own[:, 256 * g:256 * g + 256])):
                for n in range(NB):
                    store(dst[n, L - NT:L, kv_i].rearrange("t h e -> t (h e)"), src[NT * n:NT * n + NT, :])
        store(o[12][0].rearrange("n t h e -> (n t) (h e)"), k_tok[0:NS, 2, 768:1280])
        store(o[13][0].rearrange("n t h e -> (n t) (h e)"), v_own[:, 768:1280])
        sp.wait_ge(dve.sem, dve.at(("vc", 2)))
        store(o[14][0].rearrange("n t c -> (n t) c"), vc_tok[0:NS, 2, :])
        sp.wait_ge(act.sem, act.at("xd_own"))
        store(o[7][0, 0], xd_rows[0:HIST, 0, :])
        for n in range(NB):
            store(o[15][0, n, HIST - NT:HIST], xd_rows[NT * n:NT * n + NT, 1, :])
        store(o[15][0, :, 0:HIST - NT], d["state_pool"][0, :, NT:HIST])

        n_stored[1] = n_stored[0]
        sp.wait_ge(stored, n_stored[0])
        sp.wait_ge(pe.sem, pe.at(("dy", 3)))
        for row, dst, n in ((0, 0, 32), (0, 32, 32), (32, 64, 1)):
            sp.dma_start(oh_sample[dst:dst + n, :], d["c_sample"][row:row + n, :]).then_inc(landed["oh_sample"], 16)

        sp.wait_ge(pe.sem, pe.at(("PV", NU - 1)))
        sp.wait_ge(dve.sem, dve.at(("P", NU - 1)))
        sp.wait_ge(pool.sem, pool.at("z_own"))
        sp.wait_ge(landed["pages"], 16)
        def page_loads(n, cache, half, slot):
            for q in range(4):
                page = sp.value_load(pages[0:1, bass.ds(n * NPG + (4 * half + q), 1)], min_val=0,
                                     max_val=cache.shape[0] - 1)
                sp.dma_start(kv[slot][:, q:q + 1, :], cache[bass.ds(page, 1)].rearrange("a p h e -> p a (h e)"))\
                    .then_inc(kv_landed[slot], 16)

        def window_loads(i, v):
            cols = slice(256 * v, 256 * v + 256)
            sp.dma_start(kv[2][:, :, cols], d["cache_win1"][0, bass.ds(i, 1), :, v]
                         .rearrange("a (p r) h e -> p (a r) (h e)", r=4)).then_inc(win_landed[v][0], 16)
            sp.dma_start(kv[3][0:64, :, cols], d["cache_win2"][0, bass.ds(i, 1), :, v]
                         .rearrange("a (p r) h e -> p (a r) (h e)", r=16)[:, 0:4, :]).then_inc(win_landed[v][1], 16)
            sp.dma_start(win0[:, cols], d["cache_win0"][0, bass.ds(i, 1), :, v].rearrange("a p h e -> p (a h e)"))\
                .then_inc(win_landed[v][2], 16)

        def next_keys(i, half):
            need = i * 8 + (4 * half + 4)
            if not isinstance(i, int):
                need = sp.snap(sp.to_reg(need))
                sp.wait_ge(landed["pages"], 16)
            sp.wait_ge(keys_turned, need)
            page_loads(i + 1, d["cache_k"][0], half, half)

        def sample_loads(i, first, last):
            def used(x):
                return pe.at(x, NB - 2) if last else pe.at(x, i, back=1)
            if not first:
                sp.wait_ge(pe.sem, used(("kTa", 3)))
            window_loads(i, 0)
            if not last:
                next_keys(i, 0)
                next_keys(i, 1)
            if not first:
                need = used("pv_b")
                if not last:
                    need = sp.snap(sp.to_reg(need))
                    sp.wait_ge(landed["pages"], 16)
                sp.wait_ge(pe.sem, need)
            for half in range(2):
                page_loads(i, d["cache_v"][0], half, 4 + half)
            if not first:
                sp.wait_ge(pe.sem, used("pv_a"))
            window_loads(i, 1)
        for half in range(2):
            page_loads(0, d["cache_k"][0], half, half)
        sample_loads(0, True, False)
        with sp.Fori(1, NB - 1) as i:
            sample_loads(i, False, False)
        sample_loads(NB - 1, False, True)

        sp.wait_ge(q_put, 2 * NB)
        with sp.Fori(0, 4) as i:
            for b in range(4):
                for j in range(4):
                    load(unit_no(U_MIX, 20, i, 5 * b + j),
                         rows(w_in, j * 512, SEG, i * UNIT_COLS + (OFF_G + b * D_MODEL)))
                load(unit_no(U_MIX, 20, i, 5 * b + 4), rows(d["p_" + "abcd"[b]][0], 0, P_CHUNKS[b], i * UNIT_COLS))

        with sp.Fori(0, 2) as i:
            for g in range(2):
                for j in range(4):
                    load(unit_no(U_GATE, 8, i, 4 * g + j), rows(d["w_o"][0], j * 512, SEG, i * 1024 + g * UNIT_COLS))

        def up(i):
            for v in range(2):
                for j in range(4):
                    load(ffn_unit(i, 4 * v + j), rows(w_up, j * 512, SEG, i * UNIT_COLS + v * D_FF))

        def down(i):
            for j in range(4):
                load(ffn_unit(i, 8 + j if not (isinstance(i, int) and i == 11) else j),
                     rows(w_down, i * 512 - 512, SEG, j * UNIT_COLS))
        up(0)
        up(1)
        down(1)
        with sp.Fori(2, 11) as i:
            up(i)
            down(i)
        down(11)

        sp.wait_ge(act.sem, act.at("tail_rows"))
        for c in range(7):
            nk = 13 if c < 2 * FC - 84 else 12
            r = c * TAIL
            for t, rows_out in ((0, o[8][0, 0]), (2, o[16][0].rearrange("n t c -> (n t) c"))):
                k = rows_out.shape[0]
                dst = bass.AP(rows_out.tensor, rows_out.offset + c * P, [[2 * D_FF, k], [7 * P, nk], [1, P]])
                store(dst, tail_rows[r + t:r + t + k, 0:nk, :])
        for m in range(3):
            sp.wait_ge(act.sem, act.at(("y", m)))
            sp.wait_ge(dve.sem, dve.at(("y", m)))
            if m < 2:
                store(o[0][0, m * P:m * P + P], y_nat[:, m, :])
            else:
                store(o[1].rearrange("n t c -> (n t) c"), y_nat[0:NS, 2, :])
        sp.wait_ge(stored, n_stored[0])
        sp.wait_ge(copied, 16 * 16)

    @block.gpsimd
    def _(e):
        e.memset(ident[:, :], 0.0).then_inc(pool.sem, pool.step("ident0"))
        e.memset(ones[:, :], 1.0).then_inc(pool.sem, pool.step("ones"))
        e.wait_ge(pool.sem, pool.at("ident0"))
        e.affine_select(out=ident[:, :], in_=ident[:, :], compare_op=ALU.not_equal, fill=1.0, base=0,
                        pattern=[[-1, P]], channel_multiplier=1).then_inc(pool.sem, pool.step("ident"))
        e.wait_ge(pool.sem, pool.at("ident"))
        e.memset(tab[32:33, :], NEG).then_inc(pool.sem, pool.step("tab_neg"))
        e.wait_ge(pool.sem, pool.at("tab_neg"))
        e.memset(tab2[64:65, :], NEG).then_inc(pool.sem, pool.step("tab2_neg"))
        e.wait_ge(pool.sem, pool.at("tab2_neg"))
        e.memset(tab_t[:, :, :, :], 0.0).then_inc(pool.sem, pool.step("tab_t0"))
        e.wait_ge(lo_ready, U_MIX)
        e.wait_ge(z_copied, 11)
        e.memset(xe_a[:, :, 0:HIST], 0.0).then_inc(pool.sem, pool.step("xe0"))
        e.tensor_copy(xe_a[:, :, HIST:XS], Z[:, X_D:N_MIX, 0:NP_TOK]).then_inc(pool.sem, pool.step("xe1"))
        for c in range(4):
            e.tensor_copy(view(xe_a, P, c * XE + XS + HIST, [[HIST + NT, NB], [1, NT]]),
                          view(Z, P, (X_D + c) * TOK + NP_TOK, [[NT, NB], [1, NT]]))\
                .then_inc(pool.sem, pool.step(("xe2", c)))
        e.wait_ge(pool.sem, pool.at(("xe2", 3)))
        e.wait_ge(dve.sem, dve.at("xe_hist"))
        e.tensor_tensor(xe_b[:, :, 1:XE], xe_a[:, :, 1:XE], xe_a[:, :, 0:XE - 1], ALU.add)\
            .then_inc(pool.sem, pool.step("s2"))
        e.wait_ge(pool.sem, pool.at("s2"))
        e.tensor_tensor(xe_a[:, 1:4, 3:XE], xe_b[:, 1:4, 3:XE], xe_b[:, 1:4, 1:XE - 2], ALU.add)\
            .then_inc(pool.sem, pool.step("s4"))
        e.wait_ge(pool.sem, pool.at("s4"))
        e.tensor_tensor(xe_b[:, 2:4, 7:XE], xe_a[:, 2:4, 7:XE], xe_a[:, 2:4, 3:XE - 4], ALU.add)\
            .then_inc(pool.sem, pool.step("s8"))
        e.wait_ge(pool.sem, pool.at("s8"))
        e.tensor_tensor(xe_a[:, 3, 15:XE], xe_b[:, 3, 15:XE], xe_b[:, 3, 7:XE - 8], ALU.add)\
            .then_inc(pool.sem, pool.step("s16"))
        e.wait_ge(act.sem, act.at("ws_T"))
        e.affine_select(out=ws_T[:, :, :], in_=ws_T[:, :, :], compare_op=ALU.is_ge, fill=0.0, base=0,
                        pattern=[[0, 4], [1, P]], channel_multiplier=-1).then_inc(pool.sem, pool.step("ws_T"))
        e.tensor_copy(z_own[:, :, :], Z[:, 0:30, NP_TOK:TOK]).then_inc(pool.sem, pool.step("z_own"))
        e.wait_ge(landed["oh_sample"], 48)
        e.tensor_copy(oh_r[:, :], oh_sample[:, :]).then_inc(pool.sem, pool.step("oh_r"))
        e.wait_ge(pool.sem, pool.at("oh_r"))
        e.memset(qpad_b[:, :, :], 0.0).then_inc(pool.sem, pool.step("qb0"))
        e.memset(qpad_a[:, :, :], 0.0).then_inc(pool.sem, pool.step("qa0"))
        e.memset(pt_a[:, :], 0.0).then_inc(pool.sem, pool.step("pt_a0"))
        e.wait_ge(pool.sem, pool.at("qa0"))
        for h in range(B_HEADS):
            e.tensor_copy(view(qpad_b, P, 20 * h, [[64, NB], [1, NT]]),
                          z_own[:, Q_B + h, :].rearrange("p (n t) -> p n t", t=NT))\
                .then_inc(pool.sem, pool.step(("qb", h)))
        for g in range(3):
            for h in range(HPG):
                src = z_own[:, Q_A + 2 * g + h, :].rearrange("p (n t) -> p n t", t=NT)
                e.tensor_copy(view(qpad_a, P, 16 * g + 12 * h, [[QA, NB], [1, NT]]), src)\
                    .then_inc(pool.sem, pool.step(("qa", g, h)))
                if g:
                    e.tensor_copy(view(qpad_a, P, 48 + 64 * (g - 1) + 36 * h, [[QA, NB], [9, NT]]), src)\
                        .then_inc(pool.sem, pool.step(("qa9", g, h)))
        e.wait_ge(pool.sem, pool.at(("qa9", 2, 1)))
        def sample_queries(i):
            if not isinstance(i, int):
                e.wait_ge(pe.sem, pe.at("own_b", i, back=1))
            e.tensor_copy(qs_b[:, :], view(qpad_b, P, i * 64, [[1, 64]])).then_inc(q_put, 1)
            if not isinstance(i, int):
                e.wait_ge(pe.sem, pe.at("s_a", i, back=1))
            e.tensor_copy(qs_a[:, :], view(qpad_a, P, i * QA, [[1, QA]])).then_inc(q_put, 1)
        sample_queries(0)
        with e.Fori(1, NB) as i:
            sample_queries(i)

        e.wait_ge(landed["x_back"], 16)
        for q in (0, 2):
            e.wait_ge(dve.sem, dve.at(("mix_post", "w", 4 * q + 3)))
            e.tensor_tensor(x1[:, 4 * q:4 * q + 4, :], x1[:, 4 * q:4 * q + 4, :], m_T[:, 4 * q:4 * q + 4, :],
                            ALU.add).then_inc(pool.sem, pool.step(("x1", q)))
        e.wait_ge(dve.sem, dve.at("hist_c"))
        e.wait_ge(dve.sem, dve.at(("ffn_pre", "lo", 3)))
        for s in range(2):
            e.memset(H[s][:, :, 0:2], 0.0).then_inc(pool.sem, pool.step(("H0", s)))
        with e.Fori(0, 11) as i:
            e.wait_ge(conv_step, i * 24)
            for s in range(2):
                for k in range(2):
                    e.tensor_copy(view(H[s], P, HS + k, [[HW, 4], [NT + 2, NB]]),
                                  view(hist_c, P, i * 64 + (FC * s * 16 + k), [[16, 4], [2, NB]]))\
                        .then_inc(hist_put, 1)
            for s in range(2):
                e.wait_ge(h_copied, i * 4 + (2 * s + 2))
                e.tensor_copy(view(tails, P, i * (4 * TAIL) + FC * s * TAIL, [[TAIL, 4], [1, 2]]),
                              H[s][:, :, NP_TOK:HS]).then_inc(tails_put, 1)
                for k in range(2):
                    e.tensor_copy(view(tails, P, i * (4 * TAIL) + (FC * s * TAIL + 2 + k), [[TAIL, 4], [2, NB]]),
                                  view(H[s], P, HS + NT + k, [[HW, 4], [NT + 2, NB]])).then_inc(tails_put, 1)

        for q in (0, 2):
            e.wait_ge(dve.sem, dve.at(("ffn_post", "w", 4 * q + 3)))
            e.tensor_tensor(m_T[:, 4 * q:4 * q + 4, :], m_T[:, 4 * q:4 * q + 4, :], x1[:, 4 * q:4 * q + 4, :],
                            ALU.add).then_inc(pool.sem, pool.step(("yf", q)))

    @block.scalar
    def _(e):
        def hi(no, k=SEG, n=UNIT_COLS):
            u, r, slot, s = no
            e.wait_ge(w_landed[slot], r * 16 + 16)
            if not isinstance(u, int) or u >= N_SPLIT:
                e.wait_ge(unit_done, u - 1)
            e.activation(w_hi[s][:, 0:k, 0:n], w_raw[slot][:, 0:k, 0:n], ACT.Copy).then_inc(hi_ready, 1)

        def squares(tag, src, sq, q, ready):
            for s, v in ready:
                e.wait_ge(s, v)
            e.activation(sq[:, q], src[:, 4 * q:4 * q + 4, :], ACT.Square).then_inc(act.sem, act.step((tag, "sq", q)))

        def root(tag):
            e.wait_ge(dve.sem, dve.at((tag, "var")))
            e.activation(stat[:, 1, :], stat[:, 0, :], ACT.Sqrt).then_inc(act.sem, act.step((tag, "sd")))

        def norm_hi(tag, src, q):
            e.wait_ge(dve.sem, dve.at((tag, "w", 4 * q + 3)))
            e.activation(xn_hi[:, 4 * q:4 * q + 4, :], src[:, 4 * q:4 * q + 4, :], ACT.Copy)\
                .then_inc(act.sem, act.step((tag, "hi", q)))

        for c in range(1, KC, 2):
            e.wait_ge(pe.sem, pe.at(("xT", c)))
            e.activation(x_T[:, c, :], ps[:, 5, 0:TOK], ACT.Copy).then_inc(act.sem, act.step(("x_T", c)))
        e.wait_ge(dve.sem, dve.at(("x_T", KC - 2)))
        e.wait_ge(act.sem, act.at(("x_T", KC - 1)))
        e.dma_start(x_dram.ap(), x_T[:, :, :]).then_inc(landed["x_saved"], 16)
        for q in range(4):
            squares("mix_pre", x_T, sq_a, q, [])
        hi(unit_no(0, 8, 0, 0))
        root("mix_pre")
        hi(unit_no(0, 8, 0, 1))

        def bias_rows(h0, h1):
            for h in range(h0, h1):
                e.wait_ge(pe.sem, pe.at(("urow", h)))
                if h >= 4:
                    e.wait_ge(u_stored[h % 4], 16 * (h // 4))
                e.activation(urow[:, h % 4, :], ps[:, 4 + h % 3, 0:384], ACT.Copy)\
                    .then_inc(act.sem, act.step(("urow", h)))
            for h in range(h0, h1):
                e.wait_ge(act.sem, act.at(("urow", h)))
                e.dma_start(u_dram.ap()[h], urow[:, h % 4, :]).then_inc(u_stored[h % 4], 16)
        bias_rows(0, 2)
        norm_hi("mix_pre", xw, 0)
        bias_rows(2, 3)
        for q in range(1, 4):
            norm_hi("mix_pre", xw, q)
        bias_rows(3, 6)

        def z_out(g, side, n, done):
            e.wait_ge(unit_done, done)
            e.activation(Z[:, bass.ds(g * 4, n), :], ps[:, 4 * side:4 * side + n, 0:TOK], ACT.Copy).then_inc(z_copied, 1)
        hi(unit_no(0, 8, 0, 2))
        bias_rows(6, 9)
        hi(unit_no(0, 8, 0, 3))
        bias_rows(9, N_HEADS)
        with e.Fori(0, 4) as i:
            for h in range(2):
                for j in range(4):
                    hi(unit_no(4, 8, i, 4 * h + j))
                    if j == 1:
                        z_out(i * 2 + h, h, 4, i * 8 + (4 + 4 * h))
        for g in range(2):
            for j in range(4):
                hi(unit_no(36 + 4 * g, 8, 0, j), n=256 if g else UNIT_COLS)
                if j == 1:
                    z_out(8 + g, g, 4, 36 + 4 * g)
        z_out(10, 0, 2, U_MIX)
        e.wait_ge(unit_done, U_MIX)
        e.dma_start(ws_nat[:, :, :], d["c_ws"][0].rearrange("g t s -> t g s")).then_inc(landed["ws"], 16)
        e.wait_ge(lo_ready, U_MIX)
        e.dma_start(dw[:, :, :], d["d_w"][0].rearrange("g c e -> c g e")).then_inc(landed["dw"], 16)
        e.dma_start(hist_rows[:, :], d["state_pool"][0].rearrange("n j c -> (n j) c")).then_inc(landed["hist"], 16)
        e.wait_ge(z_copied, 11)
        e.activation(Z[:, U_C:X_D, :], Z[:, U_C:X_D, :], ACT.Gelu_apprx_tanh).then_inc(act.sem, act.step("gelu"))
        for m in range(3):
            n = P if m < 2 else NS
            e.wait_ge(pe.sem, pe.at(("tok", 2 * m)))
            e.activation(k_tok[0:n, m, :], view(ps, n, 0, [[1, 1280]]), ACT.Copy)\
                .then_inc(act.sem, act.step(("k_tok", m)))
        e.wait_ge(dve.sem, dve.at("xc"))
        e.activation(sq_c[:, :, :], vn[:, :, :], ACT.Square).then_inc(act.sem, act.step("xc_sq"))
        e.wait_ge(dve.sem, dve.at("c_var"))
        e.activation(stat[:, 1, :], stat[:, 0, :], ACT.Sqrt).then_inc(act.sem, act.step("c_sd"))
        e.wait_ge(pe.sem, pe.at("ws_T"))
        e.activation(ws_T[:, :, :], view(ps, P, 6 * 512, [[P, 4], [1, P]]), ACT.Copy)\
            .then_inc(act.sem, act.step("ws_T"))
        e.wait_ge(pe.sem, pe.at("xdT"))
        e.activation(xd_rows[0:HIST, 0, :], ps[0:HIST, 7, :], ACT.Copy).then_inc(act.sem, act.step("xd_prompt"))
        e.activation(xd_rows[:, 1, :], ps[0:NS, 3, :], ACT.Copy).then_inc(act.sem, act.step("xd_own"))
        e.wait_ge(landed["x_saved"], 16)
        for c in range(4):
            e.wait_ge(pe.sem, pe.at(("dy", c)))
            e.activation(O[:, 10 + c, :], ps[:, (1, 2, 6, 7)[c], 0:TOK], ACT.Identity,
                         scale=gains[:, NORM["d_scale"] + c:NORM["d_scale"] + c + 1])\
                .then_inc(act.sem, act.step(("od", c)))

        def prompt_out(k):
            groups, oc, m = units[k]
            e.wait_ge(pe.sem, pe.at(("PV", k)))
            e.activation(O[:, oc, m * P:m * P + P], ps[:, room(k)[0], 384:512], ACT.Copy)\
                .then_inc(act.sem, act.step(("O", k)))

        def exponentials(k):
            _, lp, c, _ = room(k)
            n = len(units[k][0]) * (units[k][2] + 1) * P
            e.wait_ge(dve.sem, dve.at(("nm", k)))
            e.activation(view(Lp, P, lp, [[1, n]]), view(Lp, P, lp, [[1, n]]), ACT.Exp, bias=col[:, c:c + 1],
                         accum_out=col[:, 3 + c:4 + c]).then_inc(act.sem, act.step(("E", k)))
        exponentials(0)
        for k, (groups, oc, m) in enumerate(units):
            _, lp, _, at = room(k)
            n = len(groups) * (m + 1) * P
            if k:
                prompt_out(k - 1)
            if k >= NA - 1 and k + 1 < NU:
                exponentials(k + 1)
            e.wait_ge(pe.sem, pe.at(("PT", k)))
            e.activation(view(PTp, P, lp, [[1, n]]), view(ps, P, at, [[1, n]]), ACT.Copy)\
                .then_inc(act.sem, act.step(("pt", k)))
            if k < NA - 1:
                exponentials(k + 1)
        prompt_out(NU - 1)

        e.wait_ge(dve.sem, dve.at(("P", NU - 1)))
        e.wait_ge(stored, n_stored[1])
        e.activation(own_hi[:, :], v_own[:, 768:1280], ACT.Copy).then_inc(act.sem, act.step("own_hi"))

        def even_keys(n8, q):
            e.wait_ge(keys_turned, n8 + (q + 1))
            e.activation(kt_b[:, 0, :], ps[:, q % 3, :], ACT.Copy).then_inc(keys_even, 1)

        def sample(i, last):
            name, at = sample_steps(i, last)
            for b in (0, 2):
                e.wait_ge(pe.sem, at(pe, ("kTa", b)))
                e.activation(kt_a[:, b, :], ps[:, (8 + b) % 3, :], ACT.Copy)\
                    .then_inc(act.sem, act.step(name(("kt_a", b))))
            if not last:
                even_keys(i * 8 + 8, 0)
            for half in range(2):
                e.wait_ge(kv_landed[4 + half], i * 64 + 64)
                e.activation(v_hi[half][:, :, :], kv[4 + half][:, :, :], ACT.Copy)\
                    .then_inc(act.sem, act.step(name(("v_hi", half))))
            if not last:
                even_keys(i * 8 + 8, 2)
            e.wait_ge(dve.sem, at(dve, "nm_b"))
            e.activation(L_b[:, :], L_b[:, :], ACT.Exp, bias=col[0:16, 0:1], accum_out=col[0:16, 1:2])\
                .then_inc(act.sem, act.step(name("E_b")))
            e.wait_ge(dve.sem, at(dve, "nm_a"))
            e.activation(L_a[:, :], L_a[:, :], ACT.Exp, bias=col[0:8, 3:4], accum_out=col[0:8, 4:5])\
                .then_inc(act.sem, act.step(name("E_a")))
            if not last:
                even_keys(i * 8 + 8, 4)
            e.wait_ge(pe.sem, at(pe, "ptb"))
            e.activation(pt_b[:, 0:8, 0:16], view(ps, P, 7 * 512, [[16, 8], [1, 16]]), ACT.Copy)\
                .then_inc(act.sem, act.step(name("pt_b0")))
            e.activation(pt_b[0:NS, 8, 0:16], ps[0:NS, 7, 128:144], ACT.Copy)\
                .then_inc(act.sem, act.step(name("pt_b")))
            if not last:
                even_keys(i * 8 + 8, 6)
            e.wait_ge(pe.sem, at(pe, "pv_b"))
            e.activation(ob[:, :], ps[0:32, 3, :], ACT.Copy)\
                .then_inc(act.sem, act.step(name("ob")))
            e.wait_ge(pe.sem, at(pe, "pv_a"))
            e.wait_ge(dve.sem, at(dve, "rs_a"))
            e.activation(oa[:, :], ps[0:8, 6, 0:256], ACT.Identity, scale=col[0:8, 5:6])\
                .then_inc(act.sem, act.step(name("oa")))
        for q in range(0, 8, 2):
            even_keys(0, q)
        act.begin("sample")
        with e.Fori(0, NB - 1) as i:
            sample(i, False)
        act.end(NB - 1)
        sample(NB - 1, True)

        e.wait_ge(pe.sem, pe.at(("last", "ota")))
        e.wait_ge(dve.sem, dve.at(("last", "o_a")))
        for j in range(2):
            hi(unit_no(U_MIX, 20, 0, j))
        for h in range(2):
            e.activation(O_hi[:, 7 * h:7 * h + 7, :], O[:, 7 * h:7 * h + 7, :], ACT.Copy)\
                .then_inc(act.sem, act.step(("O_hi", h)))
        with e.Fori(0, 4) as i:
            for b in range(4):
                for j in range(2, 4):
                    hi(unit_no(U_MIX, 20, i, 5 * b + j))
                hi(unit_no(U_MIX, 20, i, 5 * b + 4), k=P_CHUNKS[b])
                hi(unit_no(U_MIX, 20, i, 5 * b + 5))
                e.wait_ge(unit_done, i * 20 + (U_MIX + 5 * b + 4))
                e.wait_ge(p_used, i * 4 + b)
                e.activation(sig[:, :, :], ps[:, 0:4, 0:TOK], ACT.Sigmoid).then_inc(sig_ready, 1)
                g, n0, nb = ((1, 0, 2), (2, 0, 1), (2, 1, 1), (0, 0, 2))[b]
                first = NT if g < 2 else 0
                e.dma_start(o[9 + g][0, bass.ds(i * 2 + n0, nb), 0:WIN_LEN[g] - first],
                            d[f"cache_win{g}"][0, bass.ds(i * 2 + n0, nb), first:WIN_LEN[g]]).then_inc(copied, 16)
                hi(unit_no(U_MIX, 20, i, 5 * b + 6))
            e.wait_ge(merged_f, i + 1)
            e.activation(M_hi[:, bass.ds(i * 4, 4), :], acc[:, :, :], ACT.Copy).then_inc(merged_hi, 1)

        e.wait_ge(merged_lo, 4)
        e.dma_start(x1[:, :, :], x_dram.ap()).then_inc(landed["x_back"], 16)
        for c in range(8):
            rows_in = d["state_conv"][0].rearrange("n t c -> (n t) c")
            e.dma_start(crow[16 * c:16 * c + 16, :, :],
                        bass.AP(rows_in.tensor, rows_in.offset + c * P, [[2 * D_FF, 16], [8 * P, 11], [1, P]]))\
                .then_inc(landed["crow"], 16)
        for n in range(2, 18):
            hi(unit_no(U_GATE, 8, 0, n))
            if n % 4 == 1:
                g = n // 4 - 1
                e.wait_ge(unit_done, U_GATE + 4 * g + 4)
                e.activation(m_T[:, 4 * g:4 * g + 4, :], ps[:, 4 * (g % 2):4 * (g % 2) + 4, 0:TOK], ACT.Copy)\
                    .then_inc(m_copied, 1)
                squares("mix_post", m_T, sq_b, g, [(m_copied, g + 1)])
        root("mix_post")
        for q in range(4):
            k = dve if q % 2 else pool
            squares("ffn_pre", x1, sq_b, q, [(k.sem, k.at(("x1", q)))])
        root("ffn_pre")
        for q in range(4):
            norm_hi("ffn_pre", xw_b, q)

        def h_out(i, s, done):
            e.wait_ge(unit_done, done)
            e.wait_ge(conv_step, i * 24)
            e.wait_ge(tails_put, i * 6)
            e.wait_ge(pool.sem, pool.at(("H0", 1)))
            src = ps[:, 4 * s:4 * s + 4, :]
            e.activation(H[s][:, :, 2:HS], src[:, :, 0:NP_TOK], ACT.Copy).then_inc(h_copied, 1)
            e.activation(view(H[s], P, HS + 2, [[HW, 4], [NT + 2, NB], [1, NT]]),
                         view(ps, P, 2048 * s + NP_TOK, [[512, 4], [NT, NB], [1, NT]]), ACT.Copy).then_inc(h_copied, 1)

        def act_high(i):
            e.wait_ge(act_f, i)
            e.activation(act_hi[:, :, 0:NP_TOK], hc[0][:, :, 0:NP_TOK], ACT.Copy).then_inc(act_hi_ready, 1)
            e.activation(view(act_hi, P, NP_TOK, [[TOK, 4], [NT, NB], [1, NT]]),
                         view(hc[0], P, HS, [[HW, 4], [NT + 2, NB], [1, NT]]), ACT.Copy).then_inc(act_hi_ready, 1)

        def ffn_round(i):
            down = not isinstance(i, int) or i > 0
            u0 = ffn_unit(i, 0)[0]
            if not isinstance(i, int):
                hi(ffn_unit(i, 0))
                hi(ffn_unit(i, 1))
            if isinstance(i, int):
                hi(ffn_unit(i, 2))
            if down:
                act_high(i)
            for j in range(3 if isinstance(i, int) else 2, 6):
                hi(ffn_unit(i, j))
            h_out(i, 0, u0 + 4)
            hi(ffn_unit(i, 6))
            hi(ffn_unit(i, 7))
            for j in (8, 9):
                hi(ffn_unit(i, j) if down else ffn_unit(1, j - 8))
            h_out(i, 1, u0 + 8)
            e.wait_ge(conv_step, i * 24 + 12)
            e.activation(hc[0][:, :, 0:HW - 2], hc[0][:, :, 0:HW - 2], ACT.Gelu_apprx_tanh).then_inc(gelu_done, 1)
            if down:
                hi(ffn_unit(i, 10))
                hi(ffn_unit(i, 11))
        ffn_round(0)
        ffn_round(1)
        with e.Fori(2, 11) as i:
            ffn_round(i)
        hi(ffn_unit(11, 0))
        e.wait_ge(unit_done, ffn_unit(11, 0)[0])
        act_high(11)
        hi(ffn_unit(11, 1))
        hi(ffn_unit(11, 2))
        hi(ffn_unit(11, 3))
        e.wait_ge(lo_ready, 272)
        e.wait_ge(pe.sem, pe.at("tailT"))
        e.activation(tail_rows[:, 0:12, :], view(ps, 7 * TAIL, 0, [[P, 12], [1, P]]), ACT.Copy)\
            .then_inc(act.sem, act.step("tail_rows0"))
        e.activation(tail_rows[0:4 * TAIL, 12, :], ps[0:4 * TAIL, 3, 0:P], ACT.Copy)\
            .then_inc(act.sem, act.step("tail_rows"))
        for q in range(4):
            squares("ffn_post", m_T, sq_f, q, [(y_added, 4 + 4 * 10 + q + 1)])
        root("ffn_post")
        for m in range(3):
            n = P if m < 2 else NS
            e.wait_ge(pe.sem, pe.at(("yT", m)))
            b = 4 * ((m + 1) % 2)
            e.activation(y_nat[0:n, m, 0:1024], view(ps, n, b * 512, [[1, 1024]]), ACT.Copy)\
                .then_inc(act.sem, act.step(("y", m)))

    @block.vector
    def _(e):
        def lo(no, k=SEG, n=UNIT_COLS):
            u, _, slot, s = no
            e.wait_ge(hi_ready, u + 1)
            e.tensor_tensor(w_lo[s][:, 0:k, 0:n], w_raw[slot][:, 0:k, 0:n], w_hi[s][:, 0:k, 0:n].bitcast(F32),
                            ALU.subtract).then_inc(lo_ready, 1)

        def variance(tag, bank, n, name):
            e.wait_ge(pe.sem, pe.at(name))
            e.tensor_scalar(stat[:, 0, :], ps[:, bank, 0:TOK], 1.0 / n, EPS, ALU.mult, ALU.add)\
                .then_inc(dve.sem, dve.step((tag, "var")))

        def rstd(tag):
            e.wait_ge(act.sem, act.at((tag, "sd")))
            e.reciprocal(stat[:, 2, :], stat[:, 1, :]).then_inc(dve.sem, dve.step((tag, "rstd")))
            e.wait_ge(dve.sem, dve.at((tag, "rstd")))

        def scaled(tag, dst, src, q):
            g = NORM[tag]
            for c in range(4 * q, 4 * q + 4):
                e.scalar_tensor_tensor(out=dst[:, c, :], in0=src[:, c, :], scalar=gains[:, g + c:g + c + 1],
                                       in1=stat[:, 2, :], op0=ALU.mult, op1=ALU.mult)\
                    .then_inc(dve.sem, dve.step((tag, "w", c)))

        def norm_lo(tag, src, q):
            e.wait_ge(act.sem, act.at((tag, "hi", q)))
            e.tensor_tensor(xn_lo[:, 4 * q:4 * q + 4, :], src[:, 4 * q:4 * q + 4, :],
                            xn_hi[:, 4 * q:4 * q + 4, :].bitcast(F32), ALU.subtract)\
                .then_inc(dve.sem, dve.step((tag, "lo", q)))

        def norm(tag, dst, src, before):
            for q in (0, 1):
                scaled(tag, dst, src, q)
                before(q)
                norm_lo(tag, dst, q)
            for q in (2, 3):
                scaled(tag, dst, src, q)
            for q in (2, 3):
                norm_lo(tag, dst, q)

        for c in range(0, KC, 2):
            e.wait_ge(pe.sem, pe.at(("xT", c)))
            e.tensor_copy(x_T[:, c, :], ps[:, 4, 0:TOK]).then_inc(dve.sem, dve.step(("x_T", c)))
        e.wait_ge(landed["tab"], 16)
        e.wait_ge(pool.sem, pool.at("tab_neg"))
        e.tensor_copy(tabx[:, :, :], view(tab, 33, 0, [[1, N_HEADS], [0, P]])).then_inc(dve.sem, dve.step("tabx"))
        e.wait_ge(pe.sem, pe.at("nrowT"))
        e.tensor_copy(gains[:, :], ps[:, 6, 0:72]).then_inc(dve.sem, dve.step("gains"))
        variance("mix_pre", 7, D_MODEL, ("mix_pre", "ss", 3))
        e.wait_ge(pe.sem, pe.at("prowT"))
        e.tensor_copy(conv[:, :, :], view(ps, P, 5 * 512, [[88, 4], [1, 88]])).then_inc(dve.sem, dve.step("conv"))
        rstd("mix_pre")
        e.wait_ge(act.sem, act.at(("x_T", KC - 1)))
        norm("mix_pre", xw, x_T, lambda q: lo(unit_no(0, 8, 0, q)))

        for j in range(2, 4):
            lo(unit_no(0, 8, 0, j))
        e.wait_ge(landed["tab2"], 32)
        e.wait_ge(pool.sem, pool.at("tab_t0"))
        e.tensor_copy(view(tab_t, 65, 0, [[4, N_HEADS], [41, NT]]), view(tab2, 65, 0, [[1, N_HEADS], [0, NT]]))\
            .then_inc(dve.sem, dve.step("tab_t"))
        e.tensor_copy(tab_all[:, :, :], view(tab2, 65, 0, [[1, N_HEADS], [0, NT]]))\
            .then_inc(dve.sem, dve.step("tab_all"))
        e.wait_ge(dve.sem, dve.at("tab_all"))
        e.tensor_copy(tabr_t[:, :, :, :], tab_t[:, :, :, :]).then_inc(dve.sem, dve.step("tabr_t0"))
        e.tensor_copy(tabr_all[:, :, :], tab_all[:, :, :]).then_inc(dve.sem, dve.step("tabr_all0"))
        e.wait_ge(dve.sem, dve.at("tabr_all0"))
        e.tensor_tensor(tabr_t[32:64, :, :, :], tab_t[32:64, :, :, :], tabr_t[32:64, :, :, :].bitcast(F32),
                        ALU.subtract).then_inc(dve.sem, dve.step("tabr_t"))
        e.tensor_tensor(tabr_all[32:64, :, :], tab_all[32:64, :, :], tabr_all[32:64, :, :].bitcast(F32),
                        ALU.subtract).then_inc(dve.sem, dve.step("tabr"))
        with e.Fori(0, 4) as i:
            for j in range(8):
                lo(unit_no(4, 8, i, j))
        for j in range(4):
            lo(unit_no(36, 8, 0, j))
        for j in range(4):
            lo(unit_no(40, 8, 0, j), n=256)

        e.wait_ge(pe.sem, pe.at("vsum"))
        e.wait_ge(lo_ready, U_MIX)
        e.scalar_tensor_tensor(out=vn[:, :, :], in0=view(ps, P, 6 * 512, [[0, 4], [1, TOK]]), scalar=-1.0 / 512,
                               in1=Z[:, V_C:X_D, :], op0=ALU.mult, op1=ALU.add).then_inc(dve.sem, dve.step("xc"))
        e.wait_ge(landed["x_saved"], 16)
        for m in range(3):
            e.wait_ge(pe.sem, pe.at(("tok", 2 * m + 1)))
            n = P if m < 2 else NS
            dst = v_tok[:, m, :] if m < 2 else v_own[:, :]
            e.tensor_copy(dst, view(ps, n, 3 * 512, [[1, 1280]])).then_inc(dve.sem, dve.step(("v_tok", m)))
        e.wait_ge(pe.sem, pe.at("vvar"))
        e.tensor_scalar(stat[:, 0, :], ps[:, 7, 0:TOK], 1.0 / 512, EPS, ALU.mult, ALU.add)\
            .then_inc(dve.sem, dve.step("c_var"))
        e.wait_ge(pe.sem, pe.at("histT"))
        for c in range(4):
            e.tensor_copy(view(xe_a, P, c * XE + XS, [[HIST + NT, NB], [1, HIST]]),
                          view(ps, P, 6 * 512 + 120 * c, [[HIST, NB], [1, HIST]]))\
                .then_inc(dve.sem, dve.step("xe_hist" if c == 3 else ("xe_hist", c)))
        e.wait_ge(act.sem, act.at("c_sd"))
        e.reciprocal(stat[:, 2, :], stat[:, 1, :]).then_inc(dve.sem, dve.step("c_rstd"))
        e.wait_ge(dve.sem, dve.at("c_rstd"))
        for c in range(4):
            g = NORM["c_ln"] + c
            e.scalar_tensor_tensor(out=vn[:, c, :], in0=vn[:, c, :], scalar=gains[:, g:g + 1], in1=stat[:, 2, :],
                                   op0=ALU.mult, op1=ALU.mult).then_inc(dve.sem, dve.step(("vn", c)))
        for m in range(3):
            n = P if m < 2 else NS
            e.wait_ge(pe.sem, pe.at(("vnT", m)))
            e.tensor_copy(vc_tok[0:n, m, :], ps[0:n, m, :]).then_inc(dve.sem, dve.step(("vc", m)))
        e.wait_ge(pe.sem, pe.at("wrep"))
        for g in range(4):
            e.tensor_tensor(wd[:, g, :, :], view(ps, NS, 7 * 512 + 4 * g, [[0, NB], [1, NT]]),
                            view(same, NS, 0, [[1, NB], [0, NT]]), ALU.mult)\
                .then_inc(dve.sem, dve.step(("wd", g)))
        for g in range(4):
            e.tensor_copy(bs_own[:, g, :, :], view(bs, 1, P * g, [[0, NB], [1, NT]]))\
                .then_inc(dve.sem, dve.step(("bs_own", g)))
        for m in range(3):
            e.wait_ge(pe.sem, pe.at(("mix", m)))
            t0, n = m * P, P if m < 2 else NS
            e.tensor_tensor(O[:, 6:10, t0:t0 + n], view(ps, P, (3 + m) * 512, [[n, 4], [1, n]]),
                            Z[:, U_C:V_C, t0:t0 + n], ALU.mult).then_inc(dve.sem, dve.step(("oc", m)))
        e.wait_ge(pool.sem, pool.at("s16"))
        sums = [xe_b, xe_a, xe_b, xe_a]
        for c in range(4):
            e.tensor_tensor(sums[c][:, c, HIST:HIST + 15], sums[c][:, c, HIST:HIST + 15],
                            ramp[:, 16 * c:16 * c + 15], ALU.mult).then_inc(dve.sem, dve.step(("ramp", c)))
        e.wait_ge(dve.sem, dve.at(("ramp", 3)))
        for c in range(4):
            e.scalar_tensor_tensor(out=pooled[:, c, 0:NP_TOK], in0=sums[c][:, c, HIST:XS], scalar=1.0 / D_WIN[c],
                                   in1=Z[:, X_D + c, 0:NP_TOK], op0=ALU.mult, op1=ALU.subtract)\
                .then_inc(dve.sem, dve.step(("pooled0", c)))
            e.scalar_tensor_tensor(out=view(pooled, P, c * TOK + NP_TOK, [[NT, NB], [1, NT]]),
                                   in0=view(sums[c], P, c * XE + XS + HIST, [[HIST + NT, NB], [1, NT]]),
                                   scalar=1.0 / D_WIN[c],
                                   in1=view(Z, P, (X_D + c) * TOK + NP_TOK, [[NT, NB], [1, NT]]),
                                   op0=ALU.mult, op1=ALU.subtract).then_inc(dve.sem, dve.step(("pooled", c)))

        def logits(k):
            groups, oc, m = units[k]
            bank, lp, c, _ = room(k)
            ng, nk, h0 = len(groups), (m + 1) * P, groups[0][3]
            n = ng * nk
            e.wait_ge(pe.sem, pe.at(("S", k)))
            if k >= 2:
                e.wait_ge(pe.sem, pe.at(("PT", k - 2 if k < NA else max(NA - 2, k - 3))))
            e.scalar_tensor_tensor(out=view(Lp, P, lp, [[nk, ng], [1, nk]]),
                                   in0=view(ps, P, 512 * bank, [[512, ng], [1, nk]]), scalar=SCALE,
                                   in1=view(U, P, h0 * 256 + 256 - nk, [[512, ng], [1, nk]]),
                                   op0=ALU.mult, op1=ALU.add).then_inc(dve.sem, dve.step(("L", k)))
            e.wait_ge(dve.sem, dve.at(("L", k)))
            e.tensor_reduce(col[:, c:c + 1], view(Lp, P, lp, [[1, n]]), AX.X, ALU.max, negate=True)\
                .then_inc(dve.sem, dve.step(("nm", k)))

        def normalise(k):
            groups, oc, m = units[k]
            _, lp, c, _ = room(k)
            n = len(groups) * (m + 1) * P
            e.wait_ge(act.sem, act.at(("E", k)))
            e.reciprocal(col[:, 6 + c:7 + c], col[:, 3 + c:4 + c]).then_inc(dve.sem, dve.step(("rs", k)))
            e.wait_ge(dve.sem, dve.at(("rs", k)))
            e.tensor_scalar(view(Lp, P, lp, [[1, n]]), view(Lp, P, lp, [[1, n]]), col[:, 6 + c:7 + c], None, ALU.mult)\
                .then_inc(dve.sem, dve.step(("P", k)))
        e.wait_ge(landed["u"], 16)
        logits(0)
        for k in range(NU):
            normalise(k)
            for j in range(ahead(k - 1) + 1 if k else 1, ahead(k) + 1):
                logits(j)

        for k in range(2):
            e.wait_ge(pe.sem, pe.at(("bias_b", k)))
            e.tensor_copy(bias_b[:, 512 * k:512 * k + 512], ps[0:16, k, :]).then_inc(dve.sem, dve.step(("bias_b", k)))
        e.wait_ge(pe.sem, pe.at("bias_a"))
        e.tensor_copy(bias_a[:, 0:320], ps[0:8, 2, 0:320]).then_inc(dve.sem, dve.step("bias_past"))
        for g in range(3):
            e.tensor_copy(view(bias_a, 8, 320 + 32 * g, [[96, NB], [1, NS]]),
                          view(ps, 8, (3 * 512, 4 * 512, 4 * 512 + 256)[g], [[NS, NB], [1, NS]]))\
                .then_inc(dve.sem, dve.step(("bias_own", g)))
        e.tensor_copy(bias_b[:, PAST:PAST + NB * NS], ps[0:16, 5, 0:NB * NS]).then_inc(dve.sem, dve.step("bias"))
        e.wait_ge(dve.sem, dve.at("bias"))
        e.wait_ge(pool.sem, pool.at("pt_a0"))

        e.wait_ge(act.sem, act.at("own_hi"))
        e.tensor_tensor(own_lo[:, :], v_own[:, 768:1280], own_hi[:, :].bitcast(F32), ALU.subtract)\
            .then_inc(dve.sem, dve.step("own_lo"))

        def odd_keys(n8, q):
            e.wait_ge(keys_turned, n8 + (q + 1))
            e.tensor_copy(kt_b[:, 1, :], ps[:, q % 3, :]).then_inc(keys_odd, 1)

        def sample(i, last):
            name, at = sample_steps(i, last)

            def window_keys(b):
                n = 512 if b == 1 else 256
                e.wait_ge(pe.sem, at(pe, ("kTa", b)))
                e.tensor_copy(kt_a[:, b, 0:n], ps[:, (8 + b) % 3, 0:n]).then_inc(dve.sem, dve.step(name(("kt_a", b))))

            def then(ins, x):
                ins.then_inc(dve.sem, dve.step(name(x)))
                e.wait_ge(dve.sem, at(dve, x))
            window_keys(1)
            e.wait_ge(scored, i * 8 + 8)
            e.wait_ge(pe.sem, at(pe, "ptb", back=1))
            e.tensor_reduce(col[0:16, 6:10], view(ps, 16, 4 * 512, [[BLOCK_KEYS, N_BLOCKS], [1, BLOCK_KEYS]]),
                            AX.X, ALU.add).then_inc(dve.sem, dve.step(name("blocks")))
            e.scalar_tensor_tensor(out=L_b[:, 0:PAST], in0=view(ps, 16, 4 * 512, [[1, PAST]]), scalar=SCALE,
                                   in1=bias_b[:, 0:PAST], op0=ALU.mult, op1=ALU.add)\
                .then_inc(dve.sem, dve.step(name("L_b0")))
            e.wait_ge(pe.sem, at(pe, "own_b"))
            e.scalar_tensor_tensor(out=L_b[:, PAST:PAST + NS], in0=ps[0:16, 7, 0:NS], scalar=SCALE,
                                   in1=view(bias_b, 16, i * NS + PAST, [[1, NS]]), op0=ALU.mult, op1=ALU.add)\
                .then_inc(dve.sem, dve.step(name("L_b")))
            window_keys(3)
            if not last:
                odd_keys(i * 8 + 8, 1)
            e.wait_ge(dve.sem, at(dve, "L_b"))
            then(e.tensor_reduce(col[0:16, 10:11], col[0:16, 6:10], AX.X, ALU.min), "least")
            then(e.scalar_tensor_tensor(out=col[0:16, 12:16], in0=col[0:16, 6:10], scalar=col[0:16, 10:11],
                                        in1=rank[:, :], op0=ALU.is_equal, op1=ALU.mult), "ranks")
            then(e.tensor_reduce(col[0:16, 11:12], col[0:16, 12:16], AX.X, ALU.max), "last")
            then(e.tensor_scalar(col[0:16, 12:16], col[0:16, 12:16], col[0:16, 11:12], NEG,
                                 ALU.is_equal, ALU.mult), "drop")
            then(e.tensor_tensor(L_b[:, 0:PAST], L_b[:, 0:PAST],
                                 view(col, 16, 12, [[1, N_BLOCKS], [0, BLOCK_KEYS]]), ALU.add), "masked")
            e.tensor_reduce(col[0:16, 0:1], L_b[:, :], AX.X, ALU.max, negate=True)\
                .then_inc(dve.sem, dve.step(name("nm_b")))
            e.wait_ge(pe.sem, at(pe, "s_a"))
            e.scalar_tensor_tensor(out=L_a[:, 0:320], in0=ps[0:8, 6, 0:320], scalar=SCALE, in1=bias_a[:, 0:320],
                                   op0=ALU.mult, op1=ALU.add).then_inc(dve.sem, dve.step(name("L_a0")))
            then(e.scalar_tensor_tensor(out=L_a[:, 320:416], in0=ps[0:8, 6, 320:416], scalar=SCALE,
                                        in1=view(bias_a, 8, i * 96 + 320, [[1, 96]]),
                                        op0=ALU.mult, op1=ALU.add), "L_a")
            e.tensor_reduce(col[0:8, 3:4], L_a[:, :], AX.X, ALU.max, negate=True)\
                .then_inc(dve.sem, dve.step(name("nm_a")))
            if not last:
                odd_keys(i * 8 + 8, 3)
            e.wait_ge(act.sem, at(act, "E_b"))
            then(e.reciprocal(col[0:16, 2:3], col[0:16, 1:2]), "rs_b")
            e.tensor_scalar(L_b[:, :], L_b[:, :], col[0:16, 2:3], None, ALU.mult)\
                .then_inc(dve.sem, dve.step(name("P_b")))

            def values_lo(half):
                e.wait_ge(act.sem, at(act, ("v_hi", half)))
                e.tensor_tensor(v_lo[half][:, :, :], kv[4 + half][:, :, :], v_hi[half][:, :, :].bitcast(F32),
                                ALU.subtract).then_inc(dve.sem, dve.step(name(("v_lo", half))))
            values_lo(0)
            if not last:
                odd_keys(i * 8 + 8, 5)
            e.wait_ge(act.sem, at(act, "pt_b"))
            e.tensor_tensor(pt_b[:, 0:8, 16:32], view(ps, P, 7 * 512, [[16, 8], [1, 16]]),
                            pt_b[:, 0:8, 0:16].bitcast(F32), ALU.subtract).then_inc(dve.sem, dve.step(name("pt_b0")))
            e.tensor_tensor(pt_b[0:NS, 8, 16:32], ps[0:NS, 7, 128:144], pt_b[0:NS, 8, 0:16].bitcast(F32),
                            ALU.subtract).then_inc(dve.sem, dve.step(name("pt_b")))
            e.wait_ge(act.sem, at(act, "E_a"))
            e.reciprocal(col[0:8, 5:6], col[0:8, 4:5]).then_inc(dve.sem, dve.step(name("rs_a")))
            if not last:
                odd_keys(i * 8 + 8, 7)
            values_lo(1)
            e.wait_ge(pe.sem, at(pe, "pta"))
            e.tensor_copy(pt_a[:, 0:8], ps[:, 7, 160:168]).then_inc(dve.sem, dve.step(name("pt_a0")))
            e.tensor_copy(view(pt_a, P, 8, [[4, HPG], [9, NT]]), view(ps, P, 7 * 512 + 168, [[4, HPG], [1, NT]]))\
                .then_inc(dve.sem, dve.step(name("pt_a1")))
            e.tensor_copy(view(pt_a, 64, 40, [[4, HPG], [9, NT]]), view(ps, 64, 7 * 512 + 176, [[4, HPG], [1, NT]]))\
                .then_inc(dve.sem, dve.step(name("pt_a2")))
            e.tensor_copy(pt_a[0:NS, 72:96], ps[0:NS, 7, 184:208]).then_inc(dve.sem, dve.step(name("pt_a")))
            e.wait_ge(pe.sem, at(pe, "ota"))
            e.tensor_copy(ot_lo[:, :], view(ps, P, 7 * 512 + 16, [[36, B_HEADS], [1, NT]]))\
                .then_inc(dve.sem, dve.step(name("ot_lo")))
            e.wait_ge(dve.sem, at(dve, "ot_lo"))
            e.tensor_tensor(view(O, P, i * NT + (2 * TOK + NP_TOK), [[TOK, B_HEADS], [1, NT]]),
                            view(ps, P, 7 * 512, [[36, B_HEADS], [1, NT]]), ot_lo[:, :], ALU.add)\
                .then_inc(dve.sem, dve.step(name("o_b")))
            e.tensor_copy(view(O, P, i * NT + NP_TOK, [[TOK, HPG], [1, NT]]),
                          view(ps, P, 7 * 512 + 128, [[12, HPG], [1, NT]])).then_inc(dve.sem, dve.step(name("o_a")))
        for q in range(1, 8, 2):
            odd_keys(0, q)
        dve.begin("sample")
        with e.Fori(0, NB - 1) as i:
            sample(i, False)
        dve.end(NB - 1)
        sample(NB - 1, True)

        for j in range(2):
            lo(unit_no(U_MIX, 20, 0, j))
        for h in range(2):
            e.wait_ge(act.sem, act.at(("O_hi", h)))
            e.tensor_tensor(O_lo[:, 7 * h:7 * h + 7, :], O[:, 7 * h:7 * h + 7, :],
                            O_hi[:, 7 * h:7 * h + 7, :].bitcast(F32), ALU.subtract)\
                .then_inc(dve.sem, dve.step(("O_lo", h)))
        with e.Fori(0, 4) as i:
            def merge(b):
                e.wait_ge(unit_done, i * 20 + (U_MIX + 5 * b + 5))
                e.wait_ge(sig_ready, i * 4 + (b + 1))
                if b == 0:
                    e.wait_ge(merged_lo, i)
                dst = tmp if b else acc
                e.tensor_tensor(dst[:, :, :], ps[:, 4:8, 0:TOK], sig[:, :, :], ALU.mult).then_inc(p_used, 1)
                if b:
                    e.wait_ge(p_used, i * 4 + (b + 1))
                    if b >= 2:
                        e.wait_ge(merge_step, i * 2 + (b - 1))
                    e.tensor_tensor(acc[:, :, :], acc[:, :, :], tmp[:, :, :], ALU.add)\
                        .then_inc(merge_step if b < 3 else merged_f, 1)
            for b in range(4):
                for j in range(2, 4):
                    lo(unit_no(U_MIX, 20, i, 5 * b + j))
                lo(unit_no(U_MIX, 20, i, 5 * b + 4), k=P_CHUNKS[b])
                lo(unit_no(U_MIX, 20, i, 5 * b + 5))
                merge(b)
                lo(unit_no(U_MIX, 20, i, 5 * b + 6))
            e.wait_ge(merged_hi, i + 1)
            e.tensor_tensor(M_lo[:, bass.ds(i * 4, 4), :], acc[:, :, :], M_hi[:, bass.ds(i * 4, 4), :].bitcast(F32),
                            ALU.subtract).then_inc(merged_lo, 1)

        with e.Fori(0, 2) as i:
            for j in range(2, 10):
                lo(unit_no(U_GATE, 8, i, j))
        variance("mix_post", 3, D_MODEL, ("mix_post", "ss", 3))
        e.wait_ge(pe.sem, pe.at("histc"))
        e.tensor_copy(view(hist_c, P, 0, [[1, 1408]]), view(ps, P, 0, [[1, 1408]])).then_inc(dve.sem, dve.step("hist_c"))
        rstd("mix_post")
        e.wait_ge(m_copied, 4)
        e.wait_ge(landed["x_back"], 16)
        for q in range(4):
            scaled("mix_post", m_T, m_T, q)
            if q % 2:
                e.wait_ge(dve.sem, dve.at(("mix_post", "w", 4 * q + 3)))
                e.tensor_tensor(x1[:, 4 * q:4 * q + 4, :], x1[:, 4 * q:4 * q + 4, :], m_T[:, 4 * q:4 * q + 4, :],
                                ALU.add).then_inc(dve.sem, dve.step(("x1", q)))
        e.wait_ge(dve.sem, dve.at(("x1", 3)))
        e.wait_ge(pool.sem, pool.at(("x1", 2)))
        for q in range(4):
            e.memset(m_T[:, 4 * q:4 * q + 4, :], 0.0).then_inc(y_added, 1)
        variance("ffn_pre", 3, D_MODEL, ("ffn_pre", "ss", 3))
        rstd("ffn_pre")
        norm("ffn_pre", xw_b, x1, lambda q: None)

        def conv_pair(i, s, k):
            if k == 0:
                e.wait_ge(h_copied, i * 4 + (2 * s + 2))
                e.wait_ge(hist_put, i * 4 + (2 * s + 2))
            base = 12 * s + 6 * (k // 2)
            for tap in range(3):
                for c in (k, k + 1):
                    w = [view(conv, P, i * 4 + (FC * s + c + 88 * r), [[1, 1]]) for r in range(4)]
                    src = H[s][:, c, tap:tap + HW - 2]
                    dst = hc[s][:, c, 0:HW - 2]
                    if tap == 0:
                        e.tensor_scalar(dst, src, w[0], w[3], ALU.mult, ALU.add).then_inc(conv_step, 1)
                    else:
                        e.wait_ge(conv_step, i * 24 + (base + 2 * (tap - 1) + (c - k) + 1))
                        e.scalar_tensor_tensor(out=dst, in0=src, scalar=w[tap], in1=dst, op0=ALU.mult, op1=ALU.add)\
                            .then_inc(conv_step, 1)

        def product(i):
            e.wait_ge(gelu_done, i)
            e.wait_ge(conv_step, i * 24)
            e.tensor_tensor(hc[0][:, :, 0:HW - 2], hc[0][:, :, 0:HW - 2], hc[1][:, :, 0:HW - 2], ALU.mult)\
                .then_inc(act_f, 1)

        def act_low(i):
            e.wait_ge(act_hi_ready, i * 2)
            e.tensor_tensor(act_lo[:, :, 0:NP_TOK], hc[0][:, :, 0:NP_TOK], act_hi[:, :, 0:NP_TOK].bitcast(F32),
                            ALU.subtract).then_inc(act_ready, 1)
            lo_own = view(act_lo, P, NP_TOK, [[TOK, 4], [NT, NB], [1, NT]])
            hi_own = act_hi[:, :, NP_TOK:TOK].rearrange("p c (n t) -> p c n t", t=NT).bitcast(F32)
            e.tensor_tensor(lo_own, view(hc[0], P, HS, [[HW, 4], [NT + 2, NB], [1, NT]]), hi_own,
                            ALU.subtract).then_inc(act_ready, 1)

        def y_add(i, j, no):
            e.wait_ge(unit_done, no[0] + 1)
            e.wait_ge(y_added, i * 4 + (j - 0))
            e.tensor_tensor(m_T[:, 4 * j:4 * j + 4, :], ps[:, 4 * (j % 2):4 * (j % 2) + 4, 0:TOK],
                            m_T[:, 4 * j:4 * j + 4, :], ALU.add).then_inc(y_added, 1)

        def ffn_round(i):
            fixed = isinstance(i, int)
            down, before = not fixed or i > 0, not fixed or i > 1
            if before:
                y_add(i - 1, 2, ffn_unit(i - 1, 10))
                lo(ffn_unit(i, 0))
                y_add(i - 1, 3, ffn_unit(i - 1, 11))
                lo(ffn_unit(i, 1))
            if fixed:
                lo(ffn_unit(i, 2))
            if down:
                product(i)
            if not fixed:
                lo(ffn_unit(i, 2))
            if down:
                act_low(i)
            for j in range(3, 7):
                lo(ffn_unit(i, j))
            conv_pair(i, 0, 0)
            lo(ffn_unit(i, 7))
            conv_pair(i, 0, 2)
            if not down:
                lo(ffn_unit(1, 0))
                lo(ffn_unit(1, 1))
            if down:
                lo(ffn_unit(i, 8))
                lo(ffn_unit(i, 9))
                y_add(i, 0, ffn_unit(i, 8))
                lo(ffn_unit(i, 10))
            conv_pair(i, 1, 0)
            if down:
                y_add(i, 1, ffn_unit(i, 9))
                lo(ffn_unit(i, 11))
            conv_pair(i, 1, 2)
        ffn_round(0)
        ffn_round(1)
        with e.Fori(2, 11) as i:
            ffn_round(i)
        lo(ffn_unit(11, 0))
        product(11)
        y_add(10, 2, ffn_unit(10, 10))
        act_low(11)
        y_add(10, 3, ffn_unit(10, 11))
        lo(ffn_unit(11, 1))
        y_add(11, 0, ffn_unit(11, 0))
        lo(ffn_unit(11, 2))
        y_add(11, 1, ffn_unit(11, 1))
        lo(ffn_unit(11, 3))
        y_add(11, 2, ffn_unit(11, 2))
        y_add(11, 3, ffn_unit(11, 3))

        variance("ffn_post", 7, D_MODEL, ("ffn_post", "ss", 3))
        rstd("ffn_post")
        for q in range(4):
            scaled("ffn_post", m_T, m_T, q)
            if q % 2:
                e.wait_ge(dve.sem, dve.at(("ffn_post", "w", 4 * q + 3)))
                e.tensor_tensor(m_T[:, 4 * q:4 * q + 4, :], m_T[:, 4 * q:4 * q + 4, :], x1[:, 4 * q:4 * q + 4, :],
                                ALU.add).then_inc(dve.sem, dve.step(("yf", q)))
        for m in range(3):
            n = P if m < 2 else NS
            e.wait_ge(pe.sem, pe.at(("yT", m)))
            b = 4 * ((m + 1) % 2) + 2
            e.tensor_copy(y_nat[0:n, m, 1024:2048], view(ps, n, b * 512, [[1, 1024]]))\
                .then_inc(dve.sem, dve.step(("y", m)))

    @block.tensor
    def _(e):
        def turn(dst, src, n):
            return e.transpose(dst, src, ident[0:n, 0:n])

        def sums(tag, sq, q, bank):
            e.wait_ge(act.sem, act.at((tag, "sq", q)))
            for k in range(4):
                mm = e.matmul(ps[:, bank, 0:TOK], ones[:, :], sq[:, q, k, :], start=q == 0 and k == 0,
                              stop=q == 3 and k == 3)
            mm.then_inc(pe.sem, pe.step((tag, "ss", q)))

        def unit(no, x_hi, x_lo, k0, side, first, last, k=SEG, n=4):
            u, _, _, s = no
            e.wait_ge(lo_ready, u + 1)
            for r in range(k):
                for c in range(n):
                    dst = ps[:, 4 * side + c, 0:TOK]
                    cols = slice(c * P, c * P + P)
                    e.matmul(dst, w_hi[s][:, r, cols], x_hi[:, k0 + r, :], start=first and r == 0, stop=False)
                    e.matmul(dst, w_hi[s][:, r, cols], x_lo[:, k0 + r, :], start=False, stop=False)
                    mm = e.matmul(dst, w_lo[s][:, r, cols], x_hi[:, k0 + r, :], start=False,
                                  stop=last and r == k - 1)
            mm.then_inc(unit_done, 1)

        e.wait_ge(pool.sem, pool.at("ident"))
        e.wait_ge(landed["x"], 16)
        for c in range(KC):
            if c % 4 == 0:
                e.wait_ge(x_landed[c // 4], 16)
            if c >= 2:
                k = act if c % 2 else dve
                e.wait_ge(k.sem, k.at(("x_T", c - 2)))
            for m in range(3):
                n = P if m < 2 else NS
                mm = turn(ps[:, 4 + c % 2, m * P:m * P + n], x_nat[0:n, m, c * P:c * P + P], n)
            mm.then_inc(pe.sem, pe.step(("xT", c)))
        def bias_rows(h0, h1):
            for h in range(h0, h1):
                if h >= 3:
                    e.wait_ge(act.sem, act.at(("urow", h - 3)))
                e.matmul(ps[:, 4 + h % 3, 0:384], tabx[:, h, :], oh_prompt[:, h // 2 if h < A_HEADS else 3, :],
                         start=True, stop=True).then_inc(pe.sem, pe.step(("urow", h)))
        e.wait_ge(landed["nrow"], 16 * 6)
        turn(ps[:, 6, 0:72], nrow[:, :], 72).then_inc(pe.sem, pe.step("nrowT"))
        for q in range(4):
            sums("mix_pre", sq_a, q, 7)
        e.wait_ge(landed["prow"], 32)
        e.wait_ge(act.sem, act.at(("x_T", KC - 1)))
        for r in range(4):
            mm = turn(ps[:, 5, 88 * r:88 * r + 88], prow[:, r, :], 88)
        mm.then_inc(pe.sem, pe.step("prowT"))
        e.wait_ge(landed["oh_prompt"], 16)
        e.wait_ge(dve.sem, dve.at("tabx"))
        e.wait_ge(dve.sem, dve.at("conv"))
        bias_rows(0, 3)

        def group(nos, side, n=4):
            for j, no in enumerate(nos):
                unit(no, xn_hi, xn_lo, 4 * j, side, j == 0, j == 3, n=n)
        for j in range(4):
            e.wait_ge(dve.sem, dve.at(("mix_pre", "lo", j)))
            unit(unit_no(0, 8, 0, j), xn_hi, xn_lo, 4 * j, 0, j == 0, j == 3)
            bias_rows(3 * j + 3, min(3 * j + 6, N_HEADS))
        e.wait_ge(act.sem, act.at(("urow", N_HEADS - 1)))
        with e.Fori(0, 4) as i:
            for h in range(2):
                e.wait_ge(z_copied, i * 2 + h)
                group([unit_no(4, 8, i, 4 * h + j) for j in range(4)], 1 - h)
        e.wait_ge(z_copied, 8)
        group([unit_no(36, 8, 0, j) for j in range(4)], 1)
        e.wait_ge(z_copied, 9)
        group([unit_no(40, 8, 0, j) for j in range(4)], 0, n=2)

        e.wait_ge(z_copied, 11)
        e.wait_ge(act.sem, act.at("gelu"))
        for k in range(4):
            mm = e.matmul(ps[:, 6, 0:TOK], ones[:, :], Z[:, V_C + k, :], start=k == 0, stop=k == 3)
        mm.then_inc(pe.sem, pe.step("vsum"))
        for r in range(6):
            m, v = r // 2, r % 2
            n = P if m < 2 else NS
            if r >= 2:
                k, name = (dve, "v_tok") if v else (act, "k_tok")
                e.wait_ge(k.sem, k.at((name, m - 1)))
            chunks = [(V_A if v else K_A) + c for c in range(6)] + [(V_B if v else K_B) + c for c in range(4)]
            for c, chunk in enumerate(chunks):
                mm = turn(view(ps, n, 1536 * v + P * c, [[1, P]]), Z[:, chunk, m * P:m * P + n], P)
            mm.then_inc(pe.sem, pe.step(("tok", r)))
        e.wait_ge(act.sem, act.at("xc_sq"))
        for k in range(4):
            mm = e.matmul(ps[:, 7, 0:TOK], ones[:, :], sq_c[:, k, :], start=k == 0, stop=k == 3)
        mm.then_inc(pe.sem, pe.step("vvar"))
        e.wait_ge(landed["ws"], 16)
        for g in range(4):
            mm = turn(ps[:, 6, g * P:g * P + P], ws_nat[:, g, :], P)
        mm.then_inc(pe.sem, pe.step("ws_T"))
        e.wait_ge(dve.sem, dve.at("c_var"))
        e.wait_ge(dve.sem, dve.at(("v_tok", 2)))
        for c in range(4):
            turn(ps[0:HIST, 7, c * P:c * P + P], Z[:, X_D + c, NP_TOK - HIST:NP_TOK], P)
            mm = turn(ps[0:NS, 3, c * P:c * P + P], Z[:, X_D + c, NP_TOK:TOK], P)
        mm.then_inc(pe.sem, pe.step("xdT"))
        e.wait_ge(landed["hist"], 16)
        e.wait_ge(act.sem, act.at("ws_T"))
        for c in range(4):
            mm = turn(ps[:, 6, 120 * c:120 * c + 120], hist_rows[:, c * P:c * P + P], 120)
        mm.then_inc(pe.sem, pe.step("histT"))
        e.wait_ge(act.sem, act.at(("k_tok", 2)))
        e.wait_ge(dve.sem, dve.at(("vn", 3)))
        for m in range(3):
            n = P if m < 2 else NS
            for c in range(4):
                mm = turn(ps[0:n, m, c * P:c * P + P], vn[:, c, m * P:m * P + n], P)
            mm.then_inc(pe.sem, pe.step(("vnT", m)))
        e.wait_ge(landed["small"], 16 * 5)
        e.wait_ge(pool.sem, pool.at("ws_T"))
        e.wait_ge(act.sem, act.at("xd_own"))
        e.matmul(ps[0:NS, 7, 0:16], spread[:, :], ws_T[0:NT, :, 0:NT], start=True, stop=True)\
            .then_inc(pe.sem, pe.step("wrep"))
        for m in range(3):
            n = P if m < 2 else NS
            e.wait_ge(dve.sem, dve.at(("vc", m)))
            if m == 2:
                e.wait_ge(dve.sem, dve.at(("bs_own", 3)))
            bias = view(bs, 1, 0, [[1, 512]]) if m < 2 else view(bs_own, 1, 0, [[1, 128]])
            e.matmul(ps[:, 3 + m, 0:4 * n], ones[0:1, :], bias, start=True, stop=False, skip_group_check=True)
            for g in range(4):
                w = ws_T[:, g, :] if m < 2 else view(wd, NS, g * NS, [[1, NS]])
                mm = e.matmul(ps[:, 3 + m, g * n:g * n + n], vc_tok[0:n, m, g * P:g * P + P], w,
                              start=False, stop=g == 3, skip_group_check=True)
            mm.then_inc(pe.sem, pe.step(("mix", m)))
        e.wait_ge(landed["dw"], 16)
        for c in range(4):
            e.wait_ge(dve.sem, dve.at(("pooled", c)))
            e.matmul(ps[:, (1, 2, 6, 7)[c], 0:TOK], dw[:, c, :], pooled[:, c, :], start=True, stop=True)\
                .then_inc(pe.sem, pe.step(("dy", c)))

        def logits(k):
            groups, oc, m = units[k]
            if k >= 2:
                e.wait_ge(act.sem, act.at(("O", k - 2 if k < NA else max(NA - 2, k - 4))))
            for g, (qc, kc, _, _) in enumerate(groups):
                mm = e.matmul(ps[:, room(k)[0] + g, 0:(m + 1) * P], Z[:, qc, m * P:m * P + P],
                              Z[:, kc, 0:(m + 1) * P], start=True, stop=True)
            mm.then_inc(pe.sem, pe.step(("S", k)))
        e.wait_ge(act.sem, act.at(("od", 3)))
        e.wait_ge(dve.sem, dve.at(("oc", 2)))
        logits(0)
        for k, (groups, oc, m) in enumerate(units):
            bank, lp, _, at = room(k)
            for j in range(ahead(k - 1) + 1 if k else 1, ahead(k) + 1):
                logits(j)
            blocks = [(g, b) for g in range(len(groups)) for b in range(m + 1)]
            e.wait_ge(dve.sem, dve.at(("P", k)))
            if k:
                e.wait_ge(act.sem, act.at(("pt", k - 1 if k < NA else max(NA - 1, k - 2))))
            for n, _ in enumerate(blocks):
                mm = turn(view(ps, P, at + n * P, [[1, P]]), view(Lp, P, lp + n * P, [[1, P]]), P)
            mm.then_inc(pe.sem, pe.step(("PT", k)))
            e.wait_ge(act.sem, act.at(("pt", k)))
            for n, (g, b) in enumerate(blocks):
                v = groups[g][2]
                mm = e.matmul(ps[:, bank, 384:512], v_tok[:, b, v * P:v * P + P],
                              view(PTp, P, lp + n * P, [[1, P]]), start=n == 0, stop=n == len(blocks) - 1)
            mm.then_inc(pe.sem, pe.step(("PV", k)))

        e.wait_ge(pool.sem, pool.at("oh_r"))
        e.wait_ge(dve.sem, dve.at("tabr"))
        e.wait_ge(act.sem, act.at(("O", NU - 1)))

        def head_rows(h0, nh, t=None):
            return view(tabr_t, 65, t * 40 + h0 * 4, [[1, 4 * nh]]) if t is not None \
                else view(tabr_all, 65, h0 * 4, [[1, 4 * nh]])

        def biased(dst, h0, nh, off, n, step):
            for t in range(NT):
                mm = e.matmul(dst, head_rows(h0, nh, t), oh_r[:, off + step * t:off + step * t + n],
                              start=t == 0, stop=t == NT - 1)
            return mm
        for k in range(2):
            biased(ps[0:16, k, :], A_HEADS, 4, S_PAST + 3 + 512 * k, 512, -1).then_inc(pe.sem, pe.step(("bias_b", k)))
        biased(ps[0:8, 2, 0:128], 0, 2, S_W0 + 3, 128, -1)
        e.matmul(ps[0:8, 2, 128:256], head_rows(2, 2), oh_r[:, S_W1:S_W1 + 128], start=True, stop=True)
        e.matmul(ps[0:8, 2, 256:320], head_rows(4, 2), oh_r[:, S_W2:S_W2 + 64], start=True, stop=True)
        biased(ps[0:8, 3, 0:256], 0, 2, S_CAUSAL, 256, 256)
        biased(ps[0:8, 4, 0:256], 2, 2, S_SELF, 256, 256)
        biased(ps[0:8, 4, 256:512], 4, 2, S_SELF, 256, 256)
        biased(ps[0:16, 5, 0:256], A_HEADS, 4, S_CAUSAL, 256, 256).then_inc(pe.sem, pe.step("bias_a"))
        e.wait_ge(dve.sem, dve.at("bias"))

        def turn_keys(n, q, at):
            half, h = q // 4, q % 4
            if h == 0:
                e.wait_ge(kv_landed[half], n * 64 + 64)
            if q >= 3:
                e.wait_ge(keys_even if q % 2 else keys_odd, n * 4 + ((q - 3) // 2 + 1))
            elif at is not None:
                k = dve if q % 2 == 0 else act
                e.wait_ge(k.sem, at(k, ("kt_a", q + 1)))
            for pg in range(4):
                mm = turn(ps[:, q % 3, pg * P:pg * P + P], kv[half][:, pg, h * P:h * P + P], P)
            mm.then_inc(keys_turned, 1)

        def scores(n, q, at):
            half, h = q // 4, q % 4
            e.wait_ge(keys_odd if q % 2 else keys_even, n * 4 + (q // 2 + 1))
            if q == 0:
                e.wait_ge(q_put, n * 2 + 1)
                if at is not None:
                    e.wait_ge(dve.sem, at(dve, "L_b0"))
            e.matmul(ps[0:16, 4 + half, :], qs_b[:, 16 * h:16 * h + 16], kt_b[:, q % 2, :],
                     start=h == 0, stop=h == 3).then_inc(scored, 1)

        def keys(n, q0, q1, at):
            for q in range(q0, q1):
                turn_keys(n, q, at)
                if q:
                    scores(n, q - 1, at)

        def sample(i, last):
            name, at = sample_steps(i, last)
            nxt = i + 1
            e.wait_ge(win_landed[0][0], i * 16 + 16)
            for h in range(2):
                if h:
                    e.wait_ge(keys_even, i * 4 + 4)
                else:
                    e.wait_ge(keys_odd, i * 4 + 3)
                for r in range(4):
                    mm = turn(ps[:, (8 + h) % 3, r * P:r * P + P], kv[2][:, r, h * P:h * P + P], P)
                mm.then_inc(pe.sem, pe.step(name(("kTa", h))))
            e.wait_ge(pool.sem, pool.at("ident"))
            e.wait_ge(win_landed[0][1], i * 16 + 16)
            e.wait_ge(keys_odd, i * 4 + 4)
            for h in range(2):
                for r in range(4):
                    c = (4 * h + r) * 64
                    mm = turn(ps[:, 1, c:c + 64], kv[3][0:64, r, h * P:h * P + P], 64)
            mm.then_inc(pe.sem, pe.step(name(("kTa", 2))))
            e.wait_ge(win_landed[0][2], i * 16 + 16)
            e.wait_ge(act.sem, at(act, ("kt_a", 0)))
            for h in range(2):
                mm = turn(ps[:, 2, h * P:h * P + P], win0[:, h * P:h * P + P], P)
            mm.then_inc(pe.sem, pe.step(name(("kTa", 3))))
            e.wait_ge(dve.sem, at(dve, "o_a", back=1))
            for h in range(4):
                mm = e.matmul(ps[0:16, 7, 0:NS], qs_b[:, 16 * h:16 * h + 16], z_own[:, K_B + h, :],
                              start=h == 0, stop=h == 3)
            mm.then_inc(pe.sem, pe.step(name("own_b")))
            e.wait_ge(q_put, i * 2 + 2)
            e.wait_ge(act.sem, at(act, "oa", back=1))
            for g in range(3):
                for h in range(2):
                    e.matmul(ps[0:8, 6, 320 + 32 * g:352 + 32 * g], qs_a[:, 16 * g + 8 * h:16 * g + 8 * h + 8],
                             z_own[:, K_A + 2 * g + h, :], start=h == 0, stop=h == 1)
            if not last:
                keys(nxt, 0, 2, at)
            for b in (0, 2):
                e.wait_ge(act.sem, at(act, ("kt_a", b)))
            e.wait_ge(dve.sem, at(dve, ("kt_a", 1)))
            for h in range(2):
                for r in range(4):
                    c = 48 + 8 * (4 * h + r)
                    e.matmul(ps[0:8, 6, 128:256], qs_a[:, c:c + 8], kt_a[:, h, r * P:r * P + P],
                             start=h + r == 0, stop=h + r == 4)
            for h in range(2):
                for r in range(4):
                    c, k = 112 + 8 * (4 * h + r), (4 * h + r) * 64
                    e.matmul(ps[0:8, 6, 256:320], qs_a[:, c:c + 8], kt_a[:, 2, k:k + 64],
                             start=h + r == 0, stop=h + r == 4)
            e.wait_ge(dve.sem, at(dve, ("kt_a", 3)))
            for h in range(2):
                mm = e.matmul(ps[0:8, 6, 0:128], qs_a[:, 8 * h:8 * h + 8], kt_a[:, 3, h * P:h * P + P],
                              start=h == 0, stop=h == 1)
            mm.then_inc(pe.sem, pe.step(name("s_a")))
            if not last:
                keys(nxt, 2, 6, at)

            def value(x):
                return x if isinstance(x, int) else e.snap(e.to_reg(x))
            need = value(at(dve, "P_b"))
            e.wait_ge(pool.sem, pool.at("ident"))
            e.wait_ge(dve.sem, need)
            for pg in range(8):
                turn(ps[:, 7, 16 * pg:16 * pg + 16], L_b[:, pg * P:pg * P + P], 16)
            turn(ps[0:NS, 7, 128:144], L_b[:, PAST:PAST + NS], 16).then_inc(pe.sem, pe.step(name("ptb")))
            if not last:
                keys(nxt, 6, 8, at)
            e.wait_ge(dve.sem, at(dve, "pt_b"))
            need = value(at(act, "E_a"))
            e.wait_ge(pool.sem, pool.at("ident"))
            e.wait_ge(act.sem, need)
            turn(ps[:, 7, 160:168], L_a[:, 0:128], 8)
            turn(ps[:, 7, 168:176], L_a[:, 128:256], 8)
            turn(ps[0:64, 7, 176:184], L_a[:, 256:320], 8)
            for g in range(3):
                mm = turn(ps[0:NS, 7, 184 + 8 * g:192 + 8 * g], L_a[:, 320 + 32 * g:352 + 32 * g], 8)
            mm.then_inc(pe.sem, pe.step(name("pta")))
            e.wait_ge(act.sem, at(act, "ob", back=1))
            for pg in range(9):
                if pg % 4 == 0 and pg < 8:
                    e.wait_ge(dve.sem, at(dve, ("v_lo", pg // 4)))
                k = P if pg < 8 else NS
                hi_v, lo_v = (v_hi[pg // 4][:, pg % 4, :], v_lo[pg // 4][:, pg % 4, :]) if pg < 8 \
                    else (own_hi[:, :], own_lo[:, :])
                e.matmul(ps[0:32, 3, :], pt_b[0:k, pg, :], hi_v, start=pg == 0, stop=False, skip_group_check=True)
                mm = e.matmul(ps[0:16, 3, :], pt_b[0:k, pg, 0:16], lo_v, start=False, stop=pg == 8,
                              skip_group_check=True)
            mm.then_inc(pe.sem, pe.step(name("pv_b")))
            for w in range(3):
                e.wait_ge(win_landed[1][w], i * 16 + 16)
            e.wait_ge(dve.sem, at(dve, "pt_a"))
            e.matmul(ps[0:8, 6, 0:256], pt_a[:, 0:8], win0[:, 256:512], start=True, stop=False)
            for r in range(4):
                e.matmul(ps[0:8, 6, 0:256], pt_a[:, 8 + 8 * r:16 + 8 * r], kv[2][:, r, 256:512],
                         start=False, stop=False)
            for r in range(4):
                e.matmul(ps[0:8, 6, 0:256], pt_a[0:64, 40 + 8 * r:48 + 8 * r], kv[3][0:64, r, 256:512],
                         start=False, stop=False)
            for g in range(3):
                mm = e.matmul(ps[0:8, 6, 0:256], pt_a[0:NS, 72 + 8 * g:80 + 8 * g], v_own[:, 256 * g:256 * g + 256],
                              start=False, stop=g == 2)
            mm.then_inc(pe.sem, pe.step(name("pv_a")))
            need = value(at(act, "ob"))
            e.wait_ge(pool.sem, pool.at("ident"))
            e.wait_ge(act.sem, need)
            for h in range(4):
                mm = turn(ps[:, 7, 32 * h:32 * h + 32], ob[:, h * P:h * P + P], 32)
            mm.then_inc(pe.sem, pe.step(name("otb")))
            if not last:
                scores(nxt, 7, at)
            need = value(at(act, "oa"))
            e.wait_ge(pool.sem, pool.at("ident"))
            e.wait_ge(act.sem, need)
            for h in range(2):
                mm = turn(ps[:, 7, 128 + 8 * h:136 + 8 * h], oa[:, h * P:h * P + P], 8)
            mm.then_inc(pe.sem, pe.step(name("ota")))
        keys(0, 0, 8, None)
        scores(0, 7, None)
        pe.begin("sample")
        with e.Fori(0, NB - 1) as i:
            sample(i, False)
        pe.end(NB - 1)
        sample(NB - 1, True)

        with e.Fori(0, 4) as i:
            for b in range(4):
                e.wait_ge(sig_ready, i * 4 + b)
                for j in range(4):
                    unit(unit_no(U_MIX, 20, i, 5 * b + j), xn_hi, xn_lo, 4 * j, 0, j == 0, j == 3)
                e.wait_ge(dve.sem, dve.at(("O_lo", 1)))
                e.wait_ge(p_used, i * 4 + b)
                unit(unit_no(U_MIX, 20, i, 5 * b + 4), O_hi, O_lo, O_CHUNK[b], 1, True, True, k=P_CHUNKS[b])

        with e.Fori(0, 2) as i:
            for g in range(2):
                e.wait_ge(m_copied, i * (1 + g))
                e.wait_ge(*((p_used, 16) if g else (sig_ready, 16)))
                for j in range(4):
                    if g == 0 and j % 3 == 0:
                        e.wait_ge(merged_lo, 4 if j else 3)
                    unit(unit_no(U_GATE, 8, i, 4 * g + j), M_hi, M_lo, 4 * j, g, j == 0, j == 3)
        e.wait_ge(m_copied, 3)
        for q in range(4):
            sums("mix_post", sq_b, q, 3)
        e.wait_ge(landed["crow"], 16 * 8)
        for k in range(11):
            mm = turn(view(ps, P, k * P, [[1, P]]), crow[:, k, :], P)
        mm.then_inc(pe.sem, pe.step("histc"))
        e.wait_ge(dve.sem, dve.at(("mix_post", "var")))
        for q in range(4):
            sums("ffn_pre", sq_b, q, 3)

        def ffn_round(i):
            fixed = isinstance(i, int)
            for s in range(2):
                if not fixed or i > 0:
                    e.wait_ge(h_copied, i * 4 - 2 + 2 * s)
                    e.wait_ge(y_added, i * 4 - 1 + s)
                for j in range(4):
                    if fixed and i == 0 and s == 0:
                        e.wait_ge(dve.sem, dve.at(("ffn_pre", "lo", j)))
                    unit(ffn_unit(i, 4 * s + j), xn_hi, xn_lo, 4 * j, s, j == 0, j == 3)
            if not fixed or i > 0:
                down(i, 8)

        def down(i, j0):
            e.wait_ge(act_ready, i * 2)
            for j in range(4):
                if j < 2:
                    e.wait_ge(h_copied, i * 4 + (2 * j + 2) if j0 else 44)
                else:
                    e.wait_ge(y_added, i * 4 + (j - 1))
                unit(ffn_unit(i, j0 + j), act_hi, act_lo, 0, j % 2, True, True)
        ffn_round(0)
        ffn_round(1)
        with e.Fori(2, 11) as i:
            ffn_round(i)
        down(11, 0)

        e.wait_ge(tails_put, 66)
        e.wait_ge(y_added, 4 + 4 * 10 + 4)
        for k in range(13):
            n = 7 * TAIL if k < 12 else 4 * TAIL
            mm = turn(view(ps, n, k * P, [[1, P]]), view(tails, P, k * 7 * TAIL, [[1, n]]), P)
        mm.then_inc(pe.sem, pe.step("tailT"))
        for q in range(4):
            sums("ffn_post", sq_f, q, 7)
        e.wait_ge(dve.sem, dve.at(("ffn_post", "var")))
        for m in range(3):
            n = P if m < 2 else NS
            b = 4 * ((m + 1) % 2)
            if m == 1:
                e.wait_ge(act.sem, act.at("tail_rows"))
            if m == 2:
                e.wait_ge(act.sem, act.at(("y", 0)))
                e.wait_ge(dve.sem, dve.at(("y", 0)))
            for c in range(KC):
                if m == 0 and c % 4 == 0:
                    k = dve if c // 4 % 2 else pool
                    e.wait_ge(k.sem, k.at(("yf", c // 4)))
                mm = turn(view(ps, n, b * 512 + c * P, [[1, P]]), m_T[:, c, m * P:m * P + n], P)
            mm.then_inc(pe.sem, pe.step(("yT", m)))


_INS = ["x_prompt", "x_sample", "cache_win0", "cache_win1", "cache_win2", "cache_k", "cache_v", "page_table",
        "state_pool", "state_conv", "rel_bias_table", "norm_mix_pre", "w_in", "c_ln_g", "c_ws", "c_bs", "d_w",
        "d_scale", "p_a", "p_b", "p_c", "p_d", "w_o", "norm_mix_post", "norm_ffn_pre", "w_up", "conv_w", "conv_b",
        "w_down", "norm_ffn_post"]
_OUTS = [(1, 256, 2048), (8, 4, 2048), (1, 1, 128, 2, 2, 128), (1, 1, 256, 2, 2, 128), (1, 1, 256, 2, 2, 128),
         (1, 1, 256, 4, 128), (1, 1, 256, 4, 128), (1, 1, 15, 512), (1, 1, 2, 11264),
         (1, 8, 128, 2, 2, 128), (1, 8, 512, 2, 2, 128), (1, 8, 1028, 2, 2, 128),
         (1, 8, 4, 4, 128), (1, 8, 4, 4, 128), (1, 8, 4, 512), (1, 8, 15, 512), (1, 8, 2, 11264)]


def kernel(**inputs):
    import concourse.bacc as bacc
    from concourse.bass_utils import run_bass_kernel_spmd

    arrays = {n: np.ascontiguousarray(inputs[n]) for n in _INS}
    arrays.update(constants())
    known = {}
    for _ in range(2):
        nc = bacc.Bacc("TRN2", target_bir_lowering=False, num_devices=1, dynamic_dma_scratch_size=2048)
        d = {n: nc.dram_tensor(f"in_{n}", a.shape, mybir.dt.from_np(a.dtype), kind="ExternalInput").ap()
             for n, a in arrays.items()}
        o = [nc.dram_tensor(f"out_{i}", s, F32, kind="ExternalOutput").ap() for i, s in enumerate(_OUTS)]
        with ExitStack() as ctx:
            build(nc, known, d, o, ctx)
    r = run_bass_kernel_spmd(nc, [{f"in_{n}": a for n, a in arrays.items()}], core_ids=[0])
    return tuple(r.results[0][f"out_{i}"] for i in range(len(_OUTS)))
```
